# Optimizing a Trainium2 kernel written in Bass

```python
import jax, jax.numpy as jnp
from jax import lax
import numpy as np

D_MODEL = 1024
BATCH = 1
SEQ = 256
DEPTH = 2

HEAD_DIM = 64
ROPE_DIM = HEAD_DIM // 4
ROPE_THETA = 500000.0
NORM_EPS = 1e-6
NEG = -1e30
BAND_BLOCK = 128
MAX_POS_OFFSET = 4096

NSA_HEADS = D_MODEL // HEAD_DIM
NSA_KV_HEADS = 4
NSA_GROUP = NSA_HEADS // NSA_KV_HEADS
CMP_BLOCK = 32
CMP_STRIDE = 16
CMP_HIDDEN = 4 * HEAD_DIM
SEL_BLOCK = 64
SEL_TOPN = 8
FORCE_SCORE = 1e4
WIN = 512
NSA_Q_CHUNK = 64
NSA_IN = NSA_HEADS * HEAD_DIM + 6 * NSA_KV_HEADS * HEAD_DIM + 3 * NSA_HEADS

DIL_PATTERNS = ((128, 1), (512, 4), (2048, 16))
N_DIL = len(DIL_PATTERNS)
DIL_HEADS = D_MODEL // HEAD_DIM
DIL_IN = N_DIL * 3 * DIL_HEADS * HEAD_DIM

D_FF = ((8 * D_MODEL + 3 * 256 - 1) // (3 * 256)) * 256

N_NSA_LAYERS = (DEPTH + 1) // 2
N_DIL_LAYERS = DEPTH // 2

kernel_name = 'hybrid_nsa_dilated_swiglu_trunk'

def rmsnorm(x, g):
    xf = x.astype(jnp.float32)
    y = xf * lax.rsqrt(jnp.mean(xf * xf, axis=-1, keepdims=True) + NORM_EPS)
    return (y * g.astype(jnp.float32)).astype(x.dtype)

def rope_tables(positions):
    inv = ROPE_THETA ** (-jnp.arange(0, ROPE_DIM, 2, dtype=jnp.float32) / ROPE_DIM)
    ang = positions.astype(jnp.float32)[..., None] * inv
    return jnp.cos(ang)[:, :, None, :], jnp.sin(ang)[:, :, None, :]

def partial_rope(x, cos, sin):
    half = ROPE_DIM // 2
    x1 = x[..., :half].astype(jnp.float32)
    x2 = x[..., half:ROPE_DIM].astype(jnp.float32)
    rot = jnp.concatenate([x1 * cos - x2 * sin, x2 * cos + x1 * sin], axis=-1).astype(x.dtype)
    return jnp.concatenate([rot, x[..., ROPE_DIM:]], axis=-1)

def banded_attention(q, k, v, max_dist):
    n, L, hkv, g, dh = q.shape
    nb = -(-L // BAND_BLOCK)
    Lp = nb * BAND_BLOCK
    kw = BAND_BLOCK + max_dist
    qp = jnp.pad(q, ((0, 0), (0, Lp - L), (0, 0), (0, 0), (0, 0)))
    kp = jnp.pad(k, ((0, 0), (max_dist, Lp - L), (0, 0), (0, 0)))
    vp = jnp.pad(v, ((0, 0), (max_dist, Lp - L), (0, 0), (0, 0)))
    qb = qp.reshape(n, nb, BAND_BLOCK, hkv, g, dh).swapaxes(0, 1)
    rel = jnp.arange(BAND_BLOCK)[:, None] + max_dist - jnp.arange(kw)[None, :]
    band = (rel >= 0) & (rel <= max_dist)
    scale = dh ** -0.5

    def block(args):
        c, qc = args
        start = c * BAND_BLOCK
        kc = lax.dynamic_slice_in_dim(kp, start, kw, axis=1)
        vc = lax.dynamic_slice_in_dim(vp, start, kw, axis=1)
        kpos = start - max_dist + jnp.arange(kw)
        mask = band & (kpos >= 0)[None, :]
        s = jnp.einsum('nqhgd,nkhd->nhgqk', qc, kc).astype(jnp.float32) * scale
        s = jnp.where(mask, s, NEG)
        m = jnp.max(s, axis=-1, keepdims=True)
        p = jnp.exp(s - m)
        l = jnp.sum(p, axis=-1, keepdims=True)
        o = jnp.einsum('nhgqk,nkhd->nqhgd', (p / l).astype(vc.dtype), vc)
        lse = (m + jnp.log(l))[..., 0].transpose(0, 3, 1, 2)
        return o, lse

    o, lse = lax.map(block, (jnp.arange(nb), qb))
    o = o.swapaxes(0, 1).reshape(n, Lp, hkv, g, dh)[:, :L]
    lse = lse.swapaxes(0, 1).reshape(n, Lp, hkv, g)[:, :L]
    return o, lse

def nsa_mixer(a, cos, sin, w_in, cmp_pos, cmp_wk1, cmp_wk2, cmp_wv1, cmp_wv2, w_o):
    B, S, _ = a.shape
    H, HK, G, DH = NSA_HEADS, NSA_KV_HEADS, NSA_GROUP, HEAD_DIM
    dq, dkv = H * DH, HK * DH
    scale = DH ** -0.5
    proj = a @ w_in
    q = proj[..., :dq].reshape(B, S, H, DH)
    kv = proj[..., dq:dq + 6 * dkv].reshape(B, S, 6, HK, DH)
    k_cmp, v_cmp, k_sel, v_sel, k_win, v_win = [kv[:, :, i] for i in range(6)]
    gates = jax.nn.sigmoid(proj[..., dq + 6 * dkv:].astype(jnp.float32)).reshape(B, S, 3, HK, G)
    q_grp = q.reshape(B, S, HK, G, DH)
    q_rot = partial_rope(q, cos, sin).reshape(B, S, HK, G, DH)
    k_sel = partial_rope(k_sel, cos, sin)
    k_win = partial_rope(k_win, cos, sin)
    pos = jnp.arange(S)

    n_cmp = (S - CMP_BLOCK) // CMP_STRIDE + 1
    blk = jnp.arange(n_cmp)[:, None] * CMP_STRIDE + jnp.arange(CMP_BLOCK)[None, :]

    def compress(t, w1, w2):
        tb = t[:, blk] + cmp_pos[None, None, :, None, :]
        tb = tb.transpose(0, 1, 3, 2, 4).reshape(B, n_cmp, HK, CMP_BLOCK * DH)
        return jax.nn.silu(tb @ w1) @ w2

    kc = compress(k_cmp, cmp_wk1, cmp_wk2)
    vc = compress(v_cmp, cmp_wv1, cmp_wv2)
    c_start = jnp.arange(n_cmp) * CMP_STRIDE
    c_valid = (c_start + CMP_BLOCK - 1)[None, :] <= pos[:, None]
    s_cmp = jnp.einsum('bthgd,bchd->bhgtc', q_grp, kc).astype(jnp.float32) * scale
    p_cmp = jax.nn.softmax(jnp.where(c_valid, s_cmp, NEG), axis=-1) * c_valid
    o_cmp = jnp.einsum('bhgtc,bchd->bthgd', p_cmp.astype(vc.dtype), vc)

    n_sel = S // SEL_BLOCK
    top_n = min(SEL_TOPN, n_sel)
    j_start = jnp.arange(n_sel) * SEL_BLOCK
    overlap = ((c_start[:, None] < j_start[None, :] + SEL_BLOCK)
               & (c_start[:, None] + CMP_BLOCK > j_start[None, :])).astype(jnp.float32)
    imp = jnp.einsum('bhgtc,cj->bhtj', p_cmp, overlap)
    jb = jnp.arange(n_sel)[None, :]
    tb = (pos // SEL_BLOCK)[:, None]
    forced = (jb == 0) | (jb == tb) | (jb == tb - 1)
    score = jnp.where(forced, FORCE_SCORE, jnp.where(jb <= tb, imp, -1.0))
    _, sel_idx = lax.top_k(score, top_n)

    n_ch = S // NSA_Q_CHUNK
    n_key = top_n * SEL_BLOCK
    kb = k_sel.reshape(B, n_sel, SEL_BLOCK, HK, DH).transpose(0, 3, 1, 2, 4)
    vb = v_sel.reshape(B, n_sel, SEL_BLOCK, HK, DH).transpose(0, 3, 1, 2, 4)
    q_ch = q_rot.reshape(B, n_ch, NSA_Q_CHUNK, HK, G, DH).swapaxes(0, 1)
    i_ch = sel_idx.reshape(B, HK, n_ch, NSA_Q_CHUNK, top_n).transpose(2, 0, 1, 3, 4)
    gather = jax.vmap(jax.vmap(lambda blocks, ids: blocks[ids]))

    def sel_chunk(args):
        c, qc, ic = args
        kg = gather(kb, ic).reshape(B, HK, NSA_Q_CHUNK, n_key, DH)
        vg = gather(vb, ic).reshape(B, HK, NSA_Q_CHUNK, n_key, DH)
        kpos = (ic[..., None] * SEL_BLOCK + jnp.arange(SEL_BLOCK)).reshape(B, HK, NSA_Q_CHUNK, n_key)
        qpos = c * NSA_Q_CHUNK + jnp.arange(NSA_Q_CHUNK)
        mask = (kpos <= qpos[:, None])[:, :, None]
        s = jnp.einsum('bqhgd,bhqkd->bhgqk', qc, kg).astype(jnp.float32) * scale
        p = jax.nn.softmax(jnp.where(mask, s, NEG), axis=-1)
        return jnp.einsum('bhgqk,bhqkd->bqhgd', p.astype(vg.dtype), vg)

    o_sel = lax.map(sel_chunk, (jnp.arange(n_ch), q_ch, i_ch))
    o_sel = o_sel.swapaxes(0, 1).reshape(B, S, HK, G, DH)

    o_win, _ = banded_attention(q_rot, k_win, v_win, WIN - 1)

    branches = jnp.stack([o_cmp, o_sel, o_win], axis=2)
    o = jnp.sum(gates[..., None].astype(branches.dtype) * branches, axis=2)
    return o.reshape(B, S, H * DH) @ w_o

def to_residue(t, dil):
    B, S, H, DH = t.shape
    return t.reshape(B, S // dil, dil, H, DH).swapaxes(1, 2).reshape(B * dil, S // dil, H, DH)

def from_residue(t, B, dil):
    rest = t.shape[2:]
    L = t.shape[1]
    return t.reshape((B, dil, L) + rest).swapaxes(1, 2).reshape((B, L * dil) + rest)

def dilated_mixer(a, cos, sin, w_in, w_o):
    B, S, _ = a.shape
    H, DH = DIL_HEADS, HEAD_DIM
    proj = (a @ w_in).reshape(B, S, N_DIL, 3, H, DH)
    outs, lses = [], []
    for gi, (window, dil) in enumerate(DIL_PATTERNS):
        q = partial_rope(proj[:, :, gi, 0], cos, sin)
        k = partial_rope(proj[:, :, gi, 1], cos, sin)
        v = proj[:, :, gi, 2]
        o, lse = banded_attention(to_residue(q, dil)[:, :, :, None], to_residue(k, dil),
                                  to_residue(v, dil), window // dil)
        outs.append(from_residue(o[:, :, :, 0], B, dil))
        lses.append(from_residue(lse[:, :, :, 0], B, dil))
    alpha = jax.nn.softmax(jnp.stack(lses, axis=-1), axis=-1)
    o = jnp.einsum('bshn,bshnd->bshd', alpha.astype(a.dtype), jnp.stack(outs, axis=3))
    return o.reshape(B, S, H * DH) @ w_o

def swiglu(h, w_gu, w_down):
    gu = h @ w_gu
    g, u = gu[..., :D_FF], gu[..., D_FF:]
    return (jax.nn.silu(g) * u) @ w_down

def setup_inputs(seed: int = 0) -> dict:
    key = jax.random.key(seed)
    ks = jax.random.split(key, 20)
    f32 = jnp.float32

    def nrm(k, shape, fan_in):
        return jax.random.normal(k, shape, f32) * (fan_in ** -0.5)

    def gain(k, shape):
        return 1.0 + 0.02 * jax.random.normal(k, shape, f32)

    nA, nB = N_NSA_LAYERS, N_DIL_LAYERS
    x = jax.random.normal(ks[0], (BATCH, SEQ, D_MODEL), f32)
    positions = (jax.random.randint(ks[1], (BATCH, 1), 0, MAX_POS_OFFSET, jnp.int32)
                 + jnp.arange(SEQ, dtype=jnp.int32)[None, :])
    return {
        'x': x,
        'positions': positions,
        'norm_mix_pre': gain(ks[2], (DEPTH, D_MODEL)),
        'norm_mix_post': gain(ks[3], (DEPTH, D_MODEL)),
        'norm_ffn_pre': gain(ks[4], (DEPTH, D_MODEL)),
        'norm_ffn_post': gain(ks[5], (DEPTH, D_MODEL)),
        'ffn_w_gu': nrm(ks[6], (DEPTH, D_MODEL, 2 * D_FF), D_MODEL),
        'ffn_w_down': nrm(ks[7], (DEPTH, D_FF, D_MODEL), D_FF),
        'nsa_w_in': nrm(ks[8], (nA, D_MODEL, NSA_IN), D_MODEL),
        'nsa_cmp_pos': 0.1 * jax.random.normal(ks[9], (nA, CMP_BLOCK, HEAD_DIM), f32),
        'nsa_cmp_wk1': nrm(ks[10], (nA, CMP_BLOCK * HEAD_DIM, CMP_HIDDEN), CMP_BLOCK * HEAD_DIM),
        'nsa_cmp_wk2': nrm(ks[11], (nA, CMP_HIDDEN, HEAD_DIM), CMP_HIDDEN),
        'nsa_cmp_wv1': nrm(ks[12], (nA, CMP_BLOCK * HEAD_DIM, CMP_HIDDEN), CMP_BLOCK * HEAD_DIM),
        'nsa_cmp_wv2': nrm(ks[13], (nA, CMP_HIDDEN, HEAD_DIM), CMP_HIDDEN),
        'nsa_w_o': nrm(ks[14], (nA, NSA_HEADS * HEAD_DIM, D_MODEL), NSA_HEADS * HEAD_DIM),
        'dil_w_in': nrm(ks[15], (nB, D_MODEL, DIL_IN), D_MODEL),
        'dil_w_o': nrm(ks[16], (nB, DIL_HEADS * HEAD_DIM, D_MODEL), DIL_HEADS * HEAD_DIM),
    }

def reference(x, positions, norm_mix_pre, norm_mix_post, norm_ffn_pre, norm_ffn_post,
              ffn_w_gu, ffn_w_down, nsa_w_in, nsa_cmp_pos, nsa_cmp_wk1, nsa_cmp_wk2,
              nsa_cmp_wv1, nsa_cmp_wv2, nsa_w_o, dil_w_in, dil_w_o):
    cos, sin = rope_tables(positions)
    h = x
    for i in range(DEPTH):
        j = i // 2
        a = rmsnorm(h, norm_mix_pre[i])
        if i % 2 == 0:
            m = nsa_mixer(a, cos, sin, nsa_w_in[j], nsa_cmp_pos[j], nsa_cmp_wk1[j], nsa_cmp_wk2[j],
                          nsa_cmp_wv1[j], nsa_cmp_wv2[j], nsa_w_o[j])
        else:
            m = dilated_mixer(a, cos, sin, dil_w_in[j], dil_w_o[j])
        h = h + rmsnorm(m, norm_mix_post[i])
        f = swiglu(rmsnorm(h, norm_ffn_pre[i]), ffn_w_gu[i], ffn_w_down[i])
        h = h + rmsnorm(f, norm_ffn_post[i])
    return h


_drawn_inputs = setup_inputs


def setup_inputs(seed=0):
    import zlib

    import numpy as np

    out = dict(_drawn_inputs(seed))
    spreads = {}
    factors = {'norm_ffn_post': 3.511}
    for name, (base, spread) in spreads.items():
        noise = np.random.default_rng([zlib.crc32(name.encode()), seed]).standard_normal(out[name].shape)
        drawn = base * np.exp(spread * noise) if base else spread * noise
        out[name] = __import__('jax').numpy.asarray(drawn.astype(out[name].dtype))
    for name, factor in factors.items():
        out[name] = (out[name] * factor).astype(out[name].dtype)
    return out
```

```python
from contextlib import ExitStack

import numpy as np

import concourse.bass as bass
from concourse import mybir

ALU = mybir.AluOpType
ACT = mybir.ActivationFunctionType
AX = mybir.AxisListType.X
F32 = mybir.dt.float32
F32R = mybir.dt.float32r
BF16 = mybir.dt.bfloat16
I32 = mybir.dt.int32

P = 128
D = 1024
S = 256
MT = S // P
KT = D // P
DH = 64
H = D // DH
HK = 4
G = H // HK
FF = 2816
FJ = FF // 256
EPS = 1e-6
NEG = -1e30
SCALE = DH ** -0.5
ROT = DH // 4
THETA = 500000.0
CMP, STRIDE = 32, 16
NC = (S - CMP) // STRIDE + 1
PIECE = 2048
RAW = 3
RING = 6
AHEAD = 3
TWO_PI = 6.283185307179586
MAGIC = 12582912.0
INF = 3.0e38

N_CMPKV, N_SEL, N_WK1, N_WIN, N_WV1, N_Q, N_NSAO = 0, 2, 4, 6, 8, 10, 14
N_FFN0 = 18
FFN_PIECES = 3 * FJ
N_DIL = N_FFN0 + FFN_PIECES
N_DILO = N_DIL + 36
N_FFN1 = N_DILO + 4
N_END = N_FFN1 + FFN_PIECES


class Piece:

    def __init__(self, n0, it=0):
        self.n0, self.it = n0, it

    def __add__(self, k):
        return Piece(self.n0 + k, self.it)

    @property
    def slot(self):
        return self.n0 % RING

    @property
    def raw(self):
        return self.n0 % RAW

    def loaded(self):
        return self.it * (32 * RING // RAW) + 32 * (self.n0 // RAW + 1)

    def halves(self, k):
        return self.it * (2 * RING) + 2 * self.n0 + k

    def used(self):
        return self.it * RING + self.n0 + 1


def view(t, off, dims, p0=0, n=P):
    width = int(np.prod(t.shape[1:]))
    return bass.AP(t, p0 * width + off, [[width, n]] + [list(d) for d in dims])


def build(nc, x, positions, norm_mix_pre, norm_mix_post, norm_ffn_pre, norm_ffn_post, ffn_w_gu,
          ffn_w_down, nsa_w_in, nsa_cmp_pos, nsa_cmp_wk1, nsa_cmp_wk2, nsa_cmp_wv1, nsa_cmp_wv2,
          nsa_w_o, dil_w_in, dil_w_o, out):
    ctx = ExitStack()
    with ctx:
        place = [(int(nc.sbuf_base) + 31) // 32 * 32]

        def sb(name, shape, dt=F32, at=None):
            size = int(np.prod(shape[1:])) * mybir.dt.size(dt)
            if at is None:
                at = place[0]
                place[0] = (at + size + 31) // 32 * 32
            assert at + size <= nc.sbuf_usable_end, name
            return nc.alloc_sbuf_tensor_at(name, shape, dt, offset=at)

        def zone(size):
            at = place[0]
            place[0] = at + size
            return at

        w_raw = sb("w_raw", [P, RAW, PIECE])
        w_hi = sb("w_hi", [P, RING, PIECE], F32R)
        w_lo = sb("w_lo", [P, RING, PIECE], F32R)
        h = sb("h", [P, MT, D])
        at_tmp = zone(MT * D * 4)
        tmp = sb("tmp", [P, MT, D], at=at_tmp)
        pair = sb("pair", [P, 2, HK, S], at=at_tmp)
        xt_hi = sb("xt_hi", [P, KT, S], F32R)
        xt_lo = sb("xt_lo", [P, KT, S], F32R)
        at_gp = zone(D * 4)
        g_post = sb("g_post", [P, D], at=at_gp)
        w2k = sb("w2k", [P, 2, 2, DH], at=at_gp)
        w2v = sb("w2v", [P, 2, DH], at=at_gp + 1024)
        hid_k = sb("hid_k", [P, P], at=at_gp + 1536)
        e_hid = sb("e_hid", [P, 2, P], at=at_gp + 2048)
        rows = sb("rows", [48, P], at=at_gp + 3072)

        at_a = zone(36864)
        q_t = sb("q_t", [P, H // 2, S], at=at_a)
        gw_hi = sb("gw_hi", [P, KT, 48], F32R, at=at_a)
        gw_lo = sb("gw_lo", [P, KT, 48], F32R, at=at_a + 2048)
        qu_t = sb("qu_t", [P, H // 2, S], at=at_a + 8192)
        k_t = sb("k_t", [P, 2, HK, S], at=at_a + 16384)
        v_nsa = sb("v_nsa", [P, 2, MT, HK * DH], at=at_a + 24576)
        vc_bd = sb("vc_bd", [64, HK, G * DH], at=at_a + 28672)
        tb_f = sb("tb_f", [P, 16, HK, 16], at=at_a + 28672)
        pc_t = sb("pc_t", [64, 2 * HK, P], at=at_a + 32768)
        stage_nsa = sb("stage_nsa", [P, MT, 512], at=at_a + 32768)
        qk_t = sb("qk_t", [P, 3, 2, 4, S], at=at_a)
        v_dil = sb("v_dil", [P, 3, MT, 512], at=at_a + 24576)
        silu = sb("silu", [P, MT, 256], at=at_a)
        hs = sb("hs", [P, MT, 256], at=at_a + 2048)

        at_s = zone(10240)
        probs = sb("probs", [P, 3, 512], at=at_s)
        p_t = sb("p_t", [P, 2, 512], at=at_s + 6144)
        st_hi = sb("st_hi", [P, 1024], F32R, at=at_s)
        st_lo = sb("st_lo", [P, 1024], F32R, at=at_s + 4096)
        stage_rot = sb("stage_rot", [P, MT, 512], at=at_s)
        stage_dil = sb("stage_dil", [P, MT, 512], at=at_s)
        gw_raw = sb("gw_raw", [P, KT, 48], at=at_s + 8192)

        at_m = zone(2048)
        mask_dil = sb("mask_dil", [P, MT, 512], BF16, at=at_m)
        hid_v = sb("hid_v", [P, 2 * HK, G, 16], at=at_m)
        p_cmp = sb("p_cmp", [P, MT, H, 16], at=at_m)
        comb = sb("comb", [P, G, 2, DH], at=at_m)
        mask_nsa = sb("mask_nsa", [P, 2 * P], BF16)
        ident = sb("ident", [P, P])
        mask_c = sb("mask_c", [P, MT, 16])
        valid_c = sb("valid_c", [P, MT, 16])
        bd_mask = sb("bd_mask", [64, G])
        cos2 = sb("cos2", [P, 4, ROT])
        sin2 = sb("sin2", [P, 4, ROT])
        g_t = sb("g_t", [P, 48])
        inv_f = sb("inv_f", [P, ROT // 2])
        kc_t = sb("kc_t", [P, 64])
        gates = sb("gates", [P, MT, 48])
        rs = sb("rs", [P, MT])
        rs_post = sb("rs_post", [P, MT])
        ssq = sb("ssq", [P, 2 * MT])
        nt = sb("nt", [P, 4])
        mx = sb("mx", [P, 3, 2])
        nm = sb("nm", [P, 3, 2])
        l_nsa = sb("l_nsa", [P, 3, G, 2])
        coef = sb("coef", [P, G, 2])
        mx_c = sb("mx_c", [P, MT * H])
        l_c = sb("l_c", [P, MT * H])
        l_dil = sb("l_dil", [P, MT, 8])
        rl_dil = sb("rl_dil", [P, MT, 8])
        pos_i = sb("pos_i", [P, 4], I32, at=at_s)
        pos_f = sb("pos_f", [P, 4], at=at_s + 64)
        ang = sb("ang", [P, 4, 8], at=at_s + 128)
        turns = sb("turns", [P, 4, 8], at=at_s + 256)
        half_pi = sb("half_pi", [P, 4, 8], at=at_s + 384)
        rope_a = sb("rope_a", [P, 8, ROT], at=at_s + 8192)
        rope_b = sb("rope_b", [P, 8, ROT], at=at_s + 8704)

        ps = ctx.enter_context(nc.psum_tensor("ps", [P, 8, 512], F32))

        def bank(b, off=0, n=512):
            return ps[:, b, off:off + n]

        def xt_views(b, m, half, kt, dst, permuted):
            base = {0: 4 + 2 * m, 2: 6 - 2 * m}.get(b, 6)
            if not permuted:
                return bank(base + half, P * (kt % 4), P), dst[:, kt, m * P:(m + 1) * P]
            return (view(ps, (base + half) * 512 + P * (kt % 4), [[4, 32], [1, 4]]),
                    view(dst, kt * S + 32 * m, [[1, 32], [64, 4]]))

        def ot_views(hg, m, dst):
            b = 2 if (hg, m) == (1, 1) else 7
            return (view(ps, b * 512, [[P, 4], [64, 2], [1, 64]]),
                    view(dst, 4 * hg * S + 2 * m, [[S, 4], [1, 2], [4, 64]]))

        def sem(name):
            return ctx.enter_context(nc.semaphore(name))

        raw_loaded = [sem(f"raw_loaded{i}") for i in range(RAW)]
        hi_ready, lo_ready, piece_used = sem("hi_ready"), sem("lo_ready"), sem("piece_used")
        x_loaded = [sem(f"x_loaded{m}") for m in range(MT)]
        rows_loaded, pos_loaded, w2_loaded = sem("rows_loaded"), sem("pos_loaded"), sem("w2_loaded")
        gw_loaded, out_stored = sem("gw_loaded"), sem("out_stored")
        gp_loaded = [sem(f"gp_loaded{i}") for i in range(4)]
        ident_ready, masks_ready = sem("ident_ready"), sem("masks_ready")
        dilmask_ready, rope_ready = sem("dilmask_ready"), sem("rope_ready")
        angles_ready = sem("angles_ready")
        pool_step, dve_step = sem("pool_step"), sem("dve_step")
        rows_t, gt_ready = sem("rows_t"), sem("gt_ready")
        gw_hi_ready, gw_ready = sem("gw_hi_ready"), sem("gw_ready")
        acc_done = [sem(f"acc_done{b}") for b in range(5)]
        sq_post = [sem(f"sq_post{b}") for b in range(5)]
        h_ready = [sem(f"h_ready{b}") for b in range(5)]
        sq_h = [sem(f"sq_h{b}") for b in range(4)]
        rs_ready = [sem(f"rs_ready{b}") for b in range(4)]
        xn_ready = sem("xn_ready")
        xt_psum = [sem(f"xt_psum{b}") for b in range(4)]
        xt_hi_ready = [sem(f"xt_hi_ready{b}") for b in range(4)]
        xt_ready = [sem(f"xt_ready{b}") for b in range(4)]
        proj_done = [sem(f"proj_done{i}") for i in range(2)]
        proj_out = [sem(f"proj_out{i}") for i in range(2)]
        roped = [sem(f"roped{i}") for i in range(2)]
        turned = [sem(f"turned{i}") for i in range(2)]
        turn_out = [sem(f"turn_out{i}") for i in range(2)]
        rope_parts = sem("rope_parts")
        pair_act, pair_dve = sem("pair_act"), sem("pair_dve")
        tb_f_ready, tb_hi_ready, tb_ready = sem("tb_f_ready"), sem("tb_hi_ready"), sem("tb_ready")
        gate_sum, gate_exp = sem("gate_sum"), sem("gate_exp")
        hid_sum, hid_exp, hid_ready = sem("hid_sum"), sem("hid_exp"), sem("hid_ready")
        kc_sum, kc_out, vc_out = sem("kc_sum"), sem("kc_out"), sem("vc_out")
        sc_sum, sc_ready, pc_exp, pc_ready = sem("sc_sum"), sem("sc_ready"), sem("pc_exp"), sem("pc_ready")
        pct_psum, pct_out, ocmp_sum = sem("pct_psum"), sem("pct_out"), sem("ocmp_sum")
        scores = [sem(f"scores{i}") for i in range(2)]
        masked = [sem(f"masked{i}") for i in range(2)]
        expd = [sem(f"expd{i}") for i in range(2)]
        pt_psum = [sem(f"pt_psum{i}") for i in range(2)]
        pt_out = [sem(f"pt_out{i}") for i in range(2)]
        pt_out_dve = sem("pt_out_dve")
        pv_done = [sem(f"pv_done{i}") for i in range(2)]
        o_ready = [sem(f"o_ready{i}") for i in range(2)]
        ot_psum = [sem(f"ot_psum{i}") for i in range(2)]
        ot_hi = [sem(f"ot_hi{i}") for i in range(2)]
        ot_ready = [sem(f"ot_ready{i}") for i in range(2)]
        gu_done = [sem(f"gu_done{l}") for l in range(2)]
        silu_done = [sem(f"silu_done{l}") for l in range(2)]
        hs_ready = [sem(f"hs_ready{l}") for l in range(2)]
        ht_psum = [sem(f"ht_psum{l}") for l in range(2)]
        ht_hi = [sem(f"ht_hi{l}") for l in range(2)]
        ht_ready = [sem(f"ht_ready{l}") for l in range(2)]

        block = ctx.enter_context(nc.Block())

        @block.sync
        def _(sp):
            def load(pc, *parts):
                if pc.n0 >= RAW:
                    sp.wait_ge(lo_ready, pc.halves(2) - 2 * RAW)
                for src, c, dims in parts:
                    sp.dma_start(view(w_raw, pc.raw * PIECE + c, dims), src)\
                      .then_inc(raw_loaded[pc.raw], 16)

            def chunk(n, w, c0):
                wv = w.rearrange("(k p) c -> p k c", p=P)
                for half in range(2):
                    load(n + half, *[(wv[:, 4 * half + k:4 * half + k + 2, bass.ds(c0, 512)], 512 * k,
                                      [[512, 2], [1, 512]]) for k in (0, 2)])

            for m in range(MT):
                sp.dma_start(h[:, m, :], x[0, m * P:(m + 1) * P, :]).then_inc(x_loaded[m], 16)
            w_in = nsa_w_in[0]
            chunk(Piece(N_CMPKV), w_in, 1024)
            chunk(Piece(N_SEL), w_in, 1536)

            def cmp_w1(n, w):
                wv = w[0].rearrange("(k p) c -> p k c", p=P)
                for half in range(2):
                    load(n + half, *[(wv[:, 8 * half + k:8 * half + k + 4, :], 256 * k,
                                      [[256, 4], [1, 256]]) for k in (0, 4)])

            cmp_w1(Piece(N_WK1), nsa_cmp_wk1)
            chunk(Piece(N_WIN), w_in, 2048)
            cmp_w1(Piece(N_WV1), nsa_cmp_wv1)
            chunk(Piece(N_Q), w_in, 0)
            chunk(Piece(N_Q + 2), w_in, 512)

            def out_proj(n, w):
                chunk(Piece(n), w[0], 0)
                chunk(Piece(n + 2), w[0], 512)

            def ffn_loads(n0, layer):
                gu = ffn_w_gu[layer].rearrange("(k p) (s c) -> p k s c", p=P, s=2)
                dn = ffn_w_down[layer].rearrange("(k p) c -> p k c", p=P)

                def gu_load(pc, j):
                    for half in range(2):
                        load(pc + half, *[(gu[:, 4 * half:4 * half + 4, s, bass.ds(j * 256, 256)], 256 * s,
                                           [[512, 4], [1, 256]]) for s in range(2)])

                def dn_load(pc, j):
                    load(pc, *[(dn[:, bass.ds(j * 2 + k, 1), :], D * k, [[D, 1], [1, D]]) for k in range(2)])

                def step(pc, j):
                    gu_load(pc, j)
                    dn_load(pc + 2, j - 1)

                gu_load(Piece(n0), 0)
                step(Piece(n0 + 2), 1)
                with sp.Fori(0, (FJ - 3) // 2) as it:
                    for s in range(2):
                        step(Piece(n0 + 5 + 3 * s, it), it * 2 + (2 + s))
                step(Piece(n0 + 3 * FJ - 4), FJ - 1)
                dn_load(Piece(n0 + FFN_PIECES - 1), FJ - 1)

            out_proj(N_NSAO, nsa_w_o)
            ffn_loads(N_FFN0, 0)
            for hg in range(2):
                with sp.Fori(0, 3) as pat:
                    for t in range(3):
                        chunk(Piece(N_DIL + 18 * hg + 2 * t, pat), dil_w_in[0],
                              pat * (3 * D) + (t * D + hg * 512))
            out_proj(N_DILO, dil_w_o)
            ffn_loads(N_FFN1, 1)
            for q in range(2 * MT):
                m, half = q // 2, q % 2
                sp.wait_ge(h_ready[4], q + 1)
                sp.dma_start(out[0, m * P:(m + 1) * P, half * 512:(half + 1) * 512],
                             h[:, m, half * 512:(half + 1) * 512]).then_inc(out_stored, 16)
            sp.wait_ge(out_stored, 16 * 2 * MT)

        @block.gpsimd
        def _(pool):
            done = [0]

            def link(ins):
                done[0] += 1
                ins.then_inc(pool_step, 1)
                pool.wait_ge(pool_step, done[0])

            link(pool.memset(ident[:, :], 0.0))
            pool.affine_select(out=ident[:, :], in_=ident[:, :], compare_op=ALU.not_equal, fill=1.0,
                               base=0, pattern=[[-1, P]], channel_multiplier=1).then_inc(ident_ready, 1)
            for i in range(ROT // 2):
                f = float(np.float32(THETA) ** np.float32(-2.0 * i / ROT))
                ins = pool.memset(inv_f[:, i:i + 1], f)
            ins.then_inc(rope_ready, 1)
            link(pool.memset(mask_nsa[:, :], 0.0))
            pool.affine_select(out=mask_nsa[:, P:2 * P], in_=mask_nsa[:, P:2 * P], compare_op=ALU.is_ge,
                               fill=NEG, base=0, pattern=[[-1, P]], channel_multiplier=1)\
                .then_inc(masks_ready, 1)
            for t, good, bad in ((mask_c, 0.0, NEG), (valid_c, 1.0, 0.0)):
                link(pool.memset(t[:, :, :], good))
                pool.affine_select(out=t[:, :, :], in_=t[:, :, :], compare_op=ALU.is_ge, fill=bad,
                                   base=-(CMP - 1), pattern=[[P, MT], [-STRIDE, 16]],
                                   channel_multiplier=1).then_inc(masks_ready, 1)
            link(pool.memset(bd_mask[:, :], 1.0))
            link(pool.affine_select(out=bd_mask[:, :], in_=bd_mask[:, :], compare_op=ALU.is_ge, fill=0.0,
                                    base=0, pattern=[[-16, G]], channel_multiplier=1))
            pool.affine_select(out=bd_mask[:, :], in_=bd_mask[:, :], compare_op=ALU.is_ge, fill=0.0,
                               base=15, pattern=[[16, G]], channel_multiplier=-1).then_inc(masks_ready, 1)

            def post_gain(b, w, layer):
                pool.dma_start(g_post[:, :], bass.AP(w.tensor, layer * D, [[0, P], [1, D]]))\
                    .then_inc(gp_loaded[b - 1], 16)

            pool.wait_ge(kc_sum, 1)
            pool.wait_ge(hid_ready, 2)
            post_gain(1, norm_mix_post, 0)

            pool.wait_ge(o_ready[0], 2 * HK)
            link(pool.memset(mask_dil[:, :, 0:256], 0.0))
            link(pool.memset(mask_dil[:, :, 256:512], NEG))
            for hp in range(2):
                rows64 = slice(64 * hp, 64 * hp + 64)
                for m in range(MT):
                    p0 = mask_dil[rows64, m, 0:256].rearrange("p (r q) -> p r q", r=4)
                    link(pool.affine_select(out=p0, in_=p0, compare_op=ALU.is_ge, fill=NEG,
                                            base=2 * m + hp, pattern=[[-1, 4], [-4, 64]],
                                            channel_multiplier=4))
                    link(pool.affine_select(out=p0, in_=p0, compare_op=ALU.is_ge, fill=NEG,
                                            base=128 - 2 * m - hp, pattern=[[1, 4], [4, 64]],
                                            channel_multiplier=-4))
                    p1 = mask_dil[rows64, m, 256 + 64 * hp:320 + 64 * hp]
                    link(pool.memset(p1, 0.0))
                    link(pool.affine_select(out=p1, in_=p1, compare_op=ALU.is_ge, fill=NEG,
                                            base=0, pattern=[[-1, 64]], channel_multiplier=1))
                    p2 = mask_dil[rows64, m, 384 + 64 * hp:448 + 64 * hp]
                    for d in range(16):
                        link(pool.affine_select(out=p2, in_=p2, compare_op=ALU.not_equal, fill=0.0,
                                                base=-4 * d, pattern=[[-1, 64]], channel_multiplier=1))
            pool.sem_inc(dilmask_ready, 1)
            for b, w, layer in ((2, norm_ffn_post, 0), (3, norm_mix_post, 1), (4, norm_ffn_post, 1)):
                pool.wait_ge(h_ready[b - 1], 4)
                post_gain(b, w, layer)

        @block.scalar
        def _(act):
            def split(n, halves=(0, 1)):
                if isinstance(n, int):
                    n = Piece(n)
                if n.n0 >= N_END:
                    return
                for k in halves:
                    if k == 0:
                        act.wait_ge(raw_loaded[n.raw], n.loaded())
                        if n.n0 >= RING or not isinstance(n.it, int):
                            act.wait_ge(piece_used, n.used() - RING)
                    c = 1024 * k
                    act.activation(w_hi[:, n.slot, c:c + 1024], w_raw[:, n.raw, c:c + 1024], ACT.Copy)\
                       .then_inc(hi_ready, 1)

            def xt_out(b, m, half, gain, permuted=False):
                act.wait_ge(xt_psum[b], 2 * m + half + 1)
                for k in range(4):
                    kt = 4 * half + k
                    src, dst = xt_views(b, m, half, kt, xt_hi, permuted)
                    ins = act.activation(dst, src, ACT.Copy, scale=g_t[:, 8 * gain + kt:8 * gain + kt + 1])
                ins.then_inc(xt_hi_ready[b], 1)

            def h_squares(b, m):
                act.activation(tmp[:, m, :], h[:, m, :], ACT.Square, accum_out=ssq[:, m:m + 1])\
                   .then_inc(sq_h[b], 1)

            act.dma_start(rows[0:16, :], norm_mix_pre.rearrange("l (k p) -> (l k) p", p=P))\
               .then_inc(rows_loaded, 16)
            act.dma_start(rows[16:32, :], norm_ffn_pre.rearrange("l (k p) -> (l k) p", p=P))\
               .then_inc(rows_loaded, 16)
            act.dma_start(rows[32:48, :], nsa_cmp_pos[0].rearrange("(k a) d -> k (a d)", a=2))\
               .then_inc(rows_loaded, 16)
            act.dma_start(gw_raw[:, :, :], nsa_w_in[0].rearrange("(k p) c -> p k c", p=P)[:, :, 2560:2608])\
               .then_inc(gw_loaded, 16)
            act.dma_start(pos_i[:, 0:2], bass.AP(positions.tensor, 0, [[1, P], [P, 2]]),
                          allow_slow_non_contiguous=True)\
               .then_inc(pos_loaded, 16)
            for hp in range(2):
                act.dma_start(pos_i[64 * hp:64 * hp + 64, 2:4],
                              bass.AP(positions.tensor, hp, [[4, 64], [2, 2]]),
                              allow_slow_non_contiguous=True).then_inc(pos_loaded, 16)
            for dst, w in ((w2k[:, :, 0, :], nsa_cmp_wk2), (w2k[:, :, 1, :], nsa_cmp_wk2), (w2v[:, :, :], nsa_cmp_wv2)):
                act.dma_start(dst, w[0].rearrange("(k p) d -> p k d", p=P)).then_inc(w2_loaded, 16)
            act.wait_ge(angles_ready, 1)
            act.activation(sin2[:, :, 8:16], ang[:, :, :], ACT.Sin)
            act.activation(cos2[:, :, 0:8], half_pi[:, :, :], ACT.Sin).then_inc(rope_ready, 1)
            act.wait_ge(gt_ready, 1)
            for m in range(MT):
                for half in range(2):
                    xt_out(0, m, half, 0)
            for m in range(MT):
                act.wait_ge(x_loaded[m], 16)
                h_squares(0, m)
            act.wait_ge(gw_loaded, 16)
            act.activation(gw_hi[:, :, :], gw_raw[:, :, :], ACT.Copy).then_inc(gw_hi_ready, 1)
            for n in range(AHEAD):
                split(n)

            ev = [0]

            def proj_evac(dsts):
                e = ev[0]
                m = e % 2
                if e < 2:
                    act.wait_ge(rs_ready[0], m + 1)
                act.wait_ge(proj_done[0], e + 1)
                for dst, src in dsts(m):
                    ins = act.activation(dst, src, ACT.Copy, scale=rs[:, m:m + 1])
                ins.then_inc(proj_out[0], 1)
                ev[0] += 1

            def twice(stage, m, c):
                return (view(stage, m * 512, [[P, HK], [DH, 2], [1, DH]]),
                        view(ps, m * 512 + c, [[DH, HK], [0, 2], [1, DH]]))

            tv = [0]

            def turn_evac(parts):
                act.wait_ge(turned[0], tv[0] + 1)
                for dst, src in parts:
                    ins = act.activation(dst, src, ACT.Copy)
                ins.then_inc(turn_out[0], 1)
                tv[0] += 1

            def quads(b):
                return bank(b).rearrange("p (a t) -> p a t", a=4)

            split(3)
            proj_evac(lambda m: [twice(stage_nsa, m, 0), twice(stage_rot, m, 256)])
            split(4)
            proj_evac(lambda m: [twice(stage_nsa, m, 0), twice(stage_rot, m, 256)])
            act.wait_ge(gate_sum, 1)
            for m in range(MT):
                ins = act.activation(gates[:, m, :], bank(3, 48 * m, 48), ACT.Copy, scale=rs[:, m:m + 1])
            ins.then_inc(gate_exp, 1)
            act.wait_ge(gate_exp, 1)
            act.activation(gates[:, :, :], gates[:, :, :], ACT.Exp, scale=-1.0).then_inc(gate_exp, 1)

            def pair_evac(m, b, kv, eng, s, fn):
                t = view(ps, b * 512, [[P, 4], [1, P]], n=64)
                fn(view(pair, kv * HK * S + m * P, [[S, 4], [1, P]], n=64), t)
                lo = 1 if m == 0 else 0
                return fn(view(pair, kv * HK * S + m * P - 1 + lo, [[S, 4], [1, P - lo]], p0=64, n=64),
                          view(ps, b * 512 + lo, [[P, 4], [1, P - lo]], p0=64, n=64))

            split(5)
            act.wait_ge(turned[0], 1)
            pair_evac(0, 2, 0, act, None, lambda d, s: act.activation(d, s, ACT.Copy)).then_inc(pair_act, 1)
            proj_evac(lambda m: [twice(stage_nsa, m, 0), (v_nsa[:, 0, m, :], bank(m, 256, 256))])
            act.wait_ge(turned[0], 2)
            pair_evac(1, 5, 0, act, None, lambda d, s: act.activation(d, s, ACT.Copy)).then_inc(pair_act, 1)
            tv[0] = 2
            proj_evac(lambda m: [twice(stage_nsa, m, 0), (v_nsa[:, 0, m, :], bank(m, 256, 256))])
            split(6)
            act.wait_ge(tb_f_ready, 1)
            act.activation(st_hi[:, :], tb_f[:, :, :, :].rearrange("p a b c -> p (a b c)"), ACT.Copy)\
               .then_inc(tb_hi_ready, 1)
            turn_evac([(k_t[:, 0, :, 0:P], quads(7))])
            turn_evac([(k_t[:, 0, :, P:S], quads(2))])
            split(7)

            def hid_step(kv):
                act.wait_ge(hid_sum, kv + 1)
                act.activation(e_hid[:, kv, :], bank(3, P * (kv + 1), P), ACT.Exp, scale=-1.0)\
                   .then_inc(hid_exp, 1)

            hid_step(0)
            split(8)
            proj_evac(lambda m: [twice(stage_nsa, m, 0), (v_nsa[:, 1, m, :], bank(m, 256, 256))])
            proj_evac(lambda m: [twice(stage_nsa, m, 0), (v_nsa[:, 1, m, :], bank(m, 256, 256))])
            act.wait_ge(tb_f_ready, 2)
            act.wait_ge(hid_sum, 1)
            act.activation(st_hi[:, :], tb_f[:, :, :, :].rearrange("p a b c -> p (a b c)"), ACT.Copy)\
               .then_inc(tb_hi_ready, 1)
            split(9)
            turn_evac([(k_t[:, 1, :, 0:P], quads(4))])
            turn_evac([(k_t[:, 1, :, P:S], quads(5))])
            split(10)
            split(11)
            hid_step(1)
            split(12)
            for c in range(2):
                for m in range(MT):
                    proj_evac(lambda m: [(stage_nsa[:, m, :], bank(m)), (stage_rot[:, m, :], bank(m))])
                    if c == 0:
                        split(13 + m)
                    elif m == 0:
                        split(15)
                        turn_evac([(qu_t[:, 0:4, P:S], quads(4)), (q_t[:, 0:4, P:S], quads(5))])
                    if c == 0 and m == 1:
                        turn_evac([(qu_t[:, 0:4, 0:P], quads(7)), (q_t[:, 0:4, 0:P], quads(2))])
                    if c == 0 and m == 0:
                        act.wait_ge(kc_sum, 1)
                        act.activation(kc_t[:, :], bank(6, 0, 64), ACT.Copy).then_inc(kc_out, 1)
            split(16)
            turn_evac([(qu_t[:, 4:8, 0:P], quads(7)), (q_t[:, 4:8, 0:P], quads(2))])
            turn_evac([(qu_t[:, 4:8, P:S], quads(4)), (q_t[:, 4:8, P:S], quads(5))])

            def exp_nsa(u):
                hk, m, g = u // 8, u // 4 % 2, u % 4
                n = P * (m + 1)
                if u >= 12 and g == 0:
                    act.wait_ge(o_ready[0], u // 4 - 2)
                act.wait_ge(masked[0], u + 1)
                for br in range(2):
                    s = probs[:, u % 3, br * n:(br + 1) * n]
                    ins = act.activation(s, s, ACT.Exp, bias=nm[:, u % 3, br:br + 1], scale=SCALE,
                                         accum_out=l_nsa[:, (u // 4) % 3, g, br:br + 1])
                ins.then_inc(expd[0], 1)

            def pt_evac(i, u, n):
                act.wait_ge(pt_psum[i], u + 1)
                act.activation(p_t[:, u % 2, 0:n], bank(3 + u % 2, 0, n), ACT.Copy)\
                   .then_inc(pt_out[i], 1)

            def ot_evac(grp):
                act.wait_ge(ot_psum[0], grp + 1)
                hk, m = grp // 2, grp % 2
                act.activation(xt_hi[:, 2 * hk:2 * hk + 2, m * P:(m + 1) * P],
                               bank(7, 256, 256).rearrange("p (a t) -> p a t", a=2), ACT.Copy)\
                   .then_inc(ot_hi[0], 1)

            act.wait_ge(sc_ready, 1)
            act.activation(p_cmp[:, :, :, :], p_cmp[:, :, :, :], ACT.Exp, scale=SCALE).then_inc(pc_exp, 1)
            U = 2 * H
            for s in range(U + 9):
                if s < U:
                    exp_nsa(s)
                if s in (4, 6):
                    r = (s - 4) // 2
                    act.wait_ge(pct_psum, r + 1)
                    act.activation(pc_t[:, 4 * r:4 * r + 4, :],
                                   view(ps, 7 * 512, [[P, 4], [1, P]], n=64), ACT.Copy).then_inc(pct_out, 1)
                if 2 <= s < U + 2:
                    u = s - 2
                    pt_evac(0, u, 2 * P * (u // 4 % 2 + 1))
                if s >= 12 and s % 4 == 0:
                    ot_evac((s - 12) // 4)
            def post_squares(b, m):
                act.wait_ge(acc_done[b], m + 1)
                act.activation(tmp[:, m, :], ps[:, 2 * m:2 * m + 2, :].rearrange("p a c -> p (a c)"),
                               ACT.Square, accum_out=ssq[:, MT + m:MT + m + 1]).then_inc(sq_post[b], 1)

            def to_ffn(b, n, gain):
                split(n + 3)
                split(n + 4)
                split(n + 5)
                post_squares(b, 0)
                xt_out(b, 0, 0, gain)
                xt_out(b, 0, 1, gain)
                act.wait_ge(h_ready[b], 2)
                h_squares(b, 0)
                split(n + 6)
                post_squares(b, 1)
                xt_out(b, 1, 0, gain)
                xt_out(b, 1, 1, gain)
                act.wait_ge(h_ready[b], 4)
                h_squares(b, 1)

            def ffn(layer, n0):
                b = 1 + 2 * layer

                def silu_step(j, m):
                    act.wait_ge(gu_done[layer], j * 2 + m + 1)
                    act.activation(silu[:, m, :], bank(4 + m, 0, 256), ACT.Silu, scale=rs[:, m:m + 1])\
                       .then_inc(silu_done[layer], 1)

                def ht_out(j, m):
                    act.wait_ge(ht_psum[layer], j * 2 + m + 1)
                    act.activation(view(st_hi, m * P, [[S, 2], [1, P]]),
                                   bank(6 + m, 0, 256).rearrange("p (a t) -> p a t", a=2), ACT.Copy)\
                       .then_inc(ht_hi[layer], 1)

                def step(j, nx):
                    split(nx)
                    ht_out(j - 1, 1)
                    split(nx + 1, (0,))
                    silu_step(j, 0)
                    split(nx + 1, (1,))
                    split(nx + 2, (0,))
                    ht_out(j, 0)
                    split(nx + 2, (1,))
                    silu_step(j, 1)

                act.wait_ge(rs_ready[b], 1)
                split(Piece(n0 + 3), (0,))
                silu_step(0, 0)
                split(Piece(n0 + 3), (1,))
                split(Piece(n0 + 4), (0,))
                ht_out(0, 0)
                split(Piece(n0 + 4), (1,))
                act.wait_ge(rs_ready[b], 2)
                silu_step(0, 1)
                step(1, Piece(n0 + 5))
                with act.Fori(0, (FJ - 3) // 2) as it:
                    for s in range(2):
                        step(it * 2 + (2 + s), Piece(n0 + 8 + 3 * s, it))
                step(FJ - 1, Piece(n0 + 3 * FJ - 1))
                ht_out(FJ - 1, 1)
                split(n0 + FFN_PIECES + 2)

            to_ffn(1, N_NSAO, 2)
            ffn(0, N_FFN0)
            for m in range(MT):
                post_squares(2, m)
                act.wait_ge(h_ready[2], 2 * m + 2)
                h_squares(2, m)
            for m in range(MT):
                for half in range(2):
                    xt_out(2, m, half, 1, permuted=True)

            act.sem_inc(proj_out[1], 2)
            act.sem_inc(turn_out[1], 2)

            def dil_proj(hg, pat):
                e0 = 18 * hg
                t0 = 12 * hg

                def evac(c, m):
                    act.wait_ge(proj_done[1], pat * 6 + (e0 + 2 * c + m + 1))
                    dst = stage_dil[:, m, :] if c < 2 else view(v_dil, pat * (MT * 512) + m * 512, [[1, 512]])
                    act.activation(dst, bank(m), ACT.Copy).then_inc(proj_out[1], 1)

                def turn(c, m):
                    act.wait_ge(turned[1], pat * 4 + (t0 + 2 * c + m + 1))
                    act.activation(view(qk_t, pat * (2 * 4 * S) + (c * 4 * S + m * P), [[S, 4], [1, P]]),
                                   bank(2 + m).rearrange("p (a t) -> p a t", a=4), ACT.Copy)\
                       .then_inc(turn_out[1], 1)

                n = Piece(N_DIL + 18 * hg + AHEAD, pat)
                split(n)
                evac(0, 0)
                split(n + 1)
                evac(0, 1)
                split(n + 2, (0,))
                turn(0, 0)
                split(n + 2, (1,))
                evac(1, 0)
                turn(0, 1)
                split(n + 3)
                evac(1, 1)
                split(n + 4, (0,))
                turn(1, 0)
                split(n + 4, (1,))
                evac(2, 0)
                split(n + 5)
                evac(2, 1)
                turn(1, 1)

            def exp_dil(hg, u):
                w = 16 * hg + u
                act.wait_ge(masked[1], w + 1)
                s = probs[:, u % 3, :]
                act.activation(s, s, ACT.Exp, bias=nm[:, u % 3, 0:1], scale=SCALE,
                               accum_out=l_dil[:, u % 2, u // 2:u // 2 + 1]).then_inc(expd[1], 1)

            def ot_dil(hg, m):
                act.wait_ge(ot_psum[1], 2 * hg + m + 1)
                src, dst = ot_views(hg, m, xt_hi)
                act.activation(dst, src, ACT.Copy).then_inc(ot_hi[1], 1)

            for hg in range(2):
                with act.Fori(0, 3) as pat:
                    dil_proj(hg, pat)
                for s in range(16 + 2):
                    if s < 16:
                        exp_dil(hg, s)
                    if s >= 2:
                        u = s - 2
                        if u % 2 == 0:
                            act.wait_ge(pt_psum[1], 16 * hg + u + 1)
                            act.activation(p_t[:, 0, :], bank(3), ACT.Copy).then_inc(pt_out[1], 1)
                    if hg == 1 and s in (5, 8):
                        ot_dil(0, 0 if s == 5 else 1)
            for m in range(MT):
                ot_dil(1, m)
            to_ffn(3, N_DILO, 3)
            ffn(1, N_FFN1)
            for m in range(MT):
                post_squares(4, m)

        @block.vector
        def _(dve):
            done = [0]

            def link(ins):
                done[0] += 1
                ins.then_inc(dve_step, 1)
                dve.wait_ge(dve_step, done[0])

            def split(n, halves=(0, 1)):
                if isinstance(n, int):
                    n = Piece(n)
                if n.n0 >= N_END:
                    return
                for k in halves:
                    dve.wait_ge(hi_ready, n.halves(k + 1))
                    c = 1024 * k
                    dve.tensor_tensor(w_lo[:, n.slot, c:c + 1024], w_raw[:, n.raw, c:c + 1024],
                                      w_hi[:, n.slot, c:c + 1024].bitcast(F32), ALU.subtract)\
                       .then_inc(lo_ready, 1)

            def rsqrt(total, dst):
                v, hv, y, t = (nt[:, i:i + 1] for i in range(4))
                link(dve.tensor_scalar(v, total, 1.0 / D, EPS, ALU.mult, ALU.add))
                link(dve.tensor_scalar(y.bitcast(I32), v.bitcast(I32), 1, None, ALU.logical_shift_right))
                link(dve.tensor_scalar(y.bitcast(I32), y.bitcast(I32), -1.0, float(0x5F3759DF),
                                       ALU.mult, ALU.add))
                link(dve.tensor_scalar(hv, v, -0.5, None, ALU.mult))
                for i in range(3):
                    link(dve.scalar_tensor_tensor(t, y, hv, y, ALU.mult, ALU.mult))
                    last = dve.scalar_tensor_tensor(y if i < 2 else dst, t, 1.5, y, ALU.add, ALU.mult)
                    if i < 2:
                        link(last)
                return last

            def h_rs(b, m):
                dve.wait_ge(sq_h[b], m + 1)
                rsqrt(ssq[:, m:m + 1], rs[:, m:m + 1]).then_inc(rs_ready[b], 1)
                dve.wait_ge(rs_ready[b], m + 1)

            def xt_lo_out(b, m, half, gain, permuted=False):
                dve.wait_ge(xt_hi_ready[b], 2 * m + half + 1)
                for k in range(4):
                    kt = 4 * half + k
                    src, dst = xt_views(b, m, half, kt, xt_lo, permuted)
                    _, hi = xt_views(b, m, half, kt, xt_hi, permuted)
                    ins = dve.scalar_tensor_tensor(dst, src, g_t[:, 8 * gain + kt:8 * gain + kt + 1],
                                                   hi.bitcast(F32), ALU.mult, ALU.subtract)
                ins.then_inc(xt_ready[b], 1)

            dve.wait_ge(rows_t, 1)
            dve.tensor_copy(g_t[:, :], bank(2, 0, 48)).then_inc(gt_ready, 1)
            dve.wait_ge(pos_loaded, 48)
            dve.wait_ge(rope_ready, 1)
            link(dve.tensor_copy(pos_f[:, :], pos_i[:, :]))
            link(dve.tensor_tensor(ang[:, :, :], view(pos_f, 0, [[1, 4], [0, 8]]),
                                   view(inv_f, 0, [[0, 4], [1, 8]]), ALU.mult))
            link(dve.tensor_scalar(turns[:, :, :], ang[:, :, :], 1.0 / TWO_PI, MAGIC, ALU.mult, ALU.add))
            link(dve.tensor_scalar(turns[:, :, :], turns[:, :, :], MAGIC, None, ALU.subtract))
            c1 = 6.28125
            c2 = float(np.floor((TWO_PI - c1) * 2.0 ** 21) / 2.0 ** 21)
            for c in (c1, c2, TWO_PI - c1 - c2):
                link(dve.scalar_tensor_tensor(ang[:, :, :], turns[:, :, :], -c, ang[:, :, :],
                                              ALU.mult, ALU.add))
            link(dve.tensor_scalar(ang[:, :, :], ang[:, :, :], 3.1415925, -3.1415925, ALU.min, ALU.max))
            link(dve.scalar_tensor_tensor(half_pi[:, :, :], ang[:, :, :], -1.0, ang[:, :, :],
                                          ALU.mult, ALU.min))
            dve.tensor_scalar(half_pi[:, :, :], half_pi[:, :, :], TWO_PI / 4, None, ALU.add)\
               .then_inc(angles_ready, 1)
            for m in range(MT):
                for half in range(2):
                    xt_lo_out(0, m, half, 0)
            dve.wait_ge(rope_ready, 2)
            dve.tensor_scalar(sin2[:, :, 0:8], sin2[:, :, 8:16], -1.0, None, ALU.mult)
            link(dve.tensor_copy(cos2[:, :, 8:16], cos2[:, :, 0:8]))
            for m in range(MT):
                h_rs(0, m)
            dve.wait_ge(gw_hi_ready, 1)
            dve.tensor_tensor(gw_lo[:, :, :], gw_raw[:, :, :], gw_hi[:, :, :].bitcast(F32), ALU.subtract)\
               .then_inc(gw_ready, 1)
            for n in range(AHEAD):
                split(n)

            def rope(i, e, stage, m, heads, table):
                a, b = rope_a[:, 0:heads, :], rope_b[:, 0:heads, :]
                x16 = view(stage, m * 512, [[DH, heads], [1, ROT]])
                x1 = view(stage, m * 512, [[DH, heads], [1, 8]])
                x2 = view(stage, m * 512 + 8, [[DH, heads], [1, 8]])
                dve.wait_ge(proj_out[i], e)
                dve.tensor_tensor(a, x16, view(cos2, table * ROT, [[0, heads], [1, ROT]]), ALU.mult)
                dve.tensor_tensor(rope_b[:, 0:heads, 0:8], x2, view(sin2, table * ROT, [[0, heads], [1, 8]]),
                                  ALU.mult)
                link(dve.tensor_tensor(rope_b[:, 0:heads, 8:16], x1,
                                       view(sin2, table * ROT + 8, [[0, heads], [1, 8]]), ALU.mult))
                dve.tensor_tensor(x16, a, b, ALU.add).then_inc(roped[i], 1)
                dve.wait_ge(roped[i], e - 2)

            split(3)
            split(4)

            def pair_copy(m, b):
                t = view(ps, b * 512, [[P, 4], [1, P]], n=64)
                dve.tensor_copy(view(pair, HK * S + m * P, [[S, 4], [1, P]], n=64), t)
                lo = 1 if m == 0 else 0
                return dve.tensor_copy(
                    view(pair, HK * S + m * P - 1 + lo, [[S, 4], [1, P - lo]], p0=64, n=64),
                    view(ps, b * 512 + lo, [[P, 4], [1, P - lo]], p0=64, n=64))

            dve.wait_ge(turned[0], 1)
            pair_copy(0, 4).then_inc(pair_dve, 1)
            split(5)
            rope(0, 3, stage_nsa, 0, 2 * HK, 0)
            dve.wait_ge(turned[0], 2)
            pair_copy(1, 6).then_inc(pair_dve, 1)
            rope(0, 4, stage_nsa, 1, 2 * HK, 1)
            split(6)

            def blocks(kv):
                n = 0
                for k0 in (0, 8):
                    ins = dve.tensor_tensor(view(tb_f, k0 * 64, [[64, 8], [16, HK], [1, NC]]),
                                            view(pair, kv * HK * S + 2 * k0, [[2, 8], [S, HK], [STRIDE, NC]]),
                                            view(g_t, 32 + k0, [[1, 8], [0, HK], [0, NC]]), ALU.add)
                ins.then_inc(tb_f_ready, 1)

            def block_lo(kv):
                dve.wait_ge(tb_hi_ready, kv + 1)
                dve.tensor_tensor(st_lo[:, :], tb_f[:, :, :, :].rearrange("p a b c -> p (a b c)"),
                                  st_hi[:, :].bitcast(F32), ALU.subtract).then_inc(tb_ready, 1)

            dve.wait_ge(pair_act, 2)
            link(dve.memset(tb_f[:, :, :, :], 0.0))
            blocks(0)
            block_lo(0)
            split(7)

            def hid_out(kv):
                dve.wait_ge(hid_exp, kv + 1)
                e = e_hid[:, kv, :]
                link(dve.tensor_scalar(e, e, 1.0, None, ALU.add))
                link(dve.reciprocal(e, e))
                if kv == 0:
                    last = dve.tensor_tensor(hid_k[:, :], bank(3, P, P), e, ALU.mult)
                else:
                    last = dve.tensor_tensor(hid_v[:, :, :, :],
                                             view(ps, 3 * 512 + 2 * P, [[16, 2 * HK], [0, G], [1, 16]]),
                                             view(e_hid, P, [[16, 2 * HK], [0, G], [1, 16]]), ALU.mult)
                last.then_inc(hid_ready, 1)

            blocks(1)
            hid_out(0)
            split(8)
            rope(0, 5, stage_nsa, 0, 2 * HK, 0)
            rope(0, 6, stage_nsa, 1, 2 * HK, 1)
            block_lo(1)
            split(9)
            split(10)
            split(11)
            hid_out(1)
            split(12)
            for c in range(2):
                for m in range(MT):
                    rope(0, 7 + 2 * c + m, stage_rot, m, 8, m)
                    if c == 0:
                        split(13 + m)
                    elif m == 0:
                        split(15)
                    if c == 0 and m == 0:
                        dve.wait_ge(kc_out, 1)
                        dve.wait_ge(masks_ready, 4)
                        for hk in range(HK):
                            ins = dve.tensor_tensor(
                                view(vc_bd, hk * G * DH, [[DH, G], [1, DH]], n=64),
                                view(ps, 6 * 512 + P + hk * DH, [[0, G], [1, DH]], n=64),
                                view(bd_mask, 0, [[1, G], [0, DH]], n=64), ALU.mult)
                        ins.then_inc(vc_out, 1)
            split(16)
            dve.wait_ge(gate_exp, 2)
            flat = gates[:, :, :].rearrange("p a b -> p (a b)")
            link(dve.tensor_scalar(flat, flat, 1.0, None, ALU.add))
            link(dve.reciprocal(flat, flat))
            dve.wait_ge(sc_sum, 1)
            for odd, b in enumerate((6, 3)):
                last = dve.tensor_tensor(view(p_cmp, 16 * odd, [[256, MT], [32, H // 2], [1, 16]]),
                                         view(ps, b * 512, [[128, MT], [16, H // 2], [1, 16]]),
                                         view(mask_c, 0, [[16, MT], [0, H // 2], [1, 16]]), ALU.add)
            link(last)
            pcf = p_cmp[:, :, :, :].rearrange("p m a c -> p (m a) c")
            link(dve.tensor_reduce(mx_c[:, :], pcf, AX, ALU.max))
            dve.tensor_tensor(pcf, pcf, view(mx_c, 0, [[1, MT * H], [0, 16]]), ALU.subtract)\
               .then_inc(sc_ready, 1)

            def mask_nsa_unit(u):
                m = u // 4 % 2
                n = P * (m + 1)
                dve.wait_ge(scores[0], u + 1)
                if u >= 3:
                    dve.wait_ge(pt_psum[0], u - 2)
                for br in range(2):
                    ins = dve.tensor_tensor_reduce(
                        out=probs[:, u % 3, br * n:(br + 1) * n], in0=bank(u % 3, br * n, n),
                        in1=mask_nsa[:, 2 * P - n:2 * P], scale=1.0, scalar=-INF, op0=ALU.add, op1=ALU.max,
                        accum_out=mx[:, u % 3, br:br + 1])
                link(ins)
                dve.tensor_scalar(nm[:, u % 3, :], mx[:, u % 3, :], -SCALE, None, ALU.mult)\
                   .then_inc(masked[0], 1)

            def combine(grp):
                hk, m = grp // 2, grp % 2
                link(dve.reciprocal(coef[:, :, :], l_nsa[:, grp % 3, :, :]))
                link(dve.tensor_tensor(coef[:, :, :], coef[:, :, :],
                                       view(gates, 48 * m + 16 + 4 * hk, [[1, G], [16, 2]]), ALU.mult))
                dve.wait_ge(pv_done[0], 4 * grp + 4)
                dve.tensor_tensor(comb[:, :, :, :].rearrange("p g b d -> p (g b) d"),
                                  bank(5 + grp % 2).rearrange("p (a d) -> p a d", a=2 * G),
                                  view(coef, 0, [[1, 2 * G], [0, DH]]), ALU.mult)
                dve.wait_ge(ocmp_sum, grp + 1)
                o = view(tmp, m * D + hk * 256, [[DH, G], [1, DH]])
                link(dve.tensor_tensor(o, bank(7, 0, 256).rearrange("p (a d) -> p a d", a=G),
                                       view(l_c, 16 * m + 4 * hk, [[1, G], [0, DH]]), ALU.mult))
                link(dve.tensor_tensor(o, o, comb[:, :, 0, :], ALU.add))
                dve.tensor_tensor(o, o, comb[:, :, 1, :], ALU.add).then_inc(o_ready[0], 1)

            def ot_lo(grp):
                hk, m = grp // 2, grp % 2
                dve.wait_ge(ot_hi[0], grp + 1)
                dst = slice(2 * hk, 2 * hk + 2), slice(m * P, (m + 1) * P)
                dve.tensor_tensor(xt_lo[:, dst[0], dst[1]],
                                  bank(7, 256, 256).rearrange("p (a t) -> p a t", a=2),
                                  xt_hi[:, dst[0], dst[1]].bitcast(F32), ALU.subtract)\
                   .then_inc(ot_ready[0], 1)

            U = 2 * H
            for s in range(U + 9):
                if s == 2:
                    dve.wait_ge(pc_exp, 1)
                    link(dve.tensor_reduce(l_c[:, :], pcf, AX, ALU.add))
                    for m in range(MT):
                        last = dve.tensor_tensor(p_cmp[:, m, :, :], p_cmp[:, m, :, :],
                                                 view(valid_c, 16 * m, [[0, H], [1, 16]]), ALU.mult)
                    last.then_inc(pc_ready, 1)
                    link(dve.reciprocal(l_c[:, :], l_c[:, :]))
                    lc2 = l_c[:, :].rearrange("p (m a) -> p m a", m=MT)
                    link(dve.tensor_tensor(lc2, lc2, gates[:, :, 0:16], ALU.mult))
                if s < U:
                    mask_nsa_unit(s)
                if s >= 9 and s % 4 == 1 and s < U + 9:
                    combine((s - 9) // 4)
                if s >= 12 and s % 4 == 0:
                    ot_lo((s - 12) // 4)

            def add_post(b, m):
                dve.wait_ge(sq_post[b], m + 1)
                link(rsqrt(ssq[:, MT + m:MT + m + 1], rs_post[:, m:m + 1]))
                if m == 0:
                    dve.wait_ge(gp_loaded[b - 1], 16)
                for half in range(2):
                    c = slice(512 * half, 512 * half + 512)
                    link(dve.scalar_tensor_tensor(tmp[:, m, c], bank(2 * m + half), rs_post[:, m:m + 1],
                                                  g_post[:, c], ALU.mult, ALU.mult))
                    dve.tensor_tensor(h[:, m, c], h[:, m, c], tmp[:, m, c], ALU.add).then_inc(h_ready[b], 1)

            def to_ffn(b, n, gain):
                split(n + 3)
                split(n + 4)
                split(n + 5)
                add_post(b, 0)
                xt_lo_out(b, 0, 0, gain)
                xt_lo_out(b, 0, 1, gain)
                h_rs(b, 0)
                split(n + 6)
                add_post(b, 1)
                xt_lo_out(b, 1, 0, gain)
                xt_lo_out(b, 1, 1, gain)
                h_rs(b, 1)

            def ffn(layer, n0):
                def hs_step(j, m):
                    dve.wait_ge(silu_done[layer], j * 2 + m + 1)
                    dve.scalar_tensor_tensor(hs[:, m, :], bank(4 + m, 256, 256), rs[:, m:m + 1],
                                             silu[:, m, :], ALU.mult, ALU.mult).then_inc(hs_ready[layer], 1)

                def ht_out(j, m):
                    dve.wait_ge(ht_hi[layer], j * 2 + m + 1)
                    hi = view(st_hi, m * P, [[S, 2], [1, P]])
                    dve.tensor_tensor(view(st_lo, m * P, [[S, 2], [1, P]]),
                                      bank(6 + m, 0, 256).rearrange("p (a t) -> p a t", a=2),
                                      hi.bitcast(F32), ALU.subtract).then_inc(ht_ready[layer], 1)

                def step(j, nx):
                    split(nx)
                    ht_out(j - 1, 1)
                    split(nx + 1, (0,))
                    hs_step(j, 0)
                    split(nx + 1, (1,))
                    split(nx + 2, (0,))
                    ht_out(j, 0)
                    split(nx + 2, (1,))
                    hs_step(j, 1)

                split(Piece(n0 + 3), (0,))
                hs_step(0, 0)
                split(Piece(n0 + 3), (1,))
                split(Piece(n0 + 4), (0,))
                ht_out(0, 0)
                split(Piece(n0 + 4), (1,))
                hs_step(0, 1)
                step(1, Piece(n0 + 5))
                with dve.Fori(0, (FJ - 3) // 2) as it:
                    for s in range(2):
                        step(it * 2 + (2 + s), Piece(n0 + 8 + 3 * s, it))
                step(FJ - 1, Piece(n0 + 3 * FJ - 1))
                ht_out(FJ - 1, 1)
                split(n0 + FFN_PIECES + 2)

            to_ffn(1, N_NSAO, 2)
            ffn(0, N_FFN0)
            for m in range(MT):
                add_post(2, m)
                h_rs(2, m)
                dve.tensor_scalar(tmp[:, m, :], h[:, m, :], rs[:, m:m + 1], None, ALU.mult)\
                   .then_inc(xn_ready, 1)
            for m in range(MT):
                for half in range(2):
                    xt_lo_out(2, m, half, 1, permuted=True)

            def dil_proj(hg, pat):
                e0 = 18 * hg

                def rot(c, m):
                    rope_dil(pat * 6 + (e0 + 2 * c + m + 3), pat * 4 + (12 * hg + 2 * c + m + 1), m)

                n = Piece(N_DIL + 18 * hg + AHEAD, pat)
                split(n)
                rot(0, 0)
                split(n + 1)
                rot(0, 1)
                split(n + 2)
                rot(1, 0)
                split(n + 3)
                rot(1, 1)
                split(n + 4)
                split(n + 5)

            def rope_dil(staged, products, m):
                x16 = view(stage_dil, m * 512, [[DH, 8], [1, ROT]])
                table = 2 + m
                dve.wait_ge(proj_out[1], staged)
                dve.tensor_tensor(rope_a[:, :, :], x16, view(cos2, table * ROT, [[0, 8], [1, ROT]]), ALU.mult)
                dve.tensor_tensor(rope_b[:, :, 0:8], view(stage_dil, m * 512 + 8, [[DH, 8], [1, 8]]),
                                  view(sin2, table * ROT, [[0, 8], [1, 8]]), ALU.mult)
                dve.tensor_tensor(rope_b[:, :, 8:16], view(stage_dil, m * 512, [[DH, 8], [1, 8]]),
                                  view(sin2, table * ROT + 8, [[0, 8], [1, 8]]), ALU.mult)\
                   .then_inc(rope_parts, 1)
                dve.wait_ge(rope_parts, products)
                dve.tensor_tensor(x16, rope_a[:, :, :], rope_b[:, :, :], ALU.add).then_inc(roped[1], 1)
                dve.wait_ge(roped[1], products)

            def mask_dil_unit(hg, u):
                w = 16 * hg + u
                dve.wait_ge(scores[1], w + 1)
                if u >= 3:
                    dve.wait_ge(pt_psum[1], w - 2)
                link(dve.tensor_tensor_reduce(out=probs[:, u % 3, :], in0=bank(u % 3), in1=mask_dil[:, u % 2, :],
                                              scale=1.0, scalar=-INF, op0=ALU.add, op1=ALU.max,
                                              accum_out=mx[:, u % 3, 0:1]))
                dve.tensor_scalar(nm[:, u % 3, 0:1], mx[:, u % 3, 0:1], -SCALE, None, ALU.mult)\
                   .then_inc(masked[1], 1)

            def ot_dil(hg, m):
                dve.wait_ge(ot_hi[1], 2 * hg + m + 1)
                src, dst = ot_views(hg, m, xt_lo)
                _, hi = ot_views(hg, m, xt_hi)
                dve.tensor_tensor(dst, src, hi.bitcast(F32), ALU.subtract).then_inc(ot_ready[1], 1)

            for hg in range(2):
                with dve.Fori(0, 3) as pat:
                    dil_proj(hg, pat)
                if hg == 0:
                    dve.wait_ge(dilmask_ready, 1)
                for s in range(16 + 2):
                    if s < 16:
                        mask_dil_unit(hg, s)
                    if s >= 2 and s % 2 == 1:
                        dve.wait_ge(pt_psum[1], 16 * hg + s - 2 + 1)
                        dve.tensor_copy(p_t[:, 1, :], bank(4)).then_inc(pt_out_dve, 1)
                    if hg == 1 and s in (5, 8):
                        ot_dil(0, 0 if s == 5 else 1)
                dve.wait_ge(pv_done[1], 16 * hg + 16)
                link(dve.reciprocal(rl_dil[:, :, :], l_dil[:, :, :]))
                for m in range(MT):
                    dve.tensor_tensor(view(tmp, m * D + hg * 512, [[DH, 8], [1, DH]]),
                                      bank(5 + m).rearrange("p (a d) -> p a d", a=8),
                                      view(rl_dil, m * 8, [[1, 8], [0, DH]]), ALU.mult).then_inc(o_ready[1], 1)
            for m in range(MT):
                ot_dil(1, m)
            to_ffn(3, N_DILO, 3)
            ffn(1, N_FFN1)
            for m in range(MT):
                add_post(4, m)

        @block.tensor
        def _(pe):
            owed = [0]

            def mm(o, s, m, start, stop):
                ins = pe.matmul(o, s, m, start=start, stop=stop)
                if owed[0]:
                    owed[0] = 0
                    ins.then_inc(piece_used, 1)
                    return None
                return ins

            def turn(b, k, src, n=P):
                ins = pe.transpose(ps[0:n, b, P * k:P * k + P], src, ident[:, :])
                if owed[0]:
                    owed[0] = 0
                    ins.then_inc(piece_used, 1)
                    return None
                return ins

            def three(o, s_hi, s_lo, m_hi, m_lo, start, stop):
                mm(o, s_hi, m_hi, start, False)
                mm(o, s_hi, m_lo, False, False)
                return mm(o, s_lo, m_hi, False, stop)

            def gemm(b, m, pc, first, last, done=None, mid=None, need=None):
                for half in range(2):
                    if half and mid:
                        mid()
                    if need:
                        need(half)
                    p = pc + half
                    for u in range(4):
                        if first and u % 2 == 0:
                            pe.wait_ge(lo_ready, p.halves(u // 2 + 1))
                        kt, c = 4 * half + u, 512 * u
                        cols = slice(m * P, (m + 1) * P)
                        ins = three(bank(b), xt_hi[:, kt, cols], xt_lo[:, kt, cols],
                                    w_hi[:, p.slot, c:c + 512], w_lo[:, p.slot, c:c + 512],
                                    kt == 0, kt == KT - 1)
                    if half == 0:
                        if last:
                            ins.then_inc(piece_used, 1)
                    elif done is not None:
                        ins.then_inc(done, 1)
                        owed[0] = int(last)
                    elif last:
                        ins.then_inc(piece_used, 1)

            def xt_turn(b, m, half, src):
                base = {0: 4 + 2 * m, 2: 6 - 2 * m}.get(b, 6)
                for k in range(4):
                    kt = 4 * half + k
                    ins = turn(base + half, k, src[:, m, kt * P:(kt + 1) * P])
                ins.then_inc(xt_psum[b], 1)

            pe.wait_ge(ident_ready, 1)
            pe.wait_ge(rows_loaded, 48)
            pe.transpose(bank(2, 0, 48), rows[:, :], ident[0:48, 0:48]).then_inc(rows_t, 1)
            for m in range(MT):
                pe.wait_ge(x_loaded[m], 16)
                for half in range(2):
                    xt_turn(0, m, half, h)

            def nsa_gemm(e, n):
                if e >= 2:
                    pe.wait_ge(proj_out[0], e - 1)
                m = e % 2
                need = (lambda half: pe.wait_ge(xt_ready[0], 2 * m + half + 1)) if e < 2 else None
                gemm(m, m, Piece(n), m == 0, m == 1, done=proj_done[0], need=need)

            def turn_cmp(m, banks):
                pe.wait_ge(proj_out[0], m + 1)
                for stage, b in zip((stage_nsa, stage_rot), banks):
                    for k in range(HK):
                        ins = turn(b, k, stage[:, m, P * k:P * k + P])
                ins.then_inc(turned[0], 1)

            def turn_kv(t, m, b):
                pe.wait_ge(roped[0], t + 1)
                for k in range(HK):
                    ins = turn(b, k, stage_nsa[:, m, P * k:P * k + P])
                ins.then_inc(turned[0], 1)

            def turn_q(t, m, b_plain, b_rot):
                pe.wait_ge(roped[0], t + 1)
                for stage, b in ((stage_nsa, b_plain), (stage_rot, b_rot)):
                    for k in range(4):
                        ins = turn(b, k, stage[:, m, P * k:P * k + P])
                ins.then_inc(turned[0], 1)

            def compress(kv, n):
                pe.wait_ge(lo_ready, Piece(n + 1).halves(2))
                pe.wait_ge(tb_ready, kv + 1)
                for hh in range(2):
                    for kt in range(16):
                        c = (kt % 8) * 256 + hh * P
                        slot = Piece(n + kt // 8).slot
                        o = bank(3, P * (kv + 1) + 64 * hh, 64)
                        w1h, w1l = w_hi[:, slot, c:c + P], w_lo[:, slot, c:c + P]
                        xh, xl = st_hi[:, 64 * kt:64 * kt + 64], st_lo[:, 64 * kt:64 * kt + 64]
                        mm(o, w1h, xh, kt == 0, False)
                        mm(o, w1h, xl, False, False)
                        ins = mm(o, w1l, xh, False, kt == 15)
                        if hh == 1 and kt == 7:
                            ins.then_inc(piece_used, 1)
                ins.then_inc(hid_sum, 1)
                owed[0] = 1

            nsa_gemm(0, N_CMPKV)
            nsa_gemm(1, N_CMPKV)
            pe.wait_ge(gw_ready, 1)
            for m in range(MT):
                for kt in range(KT):
                    cols = slice(m * P, (m + 1) * P)
                    ins = three(bank(3, 48 * m, 48), xt_hi[:, kt, cols], xt_lo[:, kt, cols],
                                gw_hi[:, kt, :], gw_lo[:, kt, :], kt == 0, kt == KT - 1)
            ins.then_inc(gate_sum, 1)
            turn_cmp(0, (2, 4))
            nsa_gemm(2, N_SEL)
            turn_cmp(1, (5, 6))
            nsa_gemm(3, N_SEL)
            turn_kv(0, 0, 7)
            pe.wait_ge(gate_exp, 1)
            compress(0, N_WK1)
            pe.wait_ge(pair_act, 1)
            turn_kv(1, 1, 2)
            nsa_gemm(4, N_WIN)
            nsa_gemm(5, N_WIN)
            pe.wait_ge(pair_dve, 1)
            turn_kv(2, 0, 4)
            pe.wait_ge(hid_ready, 1)
            compress(1, N_WV1)
            pe.wait_ge(pair_act, 2)
            turn_kv(3, 1, 5)
            pe.wait_ge(w2_loaded, 48)
            pe.wait_ge(hid_ready, 2)
            pe.wait_ge(pair_dve, 2)
            for kt in range(2):
                mm(bank(6, 0, 64), w2k[:, kt, :, :].rearrange("p a d -> p (a d)"), hid_k[:, 64 * kt:64 * kt + 64],
                   kt == 0, kt == 1)
            for hk in range(HK):
                for kt in range(2):
                    ins = mm(ps[0:64, 6, P + hk * DH:P + hk * DH + DH],
                             hid_v[:, HK * kt + hk, :, :].rearrange("p g c -> p (g c)"), w2v[:, kt, :],
                             kt == 0, kt == 1)
            ins.then_inc(kc_sum, 1)
            nsa_gemm(6, N_Q)
            nsa_gemm(7, N_Q)
            pe.wait_ge(turn_out[0], 2)
            turn_q(4, 0, 7, 2)
            nsa_gemm(8, N_Q + 2)
            pe.wait_ge(turn_out[0], 4)
            turn_q(5, 1, 4, 5)
            nsa_gemm(9, N_Q + 2)
            pe.wait_ge(turn_out[0], 5)
            turn_q(6, 0, 7, 2)
            pe.wait_ge(turn_out[0], 6)
            turn_q(7, 1, 4, 5)

            pe.wait_ge(turn_out[0], 8)
            pe.wait_ge(kc_out, 1)
            pe.wait_ge(vc_out, 1)
            for m in range(MT):
                for hd in range(H):
                    p0 = DH * (hd % 2)
                    ins = pe.matmul(bank(3 if hd % 2 else 6, 128 * m + 16 * (hd // 2), 16),
                                    view(qu_t, (hd // 2) * S + m * P, [[1, P]], p0=p0, n=DH),
                                    view(kc_t, 16 * (hd // G), [[1, 16]], p0=p0, n=DH),
                                    start=True, stop=True)
            ins.then_inc(sc_sum, 1)
            pe.wait_ge(proj_out[0], 10)
            pe.wait_ge(sc_ready, 1)
            U = 2 * H

            def unit(u):
                return u // 8, u // 4 % 2, u % 4

            def scores_nsa(u):
                hk, m, g = unit(u)
                hd = hk * G + g
                p0, n = DH * (hd % 2), P * (m + 1)
                for br in range(2):
                    ins = pe.matmul(bank(u % 3, br * n, n),
                                    view(q_t, (hd // 2) * S + m * P, [[1, P]], p0=p0, n=DH),
                                    view(k_t, (br * HK + hk) * S, [[1, n]], p0=p0, n=DH),
                                    start=True, stop=True)
                ins.then_inc(scores[0], 1)

            def turn_probs(i, w, u, blocks):
                pe.wait_ge(expd[i], w + 1)
                for k in range(blocks):
                    ins = pe.transpose(bank(3 + u % 2, P * k, P), probs[:, u % 3, P * k:P * k + P],
                                       ident[:, :])
                ins.then_inc(pt_psum[i], 1)

            def pv_nsa(u):
                hk, m, g = unit(u)
                grp = u // 4
                pe.wait_ge(pt_out[0], u + 1)
                if grp >= 2 and g == 0:
                    pe.wait_ge(o_ready[0], grp - 1)
                for br in range(2):
                    for kb in range(m + 1):
                        k = br * (m + 1) + kb
                        ins = pe.matmul(bank(5 + grp % 2, (2 * g + br) * DH, DH),
                                        p_t[:, u % 2, P * k:P * k + P],
                                        v_nsa[:, br, kb, hk * DH:(hk + 1) * DH],
                                        start=kb == 0, stop=kb == m)
                ins.then_inc(pv_done[0], 1)

            for s in range(U + 9):
                if s < U:
                    scores_nsa(s)
                if s in (3, 5):
                    r = (s - 3) // 2
                    if r == 0:
                        pe.wait_ge(pc_ready, 1)
                    else:
                        pe.wait_ge(pct_out, 1)
                    for k in range(4):
                        grp = 4 * r + k
                        hk, m = grp // 2, grp % 2
                        ins = pe.transpose(ps[0:64, 7, P * k:P * k + P],
                                           p_cmp[:, m, G * hk:G * hk + G, :].rearrange("p a c -> p (a c)"),
                                           ident[:, :])
                    ins.then_inc(pct_psum, 1)
                if 2 <= s < U + 2:
                    u = s - 2
                    turn_probs(0, u, u, 2 * (unit(u)[1] + 1))
                if 3 <= s < U + 3:
                    pv_nsa(s - 3)
                if s >= 7 and s % 4 == 3 and s < U + 7:
                    grp = (s - 7) // 4
                    if grp == 0:
                        pe.wait_ge(pct_out, 2)
                    else:
                        pe.wait_ge(o_ready[0], grp)
                    pe.matmul(bank(7, 0, 256), pc_t[:, grp, :], vc_bd[:, grp // 2, :],
                              start=True, stop=True).then_inc(ocmp_sum, 1)
                if s >= 11 and s % 4 == 3:
                    grp = (s - 11) // 4
                    hk, m = grp // 2, grp % 2
                    pe.wait_ge(o_ready[0], grp + 1)
                    if grp:
                        pe.wait_ge(ot_ready[0], grp)
                    for k in range(2):
                        ins = turn(7, 2 + k, tmp[:, m, hk * 256 + P * k:hk * 256 + P * k + P])
                    ins.then_inc(ot_psum[0], 1)

            def out_proj(b, n, ready):
                pcs = (Piece(n), Piece(n + 2))
                pe.wait_ge(*ready[0])
                gemm(0, 0, pcs[0], True, False)
                gemm(1, 0, pcs[1], True, False, done=acc_done[b])
                pe.wait_ge(*ready[1])
                gemm(2, 1, pcs[0], False, True)

                def turn_m0():
                    for half in range(2):
                        pe.wait_ge(h_ready[b], half + 1)
                        xt_turn(b, 0, half, h)

                gemm(3, 1, pcs[1], False, True, done=acc_done[b], mid=turn_m0)

            def ffn(layer, n0):
                b = 1 + 2 * layer

                def gu(j, m, pc, mid=None, need=None):
                    gemm(4 + m, m, pc, m == 0, m == 1, done=gu_done[layer], mid=mid, need=need)

                def ht_turn(j, m):
                    pe.wait_ge(hs_ready[layer], j * 2 + m + 1)
                    for k in range(2):
                        ins = turn(6 + m, k, hs[:, m, P * k:P * k + P])
                    ins.then_inc(ht_psum[layer], 1)

                def down(j, m, pc, first=False, last=False):
                    pe.wait_ge(ht_ready[layer], j * 2 + m + 1)
                    if m == 0:
                        pe.wait_ge(lo_ready, pc.halves(2))
                    for k in range(2):
                        for n in range(2):
                            c = k * D + 512 * n
                            cols = slice(k * S + m * P, k * S + (m + 1) * P)
                            ins = three(bank(2 * m + n), st_hi[:, cols], st_lo[:, cols],
                                        w_hi[:, pc.slot, c:c + 512], w_lo[:, pc.slot, c:c + 512],
                                        first and k == 0, last and k == 1)
                    if last:
                        ins.then_inc(acc_done[b + 1], 1)
                    elif m == 1:
                        ins.then_inc(piece_used, 1)

                def step(j, pc, first=False):
                    gu(j, 0, pc, mid=lambda: ht_turn(j - 1, 1))
                    down(j - 1, 0, pc + 2, first)
                    gu(j, 1, pc, mid=lambda: ht_turn(j, 0))
                    down(j - 1, 1, pc + 2, first)

                def need(m):
                    return lambda half: pe.wait_ge(xt_ready[b], 2 * m + half + 1)

                gu(0, 0, Piece(n0), need=need(0))
                for half in range(2):
                    pe.wait_ge(h_ready[b], 3 + half)
                    pe.wait_ge(xt_ready[b], 1 + half)
                    xt_turn(b, 1, half, h)
                gu(0, 1, Piece(n0), need=need(1), mid=lambda: ht_turn(0, 0))
                step(1, Piece(n0 + 2), first=True)
                with pe.Fori(0, (FJ - 3) // 2) as it:
                    for s in range(2):
                        step(it * 2 + (2 + s), Piece(n0 + 5 + 3 * s, it))
                step(FJ - 1, Piece(n0 + 3 * FJ - 4))
                ht_turn(FJ - 1, 1)
                down(FJ - 1, 0, Piece(n0 + FFN_PIECES - 1), last=True)
                down(FJ - 1, 1, Piece(n0 + FFN_PIECES - 1), last=True)
                owed[0] = 1

            out_proj(1, N_NSAO, ((ot_ready[0], 7), (ot_ready[0], 8)))
            ffn(0, N_FFN0)

            for m in range(MT):
                pe.wait_ge(xn_ready, m + 1)
                for half in range(2):
                    xt_turn(2, m, half, tmp)
            pe.wait_ge(xt_ready[2], 4)

            def dil_proj(hg, pat):
                def proj(c, m):
                    e = 2 * c + m
                    pe.wait_ge(proj_out[1], pat * 6 + (18 * hg + e + 1))
                    gemm(m, m, Piece(N_DIL + 18 * hg + 2 * c, pat), m == 0, m == 1, done=proj_done[1])

                def turns_of(c, m):
                    t = 2 * c + m
                    pe.wait_ge(roped[1], pat * 4 + (12 * hg + t + 1))
                    pe.wait_ge(turn_out[1], pat * 4 + (12 * hg + t + 1))
                    for k in range(4):
                        ins = turn(2 + m, k, stage_dil[:, m, P * k:P * k + P])
                    ins.then_inc(turned[1], 1)

                proj(0, 0)
                proj(0, 1)
                turns_of(0, 0)
                proj(1, 0)
                turns_of(0, 1)
                proj(1, 1)
                turns_of(1, 0)
                proj(2, 0)
                proj(2, 1)
                turns_of(1, 1)

            def qk(pat, t, j, c, n):
                return view(qk_t, ((pat * 2 + t) * 4 + j // 2) * S + c, [[1, n]], p0=DH * (j % 2), n=DH)

            def scores_dil(u):
                j, m = u // 2, u % 2
                for pat, c, k0, n in ((0, 0, 0, S), (1, 256, m * P, P), (2, 384, m * P, P)):
                    ins = pe.matmul(bank(u % 3, c, n), qk(pat, 0, j, m * P, P), qk(pat, 1, j, k0, n),
                                    start=True, stop=True)
                ins.then_inc(scores[1], 1)

            def pv_dil(hg, u):
                j, m = u // 2, u % 2
                pe.wait_ge(pt_out_dve if u % 2 else pt_out[1], 8 * hg + u // 2 + 1)
                if hg and u == 0:
                    pe.wait_ge(o_ready[1], 2)
                for k, (pat, mk) in enumerate(((0, 0), (0, 1), (1, m), (2, m))):
                    ins = pe.matmul(bank(5 + m, j * DH, DH), p_t[:, u % 2, P * k:P * k + P],
                                    v_dil[:, pat, mk, j * DH:(j + 1) * DH], start=k == 0, stop=k == 3)
                ins.then_inc(pv_done[1], 1)

            def ot_dil(hg, m):
                pe.wait_ge(o_ready[1], 2 * hg + m + 1)
                if (hg, m) in ((0, 1), (1, 0)):
                    pe.wait_ge(ot_ready[1], 2 * hg + m)
                b = 2 if (hg, m) == (1, 1) else 7
                for k in range(4):
                    ins = turn(b, k, tmp[:, m, 512 * hg + P * k:512 * hg + P * k + P])
                ins.then_inc(ot_psum[1], 1)

            for hg in range(2):
                with pe.Fori(0, 3) as pat:
                    dil_proj(hg, pat)
                pe.wait_ge(proj_out[1], 2 + 18 * (hg + 1))
                pe.wait_ge(turn_out[1], 2 + 12 * (hg + 1))
                for s in range(16 + 3):
                    if s < 16:
                        scores_dil(s)
                    if 2 <= s < 18:
                        turn_probs(1, 16 * hg + s - 2, s - 2, 4)
                    if s >= 3:
                        pv_dil(hg, s - 3)
                    if hg == 1 and s in (3, 6):
                        ot_dil(0, 0 if s == 3 else 1)
            for m in range(MT):
                ot_dil(1, m)
            out_proj(3, N_DILO, ((ot_ready[1], 4), (ot_ready[1], 4)))
            ffn(1, N_FFN1)


_IN = ["x", "positions", "norm_mix_pre", "norm_mix_post", "norm_ffn_pre", "norm_ffn_post", "ffn_w_gu",
       "ffn_w_down", "nsa_w_in", "nsa_cmp_pos", "nsa_cmp_wk1", "nsa_cmp_wk2", "nsa_cmp_wv1",
       "nsa_cmp_wv2", "nsa_w_o", "dil_w_in", "dil_w_o"]


def kernel(**inputs):
    import concourse.bacc as bacc
    from concourse.bass_utils import run_bass_kernel_spmd

    nc = bacc.Bacc("TRN2", target_bir_lowering=False, num_devices=1)
    arrays, args = {}, []
    for name in _IN:
        a = np.ascontiguousarray(inputs[name])
        arrays[f"in_{name}"] = a
        args.append(nc.dram_tensor(f"in_{name}", a.shape, mybir.dt.from_np(a.dtype),
                                   kind="ExternalInput").ap())
    out = nc.dram_tensor("out_h", (1, S, D), F32, kind="ExternalOutput").ap()
    build(nc, *args, out)
    result = run_bass_kernel_spmd(nc, [arrays], core_ids=[0])
    return result.results[0]["out_h"]
```

```python
from contextlib import ExitStack

import numpy as np

import concourse.bass as bass
from concourse import mybir

ALU = mybir.AluOpType
ACT = mybir.ActivationFunctionType
AX = mybir.AxisListType.X
F32 = mybir.dt.float32
F32R = mybir.dt.float32r
BF16 = mybir.dt.bfloat16
I32 = mybir.dt.int32

P = 128
D = 1024
S = 256
MT = S // P
KT = D // P
DH = 64
H = D // DH
HK = 4
G = H // HK
FF = 2816
FJ = FF // 256
EPS = 1e-6
NEG = -1e30
SCALE = DH ** -0.5
ROT = DH // 4
THETA = 500000.0
CMP, STRIDE = 32, 16
NC = (S - CMP) // STRIDE + 1
PIECE = 2048
RAW = 3
RING = 6
AHEAD = 3
TWO_PI = 6.283185307179586
MAGIC = 12582912.0
INF = 3.0e38

N_CMPKV, N_SEL, N_WIN, N_WK1, N_WV1, N_Q, N_NSAO = 0, 2, 4, 6, 8, 10, 14
N_FFN0 = 18
FFN_PIECES = 3 * FJ
N_DIL = N_FFN0 + FFN_PIECES
N_DILO = N_DIL + 36
N_FFN1 = N_DILO + 4
N_END = N_FFN1 + FFN_PIECES


class Piece:

    def __init__(self, n0, it=0):
        self.n0, self.it = n0, it

    def __add__(self, k):
        return Piece(self.n0 + k, self.it)

    @property
    def slot(self):
        return self.n0 % RING

    @property
    def raw(self):
        return self.n0 % RAW

    def loaded(self):
        return self.it * (32 * RING // RAW) + 32 * (self.n0 // RAW + 1)

    def halves(self, k):
        return self.it * (2 * RING) + 2 * self.n0 + k

    def used(self):
        return self.it * RING + self.n0 + 1


def view(t, off, dims, p0=0, n=P):
    width = int(np.prod(t.shape[1:]))
    return bass.AP(t, p0 * width + off, [[width, n]] + [list(d) for d in dims])


def build(nc, x, positions, norm_mix_pre, norm_mix_post, norm_ffn_pre, norm_ffn_post, ffn_w_gu,
          ffn_w_down, nsa_w_in, nsa_cmp_pos, nsa_cmp_wk1, nsa_cmp_wk2, nsa_cmp_wv1, nsa_cmp_wv2,
          nsa_w_o, dil_w_in, dil_w_o, out):
    ctx = ExitStack()
    with ctx:
        place = [(int(nc.sbuf_base) + 31) // 32 * 32]

        def sb(name, shape, dt=F32, at=None):
            size = int(np.prod(shape[1:])) * mybir.dt.size(dt)
            if at is None:
                at = place[0]
                place[0] = (at + size + 31) // 32 * 32
            assert at + size <= nc.sbuf_usable_end, name
            return nc.alloc_sbuf_tensor_at(name, shape, dt, offset=at)

        def zone(size):
            at = place[0]
            place[0] = at + size
            return at

        w_raw = sb("w_raw", [P, RAW, PIECE])
        w_hi = sb("w_hi", [P, RING, PIECE], F32R)
        w_lo = sb("w_lo", [P, RING, PIECE], F32R)
        h = sb("h", [P, MT, D])
        at_tmp = zone(MT * D * 4)
        tmp = sb("tmp", [P, MT, D], at=at_tmp)
        probs = sb("probs", [P, 4, 512], at=at_tmp)
        pair = sb("pair", [P, 2, HK, S], at=at_tmp)
        xt_hi = sb("xt_hi", [P, KT, S], F32R)
        xt_lo = sb("xt_lo", [P, KT, S], F32R)
        at_gp = zone(D * 4)
        g_post = sb("g_post", [P, D], at=at_gp)
        w2k = sb("w2k", [P, 2, 2, DH], at=at_gp)
        w2v = sb("w2v", [P, 2, DH], at=at_gp + 1024)
        hid_k = sb("hid_k", [P, 2, 64], at=at_gp + 1536)
        e_hid = sb("e_hid", [P, 256], at=at_gp + 2048)
        hid_r = sb("hid_r", [P, 256], at=at_gp + 3072)
        rows = sb("rows", [48, P], at=at_gp + 3072)

        at_a = zone(36864)
        q_t = sb("q_t", [P, H // 2, S], at=at_a)
        tb_hi = sb("tb_hi", [P, 16, 2, 64], F32R, at=at_a)
        tb_lo = sb("tb_lo", [P, 16, 2, 64], F32R, at=at_a + 8192)
        gw_hi = sb("gw_hi", [P, KT, 48], F32R, at=at_a + 24576)
        gw_lo = sb("gw_lo", [P, KT, 48], F32R, at=at_a + 26624)
        qu_t = sb("qu_t", [P, H // 2, S], at=at_a + 8192)
        k_t = sb("k_t", [P, 2, HK, S], at=at_a + 16384)
        v_nsa = sb("v_nsa", [P, 2, MT, HK * DH], at=at_a + 24576)
        vc_bd = sb("vc_bd", [64, HK, G * DH], at=at_a + 28672)
        tb_f = sb("tb_f", [P, 16, HK, 16], at=at_a + 28672)
        pc_t = sb("pc_t", [64, 2 * HK, P], at=at_a + 32768)
        stage_nsa = sb("stage_nsa", [P, MT, 512], at=at_a + 32768)
        qk_t = sb("qk_t", [P, 3, 2, 4, S], at=at_a)
        v_dil = sb("v_dil", [P, 3, MT, 512], at=at_a + 24576)
        silu = sb("silu", [P, MT, 256], at=at_a)
        hs = sb("hs", [P, MT, 256], at=at_a + 2048)

        at_s = zone(10240)
        p_t = sb("p_t", [P, 2, 2, 512], at=at_s)
        st_hi = sb("st_hi", [P, 512], F32R, at=at_s)
        st_lo = sb("st_lo", [P, 512], F32R, at=at_s + 2048)
        stage_rot = sb("stage_rot", [P, MT, 512], at=at_s)
        stage_dil = sb("stage_dil", [P, MT, 512], at=at_s)
        gw_raw = sb("gw_raw", [P, KT, 48], at=at_s + 8192)

        at_m = zone(2048)
        mask_dil = sb("mask_dil", [P, MT, 512], BF16, at=at_m)
        hid_v = sb("hid_v", [P, 2 * HK, G, 16], at=at_m)
        p_cmp = sb("p_cmp", [P, MT, H, 16], at=at_m)
        mask_nsa = sb("mask_nsa", [P, 2 * P], BF16)
        ident = sb("ident", [P, P])
        mask_c = sb("mask_c", [P, MT, 16])
        valid_c = sb("valid_c", [P, MT, 16])
        bd_mask = sb("bd_mask", [64, G])
        cos2 = sb("cos2", [P, 4, ROT])
        sin2 = sb("sin2", [P, 4, ROT])
        g_t = sb("g_t", [P, 48])
        inv_f = sb("inv_f", [P, ROT // 2])
        kc_t = sb("kc_t", [P, 64])
        gates = sb("gates", [P, MT, 48])
        rs = sb("rs", [P, MT])
        rs_post = sb("rs_post", [P, MT])
        ssq = sb("ssq", [P, 2 * MT])
        nt = sb("nt", [P, 4])
        rs_perm = sb("rs_perm", [P, MT])
        mx = sb("mx", [P, 4, 2])
        nm = sb("nm", [P, 4, 2])
        l_u = sb("l_u", [P, 4, 2])
        rl = sb("rl", [P, 4, 2])
        mx_c = sb("mx_c", [P, MT * H])
        l_c = sb("l_c", [P, MT * H])
        pos_i = sb("pos_i", [P, 4], I32, at=at_a + 16384)
        pos_f = sb("pos_f", [P, 4], at=at_a + 16448)
        ang = sb("ang", [P, 4, 8], at=at_a + 16512)
        turns = sb("turns", [P, 4, 8], at=at_a + 16640)
        half_pi = sb("half_pi", [P, 4, 8], at=at_a + 16768)
        rope_a = sb("rope_a", [P, 8, ROT], at=at_s + 8192)
        rope_b = sb("rope_b", [P, 8, ROT], at=at_s + 8704)

        ps = ctx.enter_context(nc.psum_tensor("ps", [P, 8, 512], F32))

        def bank(b, off=0, n=512):
            return ps[:, b, off:off + n]

        def xt_views(b, m, half, kt, dst, permuted):
            base = {0: 4 + 2 * m, 2: 6 - 2 * m}.get(b, 6)
            if not permuted:
                return bank(base + half, P * (kt % 4), P), dst[:, kt, m * P:(m + 1) * P]
            return (view(ps, (base + half) * 512 + P * (kt % 4), [[4, 32], [1, 4]]),
                    view(dst, kt * S + 32 * m, [[1, 32], [64, 4]]))

        def ot_bank(hg, jq):
            return 5 + jq if hg == 0 else 7 - 2 * jq

        def ot_views(hg, jq, dst):
            return (view(ps, ot_bank(hg, jq) * 512, [[S, 2], [64, 4], [1, 64]]),
                    view(dst, (4 * hg + 2 * jq) * S, [[S, 2], [1, 4], [4, 64]]))

        def sem(name):
            return ctx.enter_context(nc.semaphore(name))

        raw_loaded = [sem(f"raw_loaded{i}") for i in range(RAW)]
        hi_ready, lo_ready, piece_used = sem("hi_ready"), sem("lo_ready"), sem("piece_used")
        x_loaded = [sem(f"x_loaded{m}") for m in range(MT)]
        rows_loaded, pos_loaded, w2_loaded = sem("rows_loaded"), sem("pos_loaded"), sem("w2_loaded")
        gw_loaded, out_stored = sem("gw_loaded"), sem("out_stored")
        gp_loaded = [sem(f"gp_loaded{i}") for i in range(4)]
        ident_ready, masks_ready = sem("ident_ready"), sem("masks_ready")
        dilmask_ready, rope_ready = sem("dilmask_ready"), sem("rope_ready")
        angles_ready = sem("angles_ready")
        pool_step, dve_step = sem("pool_step"), sem("dve_step")
        rows_t, gt_ready = sem("rows_t"), sem("gt_ready")
        gw_hi_ready, gw_ready = sem("gw_hi_ready"), sem("gw_ready")
        acc_done = [sem(f"acc_done{b}") for b in range(5)]
        sq_post = [sem(f"sq_post{b}") for b in range(5)]
        h_ready = [sem(f"h_ready{b}") for b in range(5)]
        sq_h = [sem(f"sq_h{b}") for b in range(4)]
        rs_ready = [sem(f"rs_ready{b}") for b in range(4)]
        rs_turned, rs_perm_ready = sem("rs_turned"), sem("rs_perm_ready")
        xt_psum = [sem(f"xt_psum{b}") for b in range(4)]
        xt_hi_ready = [sem(f"xt_hi_ready{b}") for b in range(4)]
        xt_ready = [sem(f"xt_ready{b}") for b in range(4)]
        proj_done = [sem(f"proj_done{i}") for i in range(2)]
        proj_out = [sem(f"proj_out{i}") for i in range(2)]
        roped = [sem(f"roped{i}") for i in range(2)]
        turned = [sem(f"turned{i}") for i in range(2)]
        turn_out = [sem(f"turn_out{i}") for i in range(2)]
        rope_parts = sem("rope_parts")
        pair_act, pair_dve = sem("pair_act"), sem("pair_dve")
        tb_f_ready, tb_hi_ready, tb_ready = sem("tb_f_ready"), sem("tb_hi_ready"), sem("tb_ready")
        gate_sum, gate_exp = sem("gate_sum"), sem("gate_exp")
        hid_sum, hid_exp, hid_ready = sem("hid_sum"), sem("hid_exp"), sem("hid_ready")
        kc_sum, kc_out, vc_out = sem("kc_sum"), sem("kc_out"), sem("vc_out")
        hid_psum, hid_out = sem("hid_psum"), sem("hid_out")
        sc_sum, sc_ready, pc_exp, pc_ready = sem("sc_sum"), sem("sc_ready"), sem("pc_exp"), sem("pc_ready")
        pct_psum, pct_out = sem("pct_psum"), sem("pct_out")
        scores = [sem(f"scores{i}") for i in range(2)]
        masked = [sem(f"masked{i}") for i in range(2)]
        expd = [sem(f"expd{i}") for i in range(2)]
        normed = [sem(f"normed{i}") for i in range(2)]
        pt_psum = [sem(f"pt_psum{i}") for i in range(2)]
        pt_out = [sem(f"pt_out{i}") for i in range(2)]
        pv_done = [sem(f"pv_done{i}") for i in range(2)]
        ot_hi = [sem(f"ot_hi{i}") for i in range(2)]
        ot_ready = [sem(f"ot_ready{i}") for i in range(2)]
        gu_done = [sem(f"gu_done{l}") for l in range(2)]
        silu_done = [sem(f"silu_done{l}") for l in range(2)]
        hs_ready = [sem(f"hs_ready{l}") for l in range(2)]
        ht_psum = [sem(f"ht_psum{l}") for l in range(2)]
        ht_hi = [sem(f"ht_hi{l}") for l in range(2)]
        ht_ready = [sem(f"ht_ready{l}") for l in range(2)]

        block = ctx.enter_context(nc.Block())

        @block.sync
        def _(sp):
            def load(pc, *parts):
                if pc.n0 >= RAW:
                    sp.wait_ge(lo_ready, pc.halves(2) - 2 * RAW)
                for src, c, dims in parts:
                    sp.dma_start(view(w_raw, pc.raw * PIECE + c, dims), src)\
                      .then_inc(raw_loaded[pc.raw], 16)

            def chunk(n, w, c0):
                wv = w.rearrange("(k p) c -> p k c", p=P)
                for half in range(2):
                    load(n + half, *[(wv[:, 4 * half + k:4 * half + k + 2, bass.ds(c0, 512)], 512 * k,
                                      [[512, 2], [1, 512]]) for k in (0, 2)])

            for m in range(MT):
                sp.dma_start(h[:, m, :], x[0, m * P:(m + 1) * P, :]).then_inc(x_loaded[m], 16)
            w_in = nsa_w_in[0]
            chunk(Piece(N_CMPKV), w_in, 1024)
            chunk(Piece(N_SEL), w_in, 1536)

            def cmp_w1(n, w):
                wv = w[0].rearrange("(k p) c -> p k c", p=P)
                for half in range(2):
                    load(n + half, *[(wv[:, 8 * half + k:8 * half + k + 4, :], 256 * k,
                                      [[256, 4], [1, 256]]) for k in (0, 4)])

            chunk(Piece(N_WIN), w_in, 2048)
            cmp_w1(Piece(N_WK1), nsa_cmp_wk1)
            cmp_w1(Piece(N_WV1), nsa_cmp_wv1)
            chunk(Piece(N_Q), w_in, 0)
            chunk(Piece(N_Q + 2), w_in, 512)

            def out_proj(n, w):
                chunk(Piece(n), w[0], 0)
                chunk(Piece(n + 2), w[0], 512)

            def ffn_loads(n0, layer):
                gu = ffn_w_gu[layer].rearrange("(k p) (s c) -> p k s c", p=P, s=2)
                dn = ffn_w_down[layer].rearrange("(k p) c -> p k c", p=P)

                def gu_load(pc, j):
                    for half in range(2):
                        load(pc + half, *[(gu[:, 4 * half:4 * half + 4, s, bass.ds(j * 256, 256)], 256 * s,
                                           [[512, 4], [1, 256]]) for s in range(2)])

                def dn_load(pc, j):
                    load(pc, *[(dn[:, bass.ds(j * 2 + k, 1), :], D * k, [[D, 1], [1, D]]) for k in range(2)])

                def step(pc, j):
                    gu_load(pc, j)
                    dn_load(pc + 2, j - 1)

                gu_load(Piece(n0), 0)
                step(Piece(n0 + 2), 1)
                with sp.Fori(0, (FJ - 3) // 2) as it:
                    for s in range(2):
                        step(Piece(n0 + 5 + 3 * s, it), it * 2 + (2 + s))
                step(Piece(n0 + 3 * FJ - 4), FJ - 1)
                dn_load(Piece(n0 + FFN_PIECES - 1), FJ - 1)

            out_proj(N_NSAO, nsa_w_o)
            ffn_loads(N_FFN0, 0)
            for hg in range(2):
                with sp.Fori(0, 3) as pat:
                    for t in range(3):
                        chunk(Piece(N_DIL + 18 * hg + 2 * t, pat), dil_w_in[0],
                              pat * (3 * D) + (t * D + hg * 512))
            out_proj(N_DILO, dil_w_o)
            ffn_loads(N_FFN1, 1)
            for q in range(2 * MT):
                m, half = q // 2, q % 2
                sp.wait_ge(h_ready[4], q + 1)
                sp.dma_start(out[0, m * P:(m + 1) * P, half * 512:(half + 1) * 512],
                             h[:, m, half * 512:(half + 1) * 512]).then_inc(out_stored, 16)
            sp.wait_ge(out_stored, 16 * 2 * MT)

        @block.gpsimd
        def _(pool):
            done = [0]

            def link(ins):
                done[0] += 1
                ins.then_inc(pool_step, 1)
                pool.wait_ge(pool_step, done[0])

            link(pool.memset(ident[:, :], 0.0))
            pool.affine_select(out=ident[:, :], in_=ident[:, :], compare_op=ALU.not_equal, fill=1.0,
                               base=0, pattern=[[-1, P]], channel_multiplier=1).then_inc(ident_ready, 1)
            for i in range(ROT // 2):
                f = float(np.float32(THETA) ** np.float32(-2.0 * i / ROT))
                ins = pool.memset(inv_f[:, i:i + 1], f)
            ins.then_inc(rope_ready, 1)
            link(pool.memset(mask_nsa[:, :], 0.0))
            pool.affine_select(out=mask_nsa[:, P:2 * P], in_=mask_nsa[:, P:2 * P], compare_op=ALU.is_ge,
                               fill=NEG, base=0, pattern=[[-1, P]], channel_multiplier=1)\
                .then_inc(masks_ready, 1)
            for t, good, bad in ((mask_c, 0.0, NEG), (valid_c, 1.0, 0.0)):
                link(pool.memset(t[:, :, :], good))
                pool.affine_select(out=t[:, :, :], in_=t[:, :, :], compare_op=ALU.is_ge, fill=bad,
                                   base=-(CMP - 1), pattern=[[P, MT], [-STRIDE, 16]],
                                   channel_multiplier=1).then_inc(masks_ready, 1)
            link(pool.memset(bd_mask[:, :], 1.0))
            link(pool.affine_select(out=bd_mask[:, :], in_=bd_mask[:, :], compare_op=ALU.is_ge, fill=0.0,
                                    base=0, pattern=[[-16, G]], channel_multiplier=1))
            pool.affine_select(out=bd_mask[:, :], in_=bd_mask[:, :], compare_op=ALU.is_ge, fill=0.0,
                               base=15, pattern=[[16, G]], channel_multiplier=-1).then_inc(masks_ready, 1)

            def post_gain(b, w, layer):
                pool.dma_start(g_post[:, :], bass.AP(w.tensor, layer * D, [[0, P], [1, D]]))\
                    .then_inc(gp_loaded[b - 1], 16)

            pool.wait_ge(kc_sum, 1)
            post_gain(1, norm_mix_post, 0)

            pool.wait_ge(pct_psum, 2)
            link(pool.memset(mask_dil[:, :, 0:256], 0.0))
            link(pool.memset(mask_dil[:, :, 256:512], NEG))
            for hp in range(2):
                rows64 = slice(64 * hp, 64 * hp + 64)
                for m in range(MT):
                    p0 = mask_dil[rows64, m, 0:256].rearrange("p (r q) -> p r q", r=4)
                    link(pool.affine_select(out=p0, in_=p0, compare_op=ALU.is_ge, fill=NEG,
                                            base=2 * m + hp, pattern=[[-1, 4], [-4, 64]],
                                            channel_multiplier=4))
                    link(pool.affine_select(out=p0, in_=p0, compare_op=ALU.is_ge, fill=NEG,
                                            base=128 - 2 * m - hp, pattern=[[1, 4], [4, 64]],
                                            channel_multiplier=-4))
                    p1 = mask_dil[rows64, m, 256 + 64 * hp:320 + 64 * hp]
                    link(pool.memset(p1, 0.0))
                    link(pool.affine_select(out=p1, in_=p1, compare_op=ALU.is_ge, fill=NEG,
                                            base=0, pattern=[[-1, 64]], channel_multiplier=1))
                    p2 = mask_dil[rows64, m, 384 + 64 * hp:448 + 64 * hp]
                    for d in range(16):
                        link(pool.affine_select(out=p2, in_=p2, compare_op=ALU.not_equal, fill=0.0,
                                                base=-4 * d, pattern=[[-1, 64]], channel_multiplier=1))
            pool.sem_inc(dilmask_ready, 1)
            for b, w, layer in ((2, norm_ffn_post, 0), (3, norm_mix_post, 1), (4, norm_ffn_post, 1)):
                pool.wait_ge(h_ready[b - 1], 4)
                post_gain(b, w, layer)

        @block.scalar
        def _(act):
            def split(n, halves=(0, 1)):
                if isinstance(n, int):
                    n = Piece(n)
                if n.n0 >= N_END:
                    return
                for k in halves:
                    if k == 0:
                        act.wait_ge(raw_loaded[n.raw], n.loaded())
                        if n.n0 >= RING or not isinstance(n.it, int):
                            act.wait_ge(piece_used, n.used() - RING)
                    c = 1024 * k
                    act.activation(w_hi[:, n.slot, c:c + 1024], w_raw[:, n.raw, c:c + 1024], ACT.Copy)\
                       .then_inc(hi_ready, 1)

            def xt_out(b, m, half, gain, permuted=False):
                act.wait_ge(xt_psum[b], 2 * m + half + 1)
                for k in range(4):
                    kt = 4 * half + k
                    src, dst = xt_views(b, m, half, kt, xt_hi, permuted)
                    ins = act.activation(dst, src, ACT.Copy, scale=g_t[:, 8 * gain + kt:8 * gain + kt + 1])
                ins.then_inc(xt_hi_ready[b], 1)

            def h_squares(b, m):
                act.activation(tmp[:, m, :], h[:, m, :], ACT.Square, accum_out=ssq[:, m:m + 1])\
                   .then_inc(sq_h[b], 1)

            act.dma_start(rows[0:16, :], norm_mix_pre.rearrange("l (k p) -> (l k) p", p=P))\
               .then_inc(rows_loaded, 16)
            act.dma_start(rows[16:32, :], norm_ffn_pre.rearrange("l (k p) -> (l k) p", p=P))\
               .then_inc(rows_loaded, 16)
            act.dma_start(rows[32:48, :], nsa_cmp_pos[0].rearrange("(k a) d -> k (a d)", a=2))\
               .then_inc(rows_loaded, 16)
            act.dma_start(gw_raw[:, :, :], nsa_w_in[0].rearrange("(k p) c -> p k c", p=P)[:, :, 2560:2608])\
               .then_inc(gw_loaded, 16)
            act.dma_start(pos_i[:, 0:2], bass.AP(positions.tensor, 0, [[1, P], [P, 2]]),
                          allow_slow_non_contiguous=True)\
               .then_inc(pos_loaded, 16)
            for hp in range(2):
                act.dma_start(pos_i[64 * hp:64 * hp + 64, 2:4],
                              bass.AP(positions.tensor, hp, [[4, 64], [2, 2]]),
                              allow_slow_non_contiguous=True).then_inc(pos_loaded, 16)
            for dst, w in ((w2k[:, :, 0, :], nsa_cmp_wk2), (w2k[:, :, 1, :], nsa_cmp_wk2), (w2v[:, :, :], nsa_cmp_wv2)):
                act.dma_start(dst, w[0].rearrange("(k p) d -> p k d", p=P)).then_inc(w2_loaded, 16)
            act.wait_ge(gt_ready, 1)
            for m in range(MT):
                for half in range(2):
                    xt_out(0, m, half, 0)
                split(m)
            for m in range(MT):
                act.wait_ge(x_loaded[m], 16)
                h_squares(0, m)
            split(2)
            act.wait_ge(gw_loaded, 16)
            act.activation(gw_hi[:, :, :], gw_raw[:, :, :], ACT.Copy).then_inc(gw_hi_ready, 1)

            ev = [0]

            def proj_evac(dsts):
                e = ev[0]
                m = e % 2
                if e < 2:
                    act.wait_ge(rs_ready[0], m + 1)
                act.wait_ge(proj_done[0], e + 1)
                for dst, src in dsts(m):
                    ins = act.activation(dst, src, ACT.Copy, scale=rs[:, m:m + 1])
                ins.then_inc(proj_out[0], 1)
                ev[0] += 1

            def twice(stage, m, c):
                return (view(stage, m * 512, [[P, HK], [DH, 2], [1, DH]]),
                        view(ps, m * 512 + c, [[DH, HK], [0, 2], [1, DH]]))

            tv = [0]

            def turn_evac(parts):
                act.wait_ge(turned[0], tv[0] + 1)
                for dst, src in parts:
                    ins = act.activation(dst, src, ACT.Copy)
                ins.then_inc(turn_out[0], 1)
                tv[0] += 1

            def quads(b):
                return bank(b).rearrange("p (a t) -> p a t", a=4)

            proj_evac(lambda m: [twice(stage_nsa, m, 0), twice(stage_rot, m, 256)])
            split(3)
            proj_evac(lambda m: [twice(stage_nsa, m, 0), twice(stage_rot, m, 256)])
            split(4)
            act.wait_ge(gate_sum, 1)
            for m in range(MT):
                ins = act.activation(gates[:, m, :], bank(3, 48 * m, 48), ACT.Copy, scale=rs[:, m:m + 1])
            ins.then_inc(gate_exp, 1)
            act.wait_ge(angles_ready, 1)
            act.activation(sin2[:, :, 8:16], ang[:, :, :], ACT.Sin)
            act.activation(cos2[:, :, 0:8], half_pi[:, :, :], ACT.Sin).then_inc(rope_ready, 1)
            act.wait_ge(gate_exp, 1)
            act.activation(gates[:, :, :], gates[:, :, :], ACT.Exp, scale=-1.0).then_inc(gate_exp, 1)

            def pair_k(m, b):
                act.wait_ge(turned[0], m + 1)
                act.activation(view(pair, m * P, [[S, 4], [1, P]], n=64),
                               view(ps, b * 512, [[P, 4], [1, P]], n=64), ACT.Copy)
                lo = 1 if m == 0 else 0
                act.activation(view(pair, m * P - 1 + lo, [[S, 4], [1, P - lo]], p0=64, n=64),
                               view(ps, b * 512 + lo, [[P, 4], [1, P - lo]], p0=64, n=64), ACT.Copy)\
                   .then_inc(pair_act, 1)

            def block_hi(kv):
                act.wait_ge(tb_f_ready, kv + 1)
                act.activation(tb_hi[:, :, kv, :], tb_f[:, :, :, :].rearrange("p a b c -> p a (b c)"), ACT.Copy)\
                   .then_inc(tb_hi_ready, 1)

            pair_k(0, 2)
            split(5)
            kv_sel = lambda m: [twice(stage_nsa, m, 0), (v_nsa[:, 0, m, :], bank(m, 256, 256))]
            kv_win = lambda m: [twice(stage_nsa, m, 0), (v_nsa[:, 1, m, :], bank(m, 256, 256))]
            proj_evac(kv_sel)
            pair_k(1, 5)
            tv[0] = 2
            split(6)
            proj_evac(kv_sel)
            block_hi(0)
            turn_evac([(k_t[:, 0, :, 0:P], quads(7))])
            split(7)
            proj_evac(kv_win)
            turn_evac([(k_t[:, 0, :, P:S], quads(2))])
            block_hi(1)
            split(8)
            proj_evac(kv_win)
            split(9)
            turn_evac([(k_t[:, 1, :, 0:P], quads(4))])
            split(10)
            split(11)
            for kv, b in enumerate((3, 6)):
                act.wait_ge(hid_sum, kv + 1)
                r = slice(64 * kv, 64 * kv + 64)
                act.activation(e_hid[r, :], ps[r, b, 0:256], ACT.Exp, scale=-1.0).then_inc(hid_exp, 1)
            turn_evac([(k_t[:, 1, :, P:S], quads(5))])
            split(12)
            q_rows = lambda m: [(stage_nsa[:, m, :], bank(m)), (stage_rot[:, m, :], bank(m))]

            def turn_q(c, m, b_plain, b_rot):
                turn_evac([(qu_t[:, 4 * c:4 * c + 4, m * P:m * P + P], quads(b_plain)),
                           (q_t[:, 4 * c:4 * c + 4, m * P:m * P + P], quads(b_rot))])

            proj_evac(q_rows)
            split(13)
            proj_evac(q_rows)
            split(14, (0,))
            turn_q(0, 0, 7, 2)
            act.wait_ge(kc_sum, 1)
            act.activation(kc_t[:, :], bank(6, 0, 64), ACT.Copy).then_inc(kc_out, 1)
            split(14, (1,))
            proj_evac(q_rows)
            split(15, (0,))
            turn_q(0, 1, 4, 5)
            split(15, (1,))
            proj_evac(q_rows)
            split(16, (0,))
            turn_q(1, 0, 7, 2)
            turn_q(1, 1, 4, 5)
            split(16, (1,))

            def exp_unit(i, w, n, parts):
                act.wait_ge(masked[i], w + 1)
                if w >= 4:
                    act.wait_ge(normed[i], w - 3)
                for br in range(parts):
                    p = probs[:, w % 4, br * n:(br + 1) * n]
                    ins = act.activation(p, p, ACT.Exp, bias=nm[:, w % 4, br:br + 1], scale=SCALE,
                                         accum_out=l_u[:, w % 4, br:br + 1])
                ins.then_inc(expd[i], 1)

            def ot_evac(grp):
                act.wait_ge(pv_done[0], grp + 1)
                hk, m = grp // 2, grp % 2
                act.activation(xt_hi[:, 2 * hk:2 * hk + 2, m * P:(m + 1) * P],
                               bank(5 + grp % 2, 0, 256).rearrange("p (a t) -> p a t", a=2), ACT.Copy)\
                   .then_inc(ot_hi[0], 1)

            act.wait_ge(sc_ready, 1)
            act.activation(p_cmp[:, :, :, :], p_cmp[:, :, :, :], ACT.Exp, scale=SCALE).then_inc(pc_exp, 1)
            U = 2 * H
            for s in range(U + 6):
                if s < U:
                    exp_unit(0, s, P * (s // 4 % 2 + 1), 2)
                if s in (4, 6):
                    r = (s - 4) // 2
                    act.wait_ge(pct_psum, r + 1)
                    act.activation(pc_t[:, 4 * r:4 * r + 4, :],
                                   view(ps, 7 * 512, [[P, 4], [1, P]], n=64), ACT.Copy).then_inc(pct_out, 1)
                if 3 <= s < U + 3:
                    u = s - 3
                    nb = 2 * (u // 4 % 2 + 1)
                    act.wait_ge(pt_psum[0], u + 1)
                    act.activation(view(p_t, (u // 2 % 2) * 1024 + (u % 2) * P, [[2 * P, nb], [1, P]]),
                                   bank(3 + u % 2, 0, nb * P).rearrange("p (a t) -> p a t", a=nb), ACT.Copy)\
                       .then_inc(pt_out[0], 1)
                if s >= 9 and s % 4 == 1:
                    ot_evac((s - 9) // 4)
            def post_squares(b, m):
                act.wait_ge(acc_done[b], m + 1)
                act.activation(tmp[:, m, :], ps[:, 2 * m:2 * m + 2, :].rearrange("p a c -> p (a c)"),
                               ACT.Square, accum_out=ssq[:, MT + m:MT + m + 1]).then_inc(sq_post[b], 1)

            def to_ffn(b, n, gain):
                split(n + 3)
                split(n + 4)
                split(n + 5)
                post_squares(b, 0)
                xt_out(b, 0, 0, gain)
                xt_out(b, 0, 1, gain)
                act.wait_ge(h_ready[b], 2)
                h_squares(b, 0)
                split(n + 6)
                post_squares(b, 1)
                xt_out(b, 1, 0, gain)
                xt_out(b, 1, 1, gain)
                act.wait_ge(h_ready[b], 4)
                h_squares(b, 1)

            def ffn(layer, n0):
                b = 1 + 2 * layer

                def silu_step(j, m):
                    act.wait_ge(gu_done[layer], j * 2 + m + 1)
                    act.activation(silu[:, m, :], bank(4 + m, 0, 256), ACT.Silu, scale=rs[:, m:m + 1])\
                       .then_inc(silu_done[layer], 1)

                def ht_out(j, m):
                    act.wait_ge(ht_psum[layer], j * 2 + m + 1)
                    act.activation(view(st_hi, m * P, [[S, 2], [1, P]]),
                                   bank(6 + m, 0, 256).rearrange("p (a t) -> p a t", a=2), ACT.Copy)\
                       .then_inc(ht_hi[layer], 1)

                def step(j, nx):
                    split(nx)
                    ht_out(j - 1, 1)
                    split(nx + 1, (0,))
                    silu_step(j, 0)
                    split(nx + 1, (1,))
                    split(nx + 2, (0,))
                    ht_out(j, 0)
                    split(nx + 2, (1,))
                    silu_step(j, 1)

                act.wait_ge(rs_ready[b], 1)
                split(Piece(n0 + 3), (0,))
                silu_step(0, 0)
                split(Piece(n0 + 3), (1,))
                split(Piece(n0 + 4), (0,))
                ht_out(0, 0)
                split(Piece(n0 + 4), (1,))
                act.wait_ge(rs_ready[b], 2)
                silu_step(0, 1)
                step(1, Piece(n0 + 5))
                with act.Fori(0, (FJ - 3) // 2) as it:
                    for s in range(2):
                        step(it * 2 + (2 + s), Piece(n0 + 8 + 3 * s, it))
                step(FJ - 1, Piece(n0 + 3 * FJ - 1))
                ht_out(FJ - 1, 1)
                split(n0 + FFN_PIECES + 2)

            to_ffn(1, N_NSAO, 2)
            ffn(0, N_FFN0)
            for m in range(MT):
                post_squares(2, m)
                for half in range(2):
                    xt_out(2, m, half, 1, permuted=True)
            for m in range(MT):
                h_squares(2, m)
            act.wait_ge(rs_perm_ready, 1)

            act.sem_inc(proj_out[1], 2)
            act.sem_inc(turn_out[1], 2)

            def dil_proj(hg, pat):
                e0 = 18 * hg
                t0 = 12 * hg

                def evac(c, m):
                    act.wait_ge(proj_done[1], pat * 6 + (e0 + 2 * c + m + 1))
                    dst = stage_dil[:, m, :] if c < 2 else view(v_dil, pat * (MT * 512) + m * 512, [[1, 512]])
                    act.activation(dst, bank(m), ACT.Copy, scale=rs_perm[:, m:m + 1]).then_inc(proj_out[1], 1)

                def turn(c, m):
                    act.wait_ge(turned[1], pat * 4 + (t0 + 2 * c + m + 1))
                    act.activation(view(qk_t, pat * (2 * 4 * S) + (c * 4 * S + m * P), [[S, 4], [1, P]]),
                                   bank(2 + m).rearrange("p (a t) -> p a t", a=4), ACT.Copy)\
                       .then_inc(turn_out[1], 1)

                n = Piece(N_DIL + 18 * hg + AHEAD, pat)
                split(n)
                evac(0, 0)
                split(n + 1)
                evac(0, 1)
                split(n + 2, (0,))
                turn(0, 0)
                split(n + 2, (1,))
                evac(1, 0)
                turn(0, 1)
                split(n + 3)
                evac(1, 1)
                split(n + 4, (0,))
                turn(1, 0)
                split(n + 4, (1,))
                evac(2, 0)
                split(n + 5)
                evac(2, 1)
                turn(1, 1)

            def ot_dil(hg, jq):
                act.wait_ge(pv_done[1], 2 * hg + jq + 1)
                src, dst = ot_views(hg, jq, xt_hi)
                act.activation(dst, src, ACT.Copy).then_inc(ot_hi[1], 1)

            for hg in range(2):
                with act.Fori(0, 3) as pat:
                    dil_proj(hg, pat)
                for s in range(16 + 4):
                    if s < 16:
                        exp_unit(1, 16 * hg + s, 512, 1)
                    if 3 <= s < 19:
                        w = 16 * hg + s - 3
                        act.wait_ge(pt_psum[1], w + 1)
                        act.activation(p_t[:, 0, w % 2, :], bank(3 + w % 2), ACT.Copy).then_inc(pt_out[1], 1)
                    if hg == 1 and s in (1, 5, 13):
                        ot_dil(*{1: (0, 0), 5: (0, 1), 13: (1, 0)}[s])
            ot_dil(1, 1)
            to_ffn(3, N_DILO, 3)
            ffn(1, N_FFN1)
            for m in range(MT):
                post_squares(4, m)

        @block.vector
        def _(dve):
            done = [0]

            def link(ins):
                done[0] += 1
                ins.then_inc(dve_step, 1)
                dve.wait_ge(dve_step, done[0])

            def split(n, halves=(0, 1)):
                if isinstance(n, int):
                    n = Piece(n)
                if n.n0 >= N_END:
                    return
                for k in halves:
                    dve.wait_ge(hi_ready, n.halves(k + 1))
                    c = 1024 * k
                    dve.tensor_tensor(w_lo[:, n.slot, c:c + 1024], w_raw[:, n.raw, c:c + 1024],
                                      w_hi[:, n.slot, c:c + 1024].bitcast(F32), ALU.subtract)\
                       .then_inc(lo_ready, 1)

            def rsqrt(total, dst):
                v, hv, y, t = (nt[:, i:i + 1] for i in range(4))
                link(dve.tensor_scalar(v, total, 1.0 / D, EPS, ALU.mult, ALU.add))
                link(dve.tensor_scalar(y.bitcast(I32), v.bitcast(I32), 1, None, ALU.logical_shift_right))
                link(dve.tensor_scalar(y.bitcast(I32), y.bitcast(I32), -1.0, float(0x5F3759DF),
                                       ALU.mult, ALU.add))
                link(dve.tensor_scalar(hv, v, -0.5, None, ALU.mult))
                for i in range(3):
                    link(dve.scalar_tensor_tensor(t, y, hv, y, ALU.mult, ALU.mult))
                    last = dve.scalar_tensor_tensor(y if i < 2 else dst, t, 1.5, y, ALU.add, ALU.mult)
                    if i < 2:
                        link(last)
                return last

            def h_rs(b, m):
                dve.wait_ge(sq_h[b], m + 1)
                rsqrt(ssq[:, m:m + 1], rs[:, m:m + 1]).then_inc(rs_ready[b], 1)
                dve.wait_ge(rs_ready[b], m + 1)

            def xt_lo_out(b, m, half, gain, permuted=False):
                dve.wait_ge(xt_hi_ready[b], 2 * m + half + 1)
                for k in range(4):
                    kt = 4 * half + k
                    src, dst = xt_views(b, m, half, kt, xt_lo, permuted)
                    _, hi = xt_views(b, m, half, kt, xt_hi, permuted)
                    ins = dve.scalar_tensor_tensor(dst, src, g_t[:, 8 * gain + kt:8 * gain + kt + 1],
                                                   hi.bitcast(F32), ALU.mult, ALU.subtract)
                ins.then_inc(xt_ready[b], 1)

            dve.wait_ge(rows_t, 1)
            dve.tensor_copy(g_t[:, :], bank(2, 0, 48)).then_inc(gt_ready, 1)
            for m in range(MT):
                for half in range(2):
                    xt_lo_out(0, m, half, 0)
                split(m)
            for m in range(MT):
                h_rs(0, m)
            split(2)
            dve.wait_ge(gw_hi_ready, 1)
            dve.tensor_tensor(gw_lo[:, :, :], gw_raw[:, :, :], gw_hi[:, :, :].bitcast(F32), ALU.subtract)\
               .then_inc(gw_ready, 1)
            dve.wait_ge(pos_loaded, 48)
            dve.wait_ge(rope_ready, 1)
            link(dve.tensor_copy(pos_f[:, :], pos_i[:, :]))
            link(dve.tensor_tensor(ang[:, :, :], view(pos_f, 0, [[1, 4], [0, 8]]),
                                   view(inv_f, 0, [[0, 4], [1, 8]]), ALU.mult))
            link(dve.tensor_scalar(turns[:, :, :], ang[:, :, :], 1.0 / TWO_PI, MAGIC, ALU.mult, ALU.add))
            link(dve.tensor_scalar(turns[:, :, :], turns[:, :, :], MAGIC, None, ALU.subtract))
            c1 = 6.28125
            c2 = float(np.floor((TWO_PI - c1) * 2.0 ** 21) / 2.0 ** 21)
            for c in (c1, c2, TWO_PI - c1 - c2):
                link(dve.scalar_tensor_tensor(ang[:, :, :], turns[:, :, :], -c, ang[:, :, :],
                                              ALU.mult, ALU.add))
            link(dve.tensor_scalar(ang[:, :, :], ang[:, :, :], 3.1415925, -3.1415925, ALU.min, ALU.max))
            link(dve.scalar_tensor_tensor(half_pi[:, :, :], ang[:, :, :], -1.0, ang[:, :, :],
                                          ALU.mult, ALU.min))
            dve.tensor_scalar(half_pi[:, :, :], half_pi[:, :, :], TWO_PI / 4, None, ALU.add)\
               .then_inc(angles_ready, 1)

            def rope(i, e, stage, m, heads, table):
                a, b = rope_a[:, 0:heads, :], rope_b[:, 0:heads, :]
                x16 = view(stage, m * 512, [[DH, heads], [1, ROT]])
                x1 = view(stage, m * 512, [[DH, heads], [1, 8]])
                x2 = view(stage, m * 512 + 8, [[DH, heads], [1, 8]])
                dve.wait_ge(proj_out[i], e)
                dve.tensor_tensor(a, x16, view(cos2, table * ROT, [[0, heads], [1, ROT]]), ALU.mult)
                dve.tensor_tensor(rope_b[:, 0:heads, 0:8], x2, view(sin2, table * ROT, [[0, heads], [1, 8]]),
                                  ALU.mult)
                link(dve.tensor_tensor(rope_b[:, 0:heads, 8:16], x1,
                                       view(sin2, table * ROT + 8, [[0, heads], [1, 8]]), ALU.mult))
                dve.tensor_tensor(x16, a, b, ALU.add).then_inc(roped[i], 1)
                dve.wait_ge(roped[i], e - 2)

            split(3)
            split(4)
            dve.wait_ge(rope_ready, 2)
            dve.tensor_scalar(sin2[:, :, 0:8], sin2[:, :, 8:16], -1.0, None, ALU.mult)
            link(dve.tensor_copy(cos2[:, :, 8:16], cos2[:, :, 0:8]))

            def pair_copy(m, b):
                t = view(ps, b * 512, [[P, 4], [1, P]], n=64)
                dve.tensor_copy(view(pair, HK * S + m * P, [[S, 4], [1, P]], n=64), t)
                lo = 1 if m == 0 else 0
                return dve.tensor_copy(
                    view(pair, HK * S + m * P - 1 + lo, [[S, 4], [1, P - lo]], p0=64, n=64),
                    view(ps, b * 512 + lo, [[P, 4], [1, P - lo]], p0=64, n=64))

            def blocks(kv):
                for k0 in (0, 8):
                    ins = dve.tensor_tensor(view(tb_f, k0 * 64, [[64, 8], [16, HK], [1, NC]]),
                                            view(pair, kv * HK * S + 2 * k0, [[2, 8], [S, HK], [STRIDE, NC]]),
                                            view(g_t, 32 + k0, [[1, 8], [0, HK], [0, NC]]), ALU.add)
                ins.then_inc(tb_f_ready, 1)

            def block_lo(kv):
                dve.wait_ge(tb_hi_ready, kv + 1)
                dve.tensor_tensor(tb_lo[:, :, kv, :], tb_f[:, :, :, :].rearrange("p a b c -> p a (b c)"),
                                  tb_hi[:, :, kv, :].bitcast(F32), ALU.subtract).then_inc(tb_ready, 1)
                dve.wait_ge(tb_ready, kv + 1)

            link(dve.memset(tb_f[:, :, :, :], 0.0))
            dve.wait_ge(turned[0], 1)
            pair_copy(0, 4).then_inc(pair_dve, 1)
            split(5)
            rope(0, 3, stage_nsa, 0, 2 * HK, 0)
            dve.wait_ge(turned[0], 2)
            pair_copy(1, 6).then_inc(pair_dve, 1)
            split(6)
            rope(0, 4, stage_nsa, 1, 2 * HK, 1)
            dve.wait_ge(pair_act, 2)
            blocks(0)
            block_lo(0)
            split(7)
            rope(0, 5, stage_nsa, 0, 2 * HK, 0)
            dve.wait_ge(pair_dve, 2)
            blocks(1)
            block_lo(1)
            split(8)
            rope(0, 6, stage_nsa, 1, 2 * HK, 1)
            split(9)
            split(10)
            split(11)
            dve.wait_ge(hid_exp, 2)
            link(dve.tensor_scalar(e_hid[:, :], e_hid[:, :], 1.0, None, ALU.add))
            link(dve.reciprocal(e_hid[:, :], e_hid[:, :]))
            for kv, b in enumerate((3, 6)):
                r = slice(64 * kv, 64 * kv + 64)
                ins = dve.tensor_tensor(hid_r[r, :], ps[r, b, 0:256], e_hid[r, :], ALU.mult)
            ins.then_inc(hid_ready, 1)
            split(12)
            dve.wait_ge(hid_psum, 1)
            dve.tensor_copy(hid_k[:, :, :], view(ps, 3 * 512, [[P, 2], [1, 64]]))
            dve.tensor_copy(hid_v[:, 0:HK, :, :], view(ps, 3 * 512 + 64, [[16, HK], [0, G], [1, 16]]))
            dve.tensor_copy(hid_v[:, HK:2 * HK, :, :], view(ps, 3 * 512 + P + 64, [[16, HK], [0, G], [1, 16]]))\
               .then_inc(hid_out, 1)
            rope(0, 7, stage_rot, 0, 8, 0)
            split(13)
            rope(0, 8, stage_rot, 1, 8, 1)
            split(14)
            dve.wait_ge(kc_out, 1)
            dve.wait_ge(masks_ready, 4)
            for hk in range(HK):
                ins = dve.tensor_tensor(view(vc_bd, hk * G * DH, [[DH, G], [1, DH]], n=64),
                                        view(ps, 6 * 512 + P + hk * DH, [[0, G], [1, DH]], n=64),
                                        view(bd_mask, 0, [[1, G], [0, DH]], n=64), ALU.mult)
            ins.then_inc(vc_out, 1)
            rope(0, 9, stage_rot, 0, 8, 0)
            split(15)
            rope(0, 10, stage_rot, 1, 8, 1)
            split(16)
            dve.wait_ge(gate_exp, 2)
            flat = gates[:, :, :].rearrange("p a b -> p (a b)")
            link(dve.tensor_scalar(flat, flat, 1.0, None, ALU.add))
            link(dve.reciprocal(flat, flat))
            dve.wait_ge(sc_sum, 1)
            for odd, b in enumerate((6, 3)):
                last = dve.tensor_tensor(view(p_cmp, 16 * odd, [[256, MT], [32, H // 2], [1, 16]]),
                                         view(ps, b * 512, [[128, MT], [16, H // 2], [1, 16]]),
                                         view(mask_c, 0, [[16, MT], [0, H // 2], [1, 16]]), ALU.add)
            link(last)
            pcf = p_cmp[:, :, :, :].rearrange("p m a c -> p (m a) c")
            link(dve.tensor_reduce(mx_c[:, :], pcf, AX, ALU.max))
            dve.tensor_tensor(pcf, pcf, view(mx_c, 0, [[1, MT * H], [0, 16]]), ALU.subtract)\
               .then_inc(sc_ready, 1)

            def mask_unit(i, w, n, masks):
                dve.wait_ge(scores[i], w + 1)
                if w >= 4:
                    dve.wait_ge(pt_psum[i], w - 3)
                for br, mask in enumerate(masks):
                    ins = dve.tensor_tensor_reduce(
                        out=probs[:, w % 4, br * n:(br + 1) * n], in0=bank(w % 3, br * n, n),
                        in1=mask, scale=1.0, scalar=-INF, op0=ALU.add, op1=ALU.max,
                        accum_out=mx[:, w % 4, br:br + 1])
                link(ins)
                k = len(masks)
                dve.tensor_scalar(nm[:, w % 4, 0:k], mx[:, w % 4, 0:k], -SCALE, None, ALU.mult)\
                   .then_inc(masked[i], 1)

            def norm_unit(i, w, n, gate_cols):
                dve.wait_ge(expd[i], w + 1)
                k = len(gate_cols)
                link(dve.reciprocal(rl[:, w % 4, 0:k], l_u[:, w % 4, 0:k]))
                for br, gate in enumerate(gate_cols):
                    p = probs[:, w % 4, br * n:(br + 1) * n]
                    if gate is None:
                        ins = dve.tensor_scalar(p, p, rl[:, w % 4, br:br + 1], None, ALU.mult)
                    else:
                        ins = dve.tensor_scalar(p, p, rl[:, w % 4, br:br + 1], gate, ALU.mult, ALU.mult)
                ins.then_inc(normed[i], 1)

            def norm_nsa(u):
                hk, m, g = u // 8, u // 4 % 2, (0, 2, 1, 3)[u % 4]
                c = 16 + hk * G + g
                norm_unit(0, u, P * (m + 1), [gates[:, m, c:c + 1], gates[:, m, c + 16:c + 17]])

            def ot_lo(grp):
                hk, m = grp // 2, grp % 2
                dve.wait_ge(ot_hi[0], grp + 1)
                kts, cols = slice(2 * hk, 2 * hk + 2), slice(m * P, (m + 1) * P)
                dve.tensor_tensor(xt_lo[:, kts, cols],
                                  bank(5 + grp % 2, 0, 256).rearrange("p (a t) -> p a t", a=2),
                                  xt_hi[:, kts, cols].bitcast(F32), ALU.subtract)\
                   .then_inc(ot_ready[0], 1)

            U = 2 * H
            for s in range(U + 6):
                if s < U:
                    n = P * (s // 4 % 2 + 1)
                    mask_unit(0, s, n, [mask_nsa[:, 2 * P - n:2 * P]] * 2)
                if s == 2:
                    dve.wait_ge(pc_exp, 1)
                    link(dve.tensor_reduce(l_c[:, :], pcf, AX, ALU.add))
                    link(dve.reciprocal(l_c[:, :], l_c[:, :]))
                    lc2 = l_c[:, :].rearrange("p (m a) -> p m a", m=MT)
                    link(dve.tensor_tensor(lc2, lc2, gates[:, :, 0:16], ALU.mult))
                    link(dve.tensor_tensor(pcf, pcf, view(l_c, 0, [[1, MT * H], [0, 16]]), ALU.mult))
                    for m in range(MT):
                        last = dve.tensor_tensor(p_cmp[:, m, :, :], p_cmp[:, m, :, :],
                                                 view(valid_c, 16 * m, [[0, H], [1, 16]]), ALU.mult)
                    last.then_inc(pc_ready, 1)
                if 1 <= s < U + 1:
                    norm_nsa(s - 1)
                if s >= 9 and s % 4 == 1:
                    ot_lo((s - 9) // 4)

            def add_post(b, m):
                dve.wait_ge(sq_post[b], m + 1)
                link(rsqrt(ssq[:, MT + m:MT + m + 1], rs_post[:, m:m + 1]))
                if m == 0:
                    dve.wait_ge(gp_loaded[b - 1], 16)
                for half in range(2):
                    c = slice(512 * half, 512 * half + 512)
                    link(dve.scalar_tensor_tensor(tmp[:, m, c], bank(2 * m + half), rs_post[:, m:m + 1],
                                                  g_post[:, c], ALU.mult, ALU.mult))
                    dve.tensor_tensor(h[:, m, c], h[:, m, c], tmp[:, m, c], ALU.add).then_inc(h_ready[b], 1)

            def to_ffn(b, n, gain):
                split(n + 3)
                split(n + 4)
                split(n + 5)
                add_post(b, 0)
                xt_lo_out(b, 0, 0, gain)
                xt_lo_out(b, 0, 1, gain)
                h_rs(b, 0)
                split(n + 6)
                add_post(b, 1)
                xt_lo_out(b, 1, 0, gain)
                xt_lo_out(b, 1, 1, gain)
                h_rs(b, 1)

            def ffn(layer, n0):
                def hs_step(j, m):
                    dve.wait_ge(silu_done[layer], j * 2 + m + 1)
                    dve.scalar_tensor_tensor(hs[:, m, :], bank(4 + m, 256, 256), rs[:, m:m + 1],
                                             silu[:, m, :], ALU.mult, ALU.mult).then_inc(hs_ready[layer], 1)

                def ht_out(j, m):
                    dve.wait_ge(ht_hi[layer], j * 2 + m + 1)
                    hi = view(st_hi, m * P, [[S, 2], [1, P]])
                    dve.tensor_tensor(view(st_lo, m * P, [[S, 2], [1, P]]),
                                      bank(6 + m, 0, 256).rearrange("p (a t) -> p a t", a=2),
                                      hi.bitcast(F32), ALU.subtract).then_inc(ht_ready[layer], 1)

                def step(j, nx):
                    split(nx)
                    ht_out(j - 1, 1)
                    split(nx + 1, (0,))
                    hs_step(j, 0)
                    split(nx + 1, (1,))
                    split(nx + 2, (0,))
                    ht_out(j, 0)
                    split(nx + 2, (1,))
                    hs_step(j, 1)

                split(Piece(n0 + 3), (0,))
                hs_step(0, 0)
                split(Piece(n0 + 3), (1,))
                split(Piece(n0 + 4), (0,))
                ht_out(0, 0)
                split(Piece(n0 + 4), (1,))
                hs_step(0, 1)
                step(1, Piece(n0 + 5))
                with dve.Fori(0, (FJ - 3) // 2) as it:
                    for s in range(2):
                        step(it * 2 + (2 + s), Piece(n0 + 8 + 3 * s, it))
                step(FJ - 1, Piece(n0 + 3 * FJ - 1))
                ht_out(FJ - 1, 1)
                split(n0 + FFN_PIECES + 2)

            to_ffn(1, N_NSAO, 2)
            ffn(0, N_FFN0)
            for m in range(MT):
                add_post(2, m)
                for half in range(2):
                    xt_lo_out(2, m, half, 1, permuted=True)
            for m in range(MT):
                h_rs(2, m)
            dve.wait_ge(rs_turned, 1)
            dve.tensor_copy(rs_perm[:, :], bank(7, 0, MT)).then_inc(rs_perm_ready, 1)

            def dil_proj(hg, pat):
                e0 = 18 * hg

                def rot(c, m):
                    rope_dil(pat * 6 + (e0 + 2 * c + m + 3), pat * 4 + (12 * hg + 2 * c + m + 1), m)

                n = Piece(N_DIL + 18 * hg + AHEAD, pat)
                split(n)
                rot(0, 0)
                split(n + 1)
                rot(0, 1)
                split(n + 2)
                rot(1, 0)
                split(n + 3)
                rot(1, 1)
                split(n + 4)
                split(n + 5)

            def rope_dil(staged, products, m):
                x16 = view(stage_dil, m * 512, [[DH, 8], [1, ROT]])
                table = 2 + m
                dve.wait_ge(proj_out[1], staged)
                dve.tensor_tensor(rope_a[:, :, :], x16, view(cos2, table * ROT, [[0, 8], [1, ROT]]), ALU.mult)
                dve.tensor_tensor(rope_b[:, :, 0:8], view(stage_dil, m * 512 + 8, [[DH, 8], [1, 8]]),
                                  view(sin2, table * ROT, [[0, 8], [1, 8]]), ALU.mult)
                dve.tensor_tensor(rope_b[:, :, 8:16], view(stage_dil, m * 512, [[DH, 8], [1, 8]]),
                                  view(sin2, table * ROT + 8, [[0, 8], [1, 8]]), ALU.mult)\
                   .then_inc(rope_parts, 1)
                dve.wait_ge(rope_parts, products)
                dve.tensor_tensor(x16, rope_a[:, :, :], rope_b[:, :, :], ALU.add).then_inc(roped[1], 1)
                dve.wait_ge(roped[1], products)

            def ot_dil(hg, jq):
                dve.wait_ge(ot_hi[1], 2 * hg + jq + 1)
                src, dst = ot_views(hg, jq, xt_lo)
                _, hi = ot_views(hg, jq, xt_hi)
                dve.tensor_tensor(dst, src, hi.bitcast(F32), ALU.subtract).then_inc(ot_ready[1], 1)

            for hg in range(2):
                with dve.Fori(0, 3) as pat:
                    dil_proj(hg, pat)
                if hg == 0:
                    dve.wait_ge(dilmask_ready, 1)
                for s in range(16 + 1):
                    if s < 16:
                        mask_unit(1, 16 * hg + s, 512, [mask_dil[:, s % 2, :]])
                    if s >= 1:
                        norm_unit(1, 16 * hg + s - 1, 512, [None])
                    if hg == 1 and s in (1, 5, 13):
                        ot_dil(*{1: (0, 0), 5: (0, 1), 13: (1, 0)}[s])
            ot_dil(1, 1)
            to_ffn(3, N_DILO, 3)
            ffn(1, N_FFN1)
            for m in range(MT):
                add_post(4, m)

        @block.tensor
        def _(pe):
            owed = [0]

            def mm(o, s, m, start, stop):
                ins = pe.matmul(o, s, m, start=start, stop=stop)
                if owed[0]:
                    owed[0] = 0
                    ins.then_inc(piece_used, 1)
                    return None
                return ins

            def turn(b, k, src, n=P):
                ins = pe.transpose(ps[0:n, b, P * k:P * k + P], src, ident[:, :])
                if owed[0]:
                    owed[0] = 0
                    ins.then_inc(piece_used, 1)
                    return None
                return ins

            def three(o, s_hi, s_lo, m_hi, m_lo, start, stop):
                mm(o, s_hi, m_hi, start, False)
                mm(o, s_hi, m_lo, False, False)
                return mm(o, s_lo, m_hi, False, stop)

            def gemm(b, m, pc, first, last, done=None, mid=None, need=None):
                for half in range(2):
                    if half and mid:
                        mid()
                    if need:
                        need(half)
                    p = pc + half
                    for u in range(4):
                        if first and u % 2 == 0:
                            pe.wait_ge(lo_ready, p.halves(u // 2 + 1))
                        kt, c = 4 * half + u, 512 * u
                        cols = slice(m * P, (m + 1) * P)
                        ins = three(bank(b), xt_hi[:, kt, cols], xt_lo[:, kt, cols],
                                    w_hi[:, p.slot, c:c + 512], w_lo[:, p.slot, c:c + 512],
                                    kt == 0, kt == KT - 1)
                    if half == 0:
                        if last:
                            ins.then_inc(piece_used, 1)
                    elif done is not None:
                        ins.then_inc(done, 1)
                        owed[0] = int(last)
                    elif last:
                        ins.then_inc(piece_used, 1)

            def xt_turn(b, m, half, src):
                base = {0: 4 + 2 * m, 2: 6 - 2 * m}.get(b, 6)
                for k in range(4):
                    kt = 4 * half + k
                    ins = turn(base + half, k, src[:, m, kt * P:(kt + 1) * P])
                ins.then_inc(xt_psum[b], 1)

            pe.wait_ge(ident_ready, 1)
            pe.wait_ge(rows_loaded, 48)
            pe.transpose(bank(2, 0, 48), rows[:, :], ident[0:48, 0:48]).then_inc(rows_t, 1)
            for m in range(MT):
                pe.wait_ge(x_loaded[m], 16)
                for half in range(2):
                    xt_turn(0, m, half, h)

            def nsa_gemm(e, n):
                if e >= 2:
                    pe.wait_ge(proj_out[0], e - 1)
                m = e % 2
                need = (lambda half: pe.wait_ge(xt_ready[0], 2 * m + half + 1)) if e < 2 else None
                gemm(m, m, Piece(n), m == 0, m == 1, done=proj_done[0], need=need)

            def turn_cmp(m, banks):
                pe.wait_ge(proj_out[0], m + 1)
                for stage, b in zip((stage_nsa, stage_rot), banks):
                    for k in range(HK):
                        ins = turn(b, k, stage[:, m, P * k:P * k + P])
                ins.then_inc(turned[0], 1)

            def turn_kv(t, m, b):
                pe.wait_ge(roped[0], t + 1)
                for k in range(HK):
                    ins = turn(b, k, stage_nsa[:, m, P * k:P * k + P])
                ins.then_inc(turned[0], 1)

            def turn_q(t, m, b_plain, b_rot):
                pe.wait_ge(roped[0], t + 1)
                for stage, b in ((stage_nsa, b_plain), (stage_rot, b_rot)):
                    for k in range(4):
                        ins = turn(b, k, stage[:, m, P * k:P * k + P])
                ins.then_inc(turned[0], 1)

            def compress(kv, n, b):
                pe.wait_ge(lo_ready, Piece(n + 1).halves(2))
                pe.wait_ge(tb_ready, 2)
                for kt in range(16):
                    p, c = Piece(n + kt // 8), (kt % 8) * 256
                    ins = three(bank(b, 0, 256), tb_hi[:, kt, :, :].rearrange("p a b -> p (a b)"),
                                tb_lo[:, kt, :, :].rearrange("p a b -> p (a b)"),
                                w_hi[:, p.slot, c:c + 256], w_lo[:, p.slot, c:c + 256], kt == 0, kt == 15)
                    if kt == 7:
                        ins.then_inc(piece_used, 1)
                ins.then_inc(hid_sum, 1)
                owed[0] = 1

            nsa_gemm(0, N_CMPKV)
            nsa_gemm(1, N_CMPKV)
            pe.wait_ge(gw_ready, 1)
            for m in range(MT):
                for kt in range(KT):
                    cols = slice(m * P, (m + 1) * P)
                    ins = three(bank(3, 48 * m, 48), xt_hi[:, kt, cols], xt_lo[:, kt, cols],
                                gw_hi[:, kt, :], gw_lo[:, kt, :], kt == 0, kt == KT - 1)
            ins.then_inc(gate_sum, 1)
            turn_cmp(0, (2, 4))
            nsa_gemm(2, N_SEL)
            turn_cmp(1, (5, 6))
            nsa_gemm(3, N_SEL)
            turn_kv(0, 0, 7)
            nsa_gemm(4, N_WIN)
            pe.wait_ge(pair_act, 1)
            turn_kv(1, 1, 2)
            nsa_gemm(5, N_WIN)
            pe.wait_ge(pair_dve, 1)
            turn_kv(2, 0, 4)
            pe.wait_ge(gate_exp, 1)
            compress(0, N_WK1, 3)
            pe.wait_ge(pair_dve, 2)
            compress(1, N_WV1, 6)
            pe.wait_ge(pair_act, 2)
            turn_kv(3, 1, 5)
            nsa_gemm(6, N_Q)
            pe.wait_ge(hid_ready, 1)
            for k in range(2):
                ins = turn(3, k, hid_r[:, P * k:P * k + P])
            ins.then_inc(hid_psum, 1)
            nsa_gemm(7, N_Q)
            pe.wait_ge(turn_out[0], 2)
            turn_q(4, 0, 7, 2)
            pe.wait_ge(w2_loaded, 48)
            pe.wait_ge(hid_out, 1)
            for kt in range(2):
                mm(bank(6, 0, 64), w2k[:, kt, :, :].rearrange("p a d -> p (a d)"), hid_k[:, kt, :],
                   kt == 0, kt == 1)
            for hk in range(HK):
                for kt in range(2):
                    ins = mm(ps[0:64, 6, P + hk * DH:P + hk * DH + DH],
                             hid_v[:, HK * kt + hk, :, :].rearrange("p g c -> p (g c)"), w2v[:, kt, :],
                             kt == 0, kt == 1)
            ins.then_inc(kc_sum, 1)
            nsa_gemm(8, N_Q + 2)
            pe.wait_ge(turn_out[0], 4)
            turn_q(5, 1, 4, 5)
            nsa_gemm(9, N_Q + 2)
            pe.wait_ge(turn_out[0], 5)
            turn_q(6, 0, 7, 2)
            pe.wait_ge(turn_out[0], 6)
            turn_q(7, 1, 4, 5)

            pe.wait_ge(turn_out[0], 8)
            pe.wait_ge(kc_out, 1)
            pe.wait_ge(vc_out, 1)
            for m in range(MT):
                for hd in range(H):
                    p0 = DH * (hd % 2)
                    ins = pe.matmul(bank(3 if hd % 2 else 6, 128 * m + 16 * (hd // 2), 16),
                                    view(qu_t, (hd // 2) * S + m * P, [[1, P]], p0=p0, n=DH),
                                    view(kc_t, 16 * (hd // G), [[1, 16]], p0=p0, n=DH),
                                    start=True, stop=True)
            ins.then_inc(sc_sum, 1)
            pe.wait_ge(proj_out[0], 10)
            pe.wait_ge(sc_ready, 1)
            U = 2 * H

            def scores_nsa(u):
                hk, m, hd = u // 8, u // 4 % 2, u // 8 * G + (0, 2, 1, 3)[u % 4]
                p0, n = DH * (hd % 2), P * (m + 1)
                if u >= 3:
                    pe.wait_ge(masked[0], u - 2)
                for br in range(2):
                    ins = pe.matmul(bank(u % 3, br * n, n),
                                    view(q_t, (hd // 2) * S + m * P, [[1, P]], p0=p0, n=DH),
                                    view(k_t, (br * HK + hk) * S, [[1, n]], p0=p0, n=DH),
                                    start=True, stop=True)
                ins.then_inc(scores[0], 1)

            def turn_probs(i, w, blocks):
                pe.wait_ge(normed[i], w + 1)
                if w >= 2:
                    pe.wait_ge(pt_out[i], w - 1)
                for k in range(blocks):
                    ins = pe.transpose(bank(3 + w % 2, P * k, P), probs[:, w % 4, P * k:P * k + P],
                                       ident[:, :])
                ins.then_inc(pt_psum[i], 1)

            def pv_nsa(hf):
                grp, odd = hf // 2, hf % 2
                hk, m = grp // 2, grp % 2
                pe.wait_ge(pt_out[0], 2 * hf + 2)
                if grp >= 2 and not odd:
                    pe.wait_ge(ot_ready[0], grp - 1)
                o = ps[DH * odd:DH * odd + DH, 5 + grp % 2, 0:256]
                for br in range(2):
                    for kb in range(m + 1):
                        blk = br * (m + 1) + kb
                        pe.matmul(o, v_nsa[:, br, kb, hk * DH:(hk + 1) * DH],
                                  view(p_t, odd * 1024 + blk * 256, [[1, 256]]),
                                  start=blk == 0, stop=False, skip_group_check=True)
                if odd:
                    if grp == 0:
                        pe.wait_ge(pct_out, 2)
                    for k in range(2):
                        ins = pe.matmul(bank(5 + grp % 2, P * k, P), vc_bd[:, hk, P * k:P * k + P],
                                        pc_t[:, grp, :], start=False, stop=k == 1, skip_group_check=True)
                    ins.then_inc(pv_done[0], 1)

            for s in range(U + 4):
                if s < U:
                    scores_nsa(s)
                if s in (3, 5):
                    r = (s - 3) // 2
                    if r == 0:
                        pe.wait_ge(pc_ready, 1)
                    else:
                        pe.wait_ge(pct_out, 1)
                    for k in range(4):
                        grp = 4 * r + k
                        hk, m = grp // 2, grp % 2
                        ins = pe.transpose(ps[0:64, 7, P * k:P * k + P],
                                           p_cmp[:, m, G * hk:G * hk + G, :].rearrange("p a c -> p (a c)"),
                                           ident[:, :])
                    ins.then_inc(pct_psum, 1)
                if 3 <= s < U + 3:
                    turn_probs(0, s - 3, 2 * ((s - 3) // 4 % 2 + 1))
                if s >= 5 and s % 2 == 1:
                    pv_nsa((s - 5) // 2)

            def out_proj(b, n, ready):
                pcs = (Piece(n), Piece(n + 2))
                pe.wait_ge(*ready[0])
                gemm(0, 0, pcs[0], True, False)
                gemm(1, 0, pcs[1], True, False, done=acc_done[b])
                pe.wait_ge(*ready[1])
                gemm(2, 1, pcs[0], False, True)

                def turn_m0():
                    for half in range(2):
                        pe.wait_ge(h_ready[b], half + 1)
                        xt_turn(b, 0, half, h)

                gemm(3, 1, pcs[1], False, True, done=acc_done[b], mid=turn_m0)

            def ffn(layer, n0):
                b = 1 + 2 * layer

                def gu(j, m, pc, mid=None, need=None):
                    gemm(4 + m, m, pc, m == 0, m == 1, done=gu_done[layer], mid=mid, need=need)

                def ht_turn(j, m):
                    pe.wait_ge(hs_ready[layer], j * 2 + m + 1)
                    for k in range(2):
                        ins = turn(6 + m, k, hs[:, m, P * k:P * k + P])
                    ins.then_inc(ht_psum[layer], 1)

                def down(j, m, pc, first=False, last=False):
                    pe.wait_ge(ht_ready[layer], j * 2 + m + 1)
                    if m == 0:
                        pe.wait_ge(lo_ready, pc.halves(2))
                    for k in range(2):
                        for n in range(2):
                            c = k * D + 512 * n
                            cols = slice(k * S + m * P, k * S + (m + 1) * P)
                            ins = three(bank(2 * m + n), st_hi[:, cols], st_lo[:, cols],
                                        w_hi[:, pc.slot, c:c + 512], w_lo[:, pc.slot, c:c + 512],
                                        first and k == 0, last and k == 1)
                    if last:
                        ins.then_inc(acc_done[b + 1], 1)
                    elif m == 1:
                        ins.then_inc(piece_used, 1)

                def step(j, pc, first=False):
                    gu(j, 0, pc, mid=lambda: ht_turn(j - 1, 1))
                    down(j - 1, 0, pc + 2, first)
                    gu(j, 1, pc, mid=lambda: ht_turn(j, 0))
                    down(j - 1, 1, pc + 2, first)

                def need(m):
                    return lambda half: pe.wait_ge(xt_ready[b], 2 * m + half + 1)

                gu(0, 0, Piece(n0), need=need(0))
                for half in range(2):
                    pe.wait_ge(h_ready[b], 3 + half)
                    pe.wait_ge(xt_ready[b], 1 + half)
                    xt_turn(b, 1, half, h)
                gu(0, 1, Piece(n0), need=need(1), mid=lambda: ht_turn(0, 0))
                step(1, Piece(n0 + 2), first=True)
                with pe.Fori(0, (FJ - 3) // 2) as it:
                    for s in range(2):
                        step(it * 2 + (2 + s), Piece(n0 + 5 + 3 * s, it))
                step(FJ - 1, Piece(n0 + 3 * FJ - 4))
                ht_turn(FJ - 1, 1)
                down(FJ - 1, 0, Piece(n0 + FFN_PIECES - 1), last=True)
                down(FJ - 1, 1, Piece(n0 + FFN_PIECES - 1), last=True)
                owed[0] = 1

            out_proj(1, N_NSAO, ((ot_ready[0], 7), (ot_ready[0], 8)))
            ffn(0, N_FFN0)

            for m in range(MT):
                for half in range(2):
                    pe.wait_ge(h_ready[2], 2 * m + half + 1)
                    xt_turn(2, m, half, h)
            pe.wait_ge(xt_ready[2], 4)
            pe.wait_ge(rs_ready[2], 2)
            for m in range(MT):
                for hp in range(2):
                    for mp in range(MT):
                        r0 = 64 * hp + 32 * m
                        ins = pe.matmul(ps[r0:r0 + 32, 7, mp:mp + 1], view(ident, 2 * mp + hp, [[4, 32]]),
                                        rs[:, m:m + 1], start=True, stop=True)
            ins.then_inc(rs_turned, 1)

            def dil_proj(hg, pat):
                def proj(c, m):
                    e = 2 * c + m
                    pe.wait_ge(proj_out[1], pat * 6 + (18 * hg + e + 1))
                    gemm(m, m, Piece(N_DIL + 18 * hg + 2 * c, pat), m == 0, m == 1, done=proj_done[1])

                def turns_of(c, m):
                    t = 2 * c + m
                    pe.wait_ge(roped[1], pat * 4 + (12 * hg + t + 1))
                    pe.wait_ge(turn_out[1], pat * 4 + (12 * hg + t + 1))
                    for k in range(4):
                        ins = turn(2 + m, k, stage_dil[:, m, P * k:P * k + P])
                    ins.then_inc(turned[1], 1)

                proj(0, 0)
                proj(0, 1)
                turns_of(0, 0)
                proj(1, 0)
                turns_of(0, 1)
                proj(1, 1)
                turns_of(1, 0)
                proj(2, 0)
                proj(2, 1)
                turns_of(1, 1)

            def qk(pat, t, j, c, n):
                return view(qk_t, ((pat * 2 + t) * 4 + j // 2) * S + c, [[1, n]], p0=DH * (j % 2), n=DH)

            def scores_dil(hg, u):
                j, m, w = u // 2, u % 2, 16 * hg + u
                if w >= 3:
                    pe.wait_ge(masked[1], w - 2)
                for pat, c, k0, n in ((0, 0, 0, S), (1, 256, m * P, P), (2, 384, m * P, P)):
                    ins = pe.matmul(bank(w % 3, c, n), qk(pat, 0, j, m * P, P), qk(pat, 1, j, k0, n),
                                    start=True, stop=True)
                ins.then_inc(scores[1], 1)

            def pv_dil(hg, u):
                j, m, w = u // 2, u % 2, 16 * hg + u
                jq = j // 4
                pe.wait_ge(pt_out[1], w + 1)
                if (hg, u) == (1, 8):
                    pe.wait_ge(ot_ready[1], 1)
                o = view(ps, ot_bank(hg, jq) * 512 + (j // 2 % 2) * S + m * P, [[1, P]],
                         p0=DH * (j % 2), n=DH)
                for k, (pat, mk) in enumerate(((0, 0), (0, 1), (1, m), (2, m))):
                    ins = pe.matmul(o, v_dil[:, pat, mk, j * DH:(j + 1) * DH],
                                    p_t[:, 0, w % 2, P * k:P * k + P], start=k == 0, stop=k == 3)
                if u % 8 == 7:
                    ins.then_inc(pv_done[1], 1)

            for hg in range(2):
                with pe.Fori(0, 3) as pat:
                    dil_proj(hg, pat)
                pe.wait_ge(proj_out[1], 2 + 18 * (hg + 1))
                pe.wait_ge(turn_out[1], 2 + 12 * (hg + 1))
                for s in range(16 + 4):
                    if s < 16:
                        scores_dil(hg, s)
                    if 3 <= s < 19:
                        turn_probs(1, 16 * hg + s - 3, 4)
                    if s >= 4:
                        pv_dil(hg, s - 4)
            out_proj(3, N_DILO, ((ot_ready[1], 4), (ot_ready[1], 4)))
            ffn(1, N_FFN1)


_IN = ["x", "positions", "norm_mix_pre", "norm_mix_post", "norm_ffn_pre", "norm_ffn_post", "ffn_w_gu",
       "ffn_w_down", "nsa_w_in", "nsa_cmp_pos", "nsa_cmp_wk1", "nsa_cmp_wk2", "nsa_cmp_wv1",
       "nsa_cmp_wv2", "nsa_w_o", "dil_w_in", "dil_w_o"]


def kernel(**inputs):
    import concourse.bacc as bacc
    from concourse.bass_utils import run_bass_kernel_spmd

    nc = bacc.Bacc("TRN2", target_bir_lowering=False, num_devices=1)
    arrays, args = {}, []
    for name in _IN:
        a = np.ascontiguousarray(inputs[name])
        arrays[f"in_{name}"] = a
        args.append(nc.dram_tensor(f"in_{name}", a.shape, mybir.dt.from_np(a.dtype),
                                   kind="ExternalInput").ap())
    out = nc.dram_tensor("out_h", (1, S, D), F32, kind="ExternalOutput").ap()
    build(nc, *args, out)
    result = run_bass_kernel_spmd(nc, [arrays], core_ids=[0])
    return result.results[0]["out_h"]
```

```python
from contextlib import ExitStack

import numpy as np

import concourse.bass as bass
from concourse import mybir

ALU = mybir.AluOpType
ACT = mybir.ActivationFunctionType
AX = mybir.AxisListType.X
F32 = mybir.dt.float32
F32R = mybir.dt.float32r
BF16 = mybir.dt.bfloat16
I32 = mybir.dt.int32

P = 128
D = 1024
S = 256
MT = S // P
KT = D // P
DH = 64
H = D // DH
HK = 4
G = H // HK
FF = 2816
FJ = FF // 256
EPS = 1e-6
NEG = -1e30
SCALE = DH ** -0.5
ROT = DH // 4
THETA = 500000.0
CMP, STRIDE = 32, 16
NC = (S - CMP) // STRIDE + 1
PIECE = 2048
RAW = 2
RING = 6
U_NSA = MT * H
AHEAD = 3
TWO_PI = 6.283185307179586
MAGIC = 12582912.0
INF = 3.0e38

N_CMPKV, N_SEL, N_WIN, N_WK1, N_WV1, N_Q, N_NSAO = 0, 2, 4, 6, 8, 10, 14
N_FFN0 = 18
FFN_PIECES = 3 * FJ
N_DIL = N_FFN0 + FFN_PIECES
N_DILO = N_DIL + 36
N_FFN1 = N_DILO + 4
N_END = N_FFN1 + FFN_PIECES


class Piece:

    def __init__(self, n0, it=0):
        self.n0, self.it = n0, it

    def __add__(self, k):
        return Piece(self.n0 + k, self.it)

    @property
    def slot(self):
        return self.n0 % RING

    @property
    def raw(self):
        return self.n0 % RAW

    def loaded(self):
        return self.it * (16 * RING // RAW) + 16 * (self.n0 // RAW + 1)

    @property
    def woven(self):
        for first in (N_FFN0, N_FFN1):
            k = self.n0 - first
            if 0 <= k < FFN_PIECES - 1:
                return k < 2 or (k - 2) % 3 < 2
        return False

    def halves(self, k):
        return self.it * (2 * RING) + 2 * self.n0 + k

    def used(self):
        return self.it * RING + self.n0 + 1


def view(t, off, dims, p0=0, n=P):
    width = int(np.prod(t.shape[1:]))
    return bass.AP(t, p0 * width + off, [[width, n]] + [list(d) for d in dims])


def build(nc, x, positions, norm_mix_pre, norm_mix_post, norm_ffn_pre, norm_ffn_post, ffn_w_gu,
          ffn_w_down, nsa_w_in, nsa_cmp_pos, nsa_cmp_wk1, nsa_cmp_wk2, nsa_cmp_wv1, nsa_cmp_wv2,
          nsa_w_o, dil_w_in, dil_w_o, out):
    ctx = ExitStack()
    with ctx:
        place = [(int(nc.sbuf_base) + 31) // 32 * 32]

        def sb(name, shape, dt=F32, at=None):
            size = int(np.prod(shape[1:])) * mybir.dt.size(dt)
            if at is None:
                at = place[0]
                place[0] = (at + size + 31) // 32 * 32
            assert at + size <= nc.sbuf_usable_end, name
            return nc.alloc_sbuf_tensor_at(name, shape, dt, offset=at)

        def zone(size):
            at = place[0]
            place[0] = at + size
            return at

        w_raw = sb("w_raw", [P, RAW, PIECE])
        w_hi = sb("w_hi", [P, RING, PIECE], F32R)
        w_lo = sb("w_lo", [P, RING, PIECE], F32R)
        h = sb("h", [P, MT, D])
        at_tmp = zone(MT * D * 4)
        tmp = sb("tmp", [P, MT, D], at=at_tmp)
        probs = sb("probs", [P, 4, 512], at=at_tmp)
        pair = sb("pair", [P, 2, HK, S], at=at_tmp)
        xt_hi = sb("xt_hi", [P, KT, S], F32R)
        xt_lo = sb("xt_lo", [P, KT, S], F32R)
        at_gp = zone(D * 4)
        g_post = sb("g_post", [P, D], at=at_gp)
        w2k = sb("w2k", [P, 2, 2, DH], at=at_gp)
        w2v = sb("w2v", [P, 2, DH], at=at_gp + 1024)
        hid_k = sb("hid_k", [P, 2, 64], at=at_gp + 1536)
        e_hid = sb("e_hid", [P, 256], at=at_gp + 2048)
        gates_t = sb("gates_t", [48, S], at=at_gp + 2048)
        hid_r = sb("hid_r", [P, 256], at=at_gp + 3072)
        rows = sb("rows", [48, P], at=at_gp + 3072)

        at_a = zone(45056)
        q_t = sb("q_t", [P, H // 2, S], at=at_a)
        tb_hi = sb("tb_hi", [P, 16, 2, 64], F32R, at=at_a)
        tb_lo = sb("tb_lo", [P, 16, 2, 64], F32R, at=at_a + 8192)
        gw_hi = sb("gw_hi", [P, KT, P], F32R, at=at_a)
        gw_lo = sb("gw_lo", [P, KT, P], F32R, at=at_a + 4096)
        gw_raw = sb("gw_raw", [P, KT, P], at=at_a + 12288)
        qu_t = sb("qu_t", [P, H // 2, S], at=at_a + 8192)
        v_nsa = sb("v_nsa", [P, 2, MT, HK * DH], at=at_a + 32768)
        vc_bd = sb("vc_bd", [64, HK, G * DH], at=at_a + 36864)
        tb_f = sb("tb_f", [P, 16, HK, 16], at=at_a + 36864)
        pc_t = sb("pc_t", [64, 2 * HK, P], at=at_a + 40960)
        stage_nsa = sb("stage_nsa", [P, MT, 512], at=at_a + 40960)
        qk_t = sb("qk_t", [P, 3, 2, 4, S], at=at_a)
        v_dil = sb("v_dil", [P, 3, MT, 512], at=at_a + 24576)
        silu = sb("silu", [P, MT, 256], at=at_a)
        hs = sb("hs", [P, MT, 256], at=at_a + 2048)

        k_z = sb("k_z", [P, 2, 2, HK, S], at=at_a + 16384)

        at_s = zone(10240)
        p_t = sb("p_t", [P, 4, 512], at=at_s)
        st_hi = sb("st_hi", [P, 512], F32R, at=at_s)
        st_lo = sb("st_lo", [P, 512], F32R, at=at_s + 2048)
        stage_rot = sb("stage_rot", [P, MT, 512], at=at_s)
        stage_dil = sb("stage_dil", [P, MT, 512], at=at_s)

        at_m = zone(2048)
        mask_dil = sb("mask_dil", [P, MT, 512], BF16, at=at_m)
        hid_v = sb("hid_v", [P, 2 * HK, G, 16], at=at_m)
        p_cmp = sb("p_cmp", [P, MT, H, 16], at=at_m)
        mask_nsa = sb("mask_nsa", [P, 2 * P], BF16)
        ident = sb("ident", [P, P])
        mask_c = sb("mask_c", [P, MT, 16])
        valid_c = sb("valid_c", [P, MT, 16])
        bd_mask = sb("bd_mask", [64, G])
        cos2 = sb("cos2", [P, MT, ROT])
        sin2 = sb("sin2", [P, MT, ROT])
        g_t = sb("g_t", [P, 48])
        inv_f = sb("inv_f", [P, ROT // 2])
        kc_bd = sb("kc_bd", [P, HK, 32])
        gates = sb("gates", [P, MT, 48])
        rs = sb("rs", [P, MT])
        rs_post = sb("rs_post", [P, MT])
        ssq = sb("ssq", [P, 2 * MT])
        nt = sb("nt", [P, 4])
        rs_perm = sb("rs_perm", [P, MT])
        mn = sb("mn", [P, 4, 2])
        l_u = sb("l_u", [P, 4, 2])
        rl = sb("rl", [P, 4, 2])
        mx_c = sb("mx_c", [P, MT, H])
        l_c = sb("l_c", [P, MT, H])
        pos_i = sb("pos_i", [P, MT], I32, at=at_a + 8192)
        pos_f = sb("pos_f", [P, MT], at=at_a + 8256)
        ang = sb("ang", [P, MT, 8], at=at_a + 8320)
        turns = sb("turns", [P, MT, 8], at=at_a + 8448)
        half_pi = sb("half_pi", [P, MT, 8], at=at_a + 8576)
        rope_a = sb("rope_a", [P, 8, ROT], at=at_s + 8192)
        rope_b = sb("rope_b", [P, 8, ROT], at=at_s + 8704)

        ps = ctx.enter_context(nc.psum_tensor("ps", [P, 8, 512], F32))

        def bank(b, off=0, n=512):
            return ps[:, b, off:off + n]

        def xt_bank(b, m, half):
            return {0: 4 + 2 * m + half, 2: 4 + m + 2 * half}.get(b, 6 + half)

        def xt_views(b, m, half, kt, dst):
            b_xt = xt_bank(b, m, half)
            return bank(b_xt, P * (kt % 4), P), dst[:, kt, m * P:(m + 1) * P]

        def unit_nsa(u):
            return u // 4 * 2 + u % 2, u // 2 % 2

        def ffn_order(j, m):
            return 2 * m + j if isinstance(j, int) and j < 2 else j * 2 + m

        def gu_bank(j, m):
            return 4 + (j if isinstance(j, int) and j < 2 else m)

        def score_bank(w):
            return (0, 2, 1)[w % 3]

        def tile_order(c, m, first):
            return c + 2 * m if first and c < 2 else 2 * c + m

        def proj_bank(c, m, first):
            return (6, 5)[m] if first and c == 1 else m

        def ot_bank(hg, jq):
            return 5 + jq if hg == 0 else 7 - 2 * jq

        def ot_views(hg, jq, dst):
            return (view(ps, ot_bank(hg, jq) * 512, [[S, 2], [P, 2], [1, P]]),
                    view(dst, (4 * hg + 2 * jq) * S, [[S, 2], [1, 2], [2, P]]))

        def sem(name):
            return ctx.enter_context(nc.semaphore(name))

        raw_loaded = [[sem(f"raw_loaded{i}_{k}") for k in range(2)] for i in range(RAW)]
        hi_ready, lo_ready, piece_used = sem("hi_ready"), sem("lo_ready"), sem("piece_used")
        x_loaded = [sem(f"x_loaded{m}") for m in range(MT)]
        rows_loaded, pos_loaded, w2_loaded = sem("rows_loaded"), sem("pos_loaded"), sem("w2_loaded")
        gw_loaded, out_stored = sem("gw_loaded"), sem("out_stored")
        gp_loaded = [sem(f"gp_loaded{i}") for i in range(4)]
        ident_ready, masks_ready = sem("ident_ready"), sem("masks_ready")
        dilmask_ready, rope_ready = sem("dilmask_ready"), sem("rope_ready")
        angles_ready = sem("angles_ready")
        pool_step, dve_step = sem("pool_step"), sem("dve_step")
        rows_t, gt_ready = sem("rows_t"), sem("gt_ready")
        gw_hi_ready, gw_ready = sem("gw_hi_ready"), sem("gw_ready")
        acc_done = [sem(f"acc_done{b}") for b in range(5)]
        sq_post = [sem(f"sq_post{b}") for b in range(5)]
        post_ready = [sem(f"post_ready{b}") for b in range(5)]
        h_ready = [sem(f"h_ready{b}") for b in range(5)]
        sq_h = [sem(f"sq_h{b}") for b in range(4)]
        rs_ready = [sem(f"rs_ready{b}") for b in range(4)]
        rs_turned, rs_perm_ready = sem("rs_turned"), sem("rs_perm_ready")
        xt_psum = [sem(f"xt_psum{b}") for b in range(4)]
        xt_hi_ready = [sem(f"xt_hi_ready{b}") for b in range(4)]
        xt_ready = [sem(f"xt_ready{b}") for b in range(4)]
        proj_done = [sem(f"proj_done{i}") for i in range(2)]
        proj_out = [sem(f"proj_out{i}") for i in range(2)]
        roped = [sem(f"roped{i}") for i in range(2)]
        turned = [sem(f"turned{i}") for i in range(2)]
        turn_out = [sem(f"turn_out{i}") for i in range(2)]
        rope_parts = sem("rope_parts")
        pair_act, pair_dve = sem("pair_act"), sem("pair_dve")
        tb_f_ready, tb_hi_ready, tb_ready = sem("tb_f_ready"), sem("tb_hi_ready"), sem("tb_ready")
        gate_zero, gate_sum, gate_copied = sem("gate_zero"), sem("gate_sum"), sem("gate_copied")
        gate_turned, gate_exp = sem("gate_turned"), sem("gate_exp")
        hid_sum, hid_exp, hid_ready = sem("hid_sum"), sem("hid_exp"), sem("hid_ready")
        kc_sum, kc_out, vc_out = sem("kc_sum"), sem("kc_out"), sem("vc_out")
        hid_psum, hid_out = sem("hid_psum"), sem("hid_out")
        sc_sum, sc_ready, pc_exp, pc_ready = sem("sc_sum"), sem("sc_ready"), sem("pc_exp"), sem("pc_ready")
        pct_psum, pct_out = sem("pct_psum"), sem("pct_out")
        scores = [sem(f"scores{i}") for i in range(2)]
        masked = [sem(f"masked{i}") for i in range(2)]
        expd = [sem(f"expd{i}") for i in range(2)]
        normed = [sem(f"normed{i}") for i in range(2)]
        pt_psum = [sem(f"pt_psum{i}") for i in range(2)]
        pt_out = [sem(f"pt_out{i}") for i in range(2)]
        pv_done = [sem(f"pv_done{i}") for i in range(2)]
        ot_hi = [sem(f"ot_hi{i}") for i in range(2)]
        ot_ready = [sem(f"ot_ready{i}") for i in range(2)]
        gu_done = [sem(f"gu_done{l}") for l in range(2)]
        silu_done = [sem(f"silu_done{l}") for l in range(2)]
        hs_ready = [sem(f"hs_ready{l}") for l in range(2)]
        ht_psum = [sem(f"ht_psum{l}") for l in range(2)]
        ht_hi = [sem(f"ht_hi{l}") for l in range(2)]
        ht_ready = [sem(f"ht_ready{l}") for l in range(2)]

        block = ctx.enter_context(nc.Block())

        @block.sync
        def _(sp):
            def load(pc, *parts):
                for k, (src, c, dims) in enumerate(parts):
                    if pc.n0 >= RAW and not (pc.woven and k):
                        sp.wait_ge(lo_ready, pc.halves(2 if pc.woven else k + 1) - 2 * RAW)
                    sp.dma_start(view(w_raw, pc.raw * PIECE + c, dims), src)\
                      .then_inc(raw_loaded[pc.raw][k], 16)

            def chunk(n, w, c0, between=None):
                wv = w.rearrange("(k p) c -> p k c", p=P)
                for half in range(2):
                    if half and between:
                        between()
                    load(n + half, *[(wv[:, 4 * half + k:4 * half + k + 2, bass.ds(c0, 512)], 512 * k,
                                      [[512, 2], [1, 512]]) for k in (0, 2)])

            def x_load(m):
                sp.dma_start(h[:, m, :], x[0, m * P:(m + 1) * P, :]).then_inc(x_loaded[m], 16)

            w_in = nsa_w_in[0]
            x_load(0)
            chunk(Piece(N_CMPKV), w_in, 1024, between=lambda: x_load(1))
            sp.dma_start(gw_raw[:, :, 0:48], nsa_w_in[0].rearrange("(k p) c -> p k c", p=P)[:, :, 2560:2608])\
              .then_inc(gw_loaded, 16)
            sp.dma_start(pos_i[:, :], bass.AP(positions.tensor, 0, [[1, P], [P, 2]]),
                         allow_slow_non_contiguous=True).then_inc(pos_loaded, 16)
            chunk(Piece(N_SEL), w_in, 1536)
            for dst, w in ((w2k[:, :, 0, :], nsa_cmp_wk2), (w2k[:, :, 1, :], nsa_cmp_wk2), (w2v[:, :, :], nsa_cmp_wv2)):
                sp.dma_start(dst, w[0].rearrange("(k p) d -> p k d", p=P)).then_inc(w2_loaded, 16)

            def cmp_w1(n, w):
                wv = w[0].rearrange("(k p) c -> p k c", p=P)
                for half in range(2):
                    load(n + half, *[(wv[:, 8 * half + k:8 * half + k + 4, :], 256 * k,
                                      [[256, 4], [1, 256]]) for k in (0, 4)])

            chunk(Piece(N_WIN), w_in, 2048)
            cmp_w1(Piece(N_WK1), nsa_cmp_wk1)
            cmp_w1(Piece(N_WV1), nsa_cmp_wv1)
            chunk(Piece(N_Q), w_in, 0)
            chunk(Piece(N_Q + 2), w_in, 512)

            def out_proj(n, w):
                chunk(Piece(n), w[0], 0)
                chunk(Piece(n + 2), w[0], 512)

            def ffn_loads(n0, layer):
                gu = ffn_w_gu[layer].rearrange("(k p) (s c) -> p k s c", p=P, s=2)
                dn = ffn_w_down[layer].rearrange("(k p) c -> p k c", p=P)

                def gu_load(pc, j):
                    for half in range(2):
                        load(pc + half, *[(gu[:, 4 * half:4 * half + 4, s, bass.ds(j * 256, 256)], 256 * s,
                                           [[512, 4], [1, 256]]) for s in range(2)])

                def dn_load(pc, j):
                    load(pc, *[(dn[:, bass.ds(j * 2 + k, 1), :], D * k, [[D, 1], [1, D]]) for k in range(2)])

                def step(pc, j):
                    gu_load(pc, j)
                    dn_load(pc + 2, j - 1)

                gu_load(Piece(n0), 0)
                step(Piece(n0 + 2), 1)
                with sp.Fori(0, (FJ - 3) // 2) as it:
                    for s in range(2):
                        step(Piece(n0 + 5 + 3 * s, it), it * 2 + (2 + s))
                step(Piece(n0 + 3 * FJ - 4), FJ - 1)
                dn_load(Piece(n0 + FFN_PIECES - 1), FJ - 1)

            out_proj(N_NSAO, nsa_w_o)
            ffn_loads(N_FFN0, 0)
            for hg in range(2):
                with sp.Fori(0, 3) as pat:
                    for t in range(3):
                        chunk(Piece(N_DIL + 18 * hg + 2 * t, pat), dil_w_in[0],
                              pat * (3 * D) + (t * D + hg * 512))
            out_proj(N_DILO, dil_w_o)
            ffn_loads(N_FFN1, 1)
            for q in range(2 * MT):
                m, half = q // 2, q % 2
                sp.wait_ge(h_ready[4], q + 1)
                sp.dma_start(out[0, m * P:(m + 1) * P, half * 512:(half + 1) * 512],
                             h[:, m, half * 512:(half + 1) * 512]).then_inc(out_stored, 16)
            sp.wait_ge(out_stored, 16 * 2 * MT)

        @block.gpsimd
        def _(pool):
            done = [0]

            def link(ins):
                done[0] += 1
                ins.then_inc(pool_step, 1)
                pool.wait_ge(pool_step, done[0])

            link(pool.memset(ident[:, :], 0.0))
            pool.affine_select(out=ident[:, :], in_=ident[:, :], compare_op=ALU.not_equal, fill=1.0,
                               base=0, pattern=[[-1, P]], channel_multiplier=1).then_inc(ident_ready, 1)
            pool.memset(gw_raw[:, :, 48:P], 0.0).then_inc(gate_zero, 1)
            for i in range(ROT // 2):
                f = float(np.float32(THETA) ** np.float32(-2.0 * i / ROT))
                ins = pool.memset(inv_f[:, i:i + 1], f)
            ins.then_inc(rope_ready, 1)
            link(pool.memset(mask_nsa[:, :], 0.0))
            pool.affine_select(out=mask_nsa[:, P:2 * P], in_=mask_nsa[:, P:2 * P], compare_op=ALU.is_ge,
                               fill=-NEG, base=0, pattern=[[-1, P]], channel_multiplier=1)\
                .then_inc(masks_ready, 1)
            for t, good, bad in ((mask_c, 0.0, NEG), (valid_c, 1.0, 0.0)):
                link(pool.memset(t[:, :, :], good))
                pool.affine_select(out=t[:, :, :], in_=t[:, :, :], compare_op=ALU.is_ge, fill=bad,
                                   base=-(CMP - 1), pattern=[[P, MT], [-STRIDE, 16]],
                                   channel_multiplier=1).then_inc(masks_ready, 1)
            link(pool.memset(kc_bd[:, :, :], 0.0))
            for par in range(2):
                link(pool.memset(k_z[64 - 64 * par:128 - 64 * par, par, :, :, :], 0.0))
            link(pool.memset(bd_mask[:, :], 1.0))
            link(pool.affine_select(out=bd_mask[:, :], in_=bd_mask[:, :], compare_op=ALU.is_ge, fill=0.0,
                                    base=0, pattern=[[-16, G]], channel_multiplier=1))
            pool.affine_select(out=bd_mask[:, :], in_=bd_mask[:, :], compare_op=ALU.is_ge, fill=0.0,
                               base=15, pattern=[[16, G]], channel_multiplier=-1).then_inc(masks_ready, 1)

            def post_gain(b, w, layer):
                pool.dma_start(g_post[:, :], bass.AP(w.tensor, layer * D, [[0, P], [1, D]]))\
                    .then_inc(gp_loaded[b - 1], 16)

            pool.wait_ge(kc_sum, 1)
            post_gain(1, norm_mix_post, 0)

            pool.wait_ge(pct_psum, 2)
            link(pool.memset(mask_dil[:, :, 0:256], 0.0))
            link(pool.memset(mask_dil[:, :, 256:512], -NEG))
            for m in range(MT):
                p0 = mask_dil[:, m, 0:256].rearrange("p (b q) -> p b q", b=2)
                link(pool.affine_select(out=p0, in_=p0, compare_op=ALU.is_ge, fill=-NEG,
                                        base=m, pattern=[[-1, 2], [-2, P]], channel_multiplier=2))
                link(pool.affine_select(out=p0, in_=p0, compare_op=ALU.is_ge, fill=-NEG,
                                        base=128 - m, pattern=[[1, 2], [2, P]], channel_multiplier=-2))
            for c, step in ((256, 2), (384, 8)):
                pd = mask_dil[:, 0, c:c + P]
                for d in range(0, P, step):
                    link(pool.affine_select(out=pd, in_=pd, compare_op=ALU.not_equal, fill=0.0,
                                            base=-d, pattern=[[-1, P]], channel_multiplier=1))
            link(pool.tensor_copy(mask_dil[:, 1, 256:512], mask_dil[:, 0, 256:512]))
            pool.sem_inc(dilmask_ready, 1)
            nexts = {1: (norm_ffn_post, 0), 2: (norm_mix_post, 1), 3: (norm_ffn_post, 1)}
            for b in range(1, 5):
                for q in range(2 * MT):
                    m, c = q // 2, slice(512 * (q % 2), 512 * (q % 2) + 512)
                    pool.wait_ge(post_ready[b], q + 1)
                    pool.tensor_tensor(h[:, m, c], h[:, m, c], tmp[:, m, c], ALU.add).then_inc(h_ready[b], 1)
                if b < 4:
                    post_gain(b + 1, *nexts[b])

        @block.scalar
        def _(act):
            def split(n, halves=(0, 1)):
                if isinstance(n, int):
                    n = Piece(n)
                if n.n0 >= N_END:
                    return
                for k in halves:
                    act.wait_ge(raw_loaded[n.raw][k], n.loaded())
                    if k == 0:
                        if n.woven:
                            act.wait_ge(raw_loaded[n.raw][1], n.loaded())
                        if n.n0 >= RING or not isinstance(n.it, int):
                            act.wait_ge(piece_used, n.used() - RING)
                    c = 1024 * k
                    act.activation(w_hi[:, n.slot, c:c + 1024], w_raw[:, n.raw, c:c + 1024], ACT.Copy)\
                       .then_inc(hi_ready, 1)

            def xt_out(b, m, half, gain):
                act.wait_ge(xt_psum[b], 2 * m + half + 1)
                for k in range(4):
                    kt = 4 * half + k
                    src, dst = xt_views(b, m, half, kt, xt_hi)
                    ins = act.activation(dst, src, ACT.Copy, scale=g_t[:, 8 * gain + kt:8 * gain + kt + 1])
                ins.then_inc(xt_hi_ready[b], 1)

            def h_squares(b, m):
                act.activation(tmp[:, m, :], h[:, m, :], ACT.Square, accum_out=ssq[:, m:m + 1])\
                   .then_inc(sq_h[b], 1)

            act.dma_start(rows[0:16, :], norm_mix_pre.rearrange("l (k p) -> (l k) p", p=P))\
               .then_inc(rows_loaded, 16)
            act.dma_start(rows[16:32, :], norm_ffn_pre.rearrange("l (k p) -> (l k) p", p=P))\
               .then_inc(rows_loaded, 16)
            act.dma_start(rows[32:48, :], nsa_cmp_pos[0].rearrange("(k a) d -> k (a d)", a=2))\
               .then_inc(rows_loaded, 16)
            act.wait_ge(x_loaded[0], 16)
            h_squares(0, 0)
            act.wait_ge(gt_ready, 1)
            xt_out(0, 0, 0, 0)
            split(0)
            xt_out(0, 0, 1, 0)
            split(1)
            xt_out(0, 1, 0, 0)
            xt_out(0, 1, 1, 0)
            act.wait_ge(x_loaded[1], 16)
            h_squares(0, 1)
            split(2)
            act.wait_ge(gw_loaded, 16)
            act.wait_ge(gate_zero, 1)
            act.activation(gw_hi[:, :, :], gw_raw[:, :, :], ACT.Copy).then_inc(gw_hi_ready, 1)

            ev = [0]

            def proj_evac(dsts):
                e = ev[0]
                m = e % 2
                if e < 2:
                    act.wait_ge(rs_ready[0], m + 1)
                act.wait_ge(proj_done[0], e + 1)
                for dst, src in dsts(m):
                    ins = act.activation(dst, src, ACT.Copy, scale=rs[:, m:m + 1])
                ins.then_inc(proj_out[0], 1)
                ev[0] += 1

            def twice(stage, m, c):
                return (view(stage, m * 512, [[P, HK], [DH, 2], [1, DH]]),
                        view(ps, m * 512 + c, [[DH, HK], [0, 2], [1, DH]]))

            tv = [0]

            def turn_evac(parts):
                act.wait_ge(turned[0], tv[0] + 1)
                for dst, src, *scale in parts:
                    ins = act.activation(dst, src, ACT.Copy, scale=scale[0] if scale else 1.0)
                ins.then_inc(turn_out[0], 1)
                tv[0] += 1

            def turn_kv(br, m, b):
                turn_evac([(k_z[64 * par:64 * par + 64, par, br, :, m * P:(m + 1) * P],
                            ps[64 * par:64 * par + 64, b, :].rearrange("p (a t) -> p a t", a=HK))
                           for par in range(2)])

            def quads(b):
                return bank(b).rearrange("p (a t) -> p a t", a=4)

            proj_evac(lambda m: [twice(stage_nsa, m, 0), twice(stage_rot, m, 256)])
            split(3)
            proj_evac(lambda m: [twice(stage_nsa, m, 0), twice(stage_rot, m, 256)])
            split(4)
            act.wait_ge(gate_sum, 1)
            act.activation(gates_t[:, :], ps[0:48, 3, 0:256], ACT.Copy).then_inc(gate_copied, 1)
            act.wait_ge(angles_ready, 1)
            act.activation(sin2[:, :, 8:16], ang[:, :, :], ACT.Sin)
            act.activation(cos2[:, :, 0:8], half_pi[:, :, :], ACT.Sin).then_inc(rope_ready, 1)

            def pair_k(m, b):
                act.wait_ge(turned[0], m + 1)
                act.activation(view(pair, m * P, [[S, 4], [1, P]], n=64),
                               view(ps, b * 512, [[P, 4], [1, P]], n=64), ACT.Copy)
                lo = 1 if m == 0 else 0
                act.activation(view(pair, m * P - 1 + lo, [[S, 4], [1, P - lo]], p0=64, n=64),
                               view(ps, b * 512 + lo, [[P, 4], [1, P - lo]], p0=64, n=64), ACT.Copy)\
                   .then_inc(pair_act, 1)

            def block_hi(kv):
                act.wait_ge(tb_f_ready, kv + 1)
                act.activation(tb_hi[:, :, kv, :], tb_f[:, :, :, :].rearrange("p a b c -> p a (b c)"), ACT.Copy)\
                   .then_inc(tb_hi_ready, 1)

            pair_k(0, 2)
            split(5)
            kv_sel = lambda m: [twice(stage_nsa, m, 0), (v_nsa[:, 0, m, :], bank(m, 256, 256))]
            kv_win = lambda m: [twice(stage_nsa, m, 0), (v_nsa[:, 1, m, :], bank(m, 256, 256))]
            proj_evac(kv_sel)
            pair_k(1, 5)
            tv[0] = 2
            act.wait_ge(gate_turned, 1)
            for m in range(MT):
                ins = act.activation(gates[:, m, :], bank(3, 256 + 48 * m, 48), ACT.Copy,
                                     scale=rs[:, m:m + 1])
            ins.then_inc(gate_exp, 1)
            act.wait_ge(gate_exp, 1)
            act.activation(gates[:, :, :], gates[:, :, :], ACT.Exp, scale=-1.0).then_inc(gate_exp, 1)
            split(6)
            proj_evac(kv_sel)
            block_hi(0)
            turn_kv(0, 0, 7)
            split(7, (0,))
            block_hi(1)
            split(7, (1,))
            proj_evac(kv_win)
            turn_kv(0, 1, 2)
            split(8)
            proj_evac(kv_win)
            split(9)
            turn_kv(1, 0, 4)
            split(10)
            split(11)
            for kv, b in enumerate((3, 6)):
                act.wait_ge(hid_sum, kv + 1)
                r = slice(64 * kv, 64 * kv + 64)
                act.activation(e_hid[r, :], ps[r, b, 0:256], ACT.Exp, scale=-1.0).then_inc(hid_exp, 1)
            turn_kv(1, 1, 5)
            split(12)
            q_rows = lambda m: [(stage_nsa[:, m, :], bank(m)), (stage_rot[:, m, :], bank(m))]

            def turn_q(c, m, b_plain, b_rot):
                turn_evac([(qu_t[:, 4 * c:4 * c + 4, m * P:m * P + P], quads(b_plain)),
                           (q_t[:, 4 * c:4 * c + 4, m * P:m * P + P], quads(b_rot), -SCALE)])

            def cmp_exp(r):
                act.wait_ge(sc_ready, r + 1)
                p = p_cmp[:, :, 8 * r:8 * r + 8, :]
                act.activation(p, p, ACT.Exp, scale=SCALE).then_inc(pc_exp, 1)

            def cmp_turned(r):
                act.wait_ge(pct_psum, r + 1)
                act.activation(pc_t[:, 4 * r:4 * r + 4, :],
                               view(ps, (6 + r) * 512, [[P, 4], [1, P]], n=64), ACT.Copy).then_inc(pct_out, 1)

            proj_evac(q_rows)
            split(13)
            proj_evac(q_rows)
            split(14, (0,))
            turn_q(0, 0, 7, 2)
            act.wait_ge(kc_sum, 1)
            act.wait_ge(masks_ready, 4)
            for r0 in (0, 64):
                ins = act.activation(view(kc_bd, r0 // 4, [[32, HK], [1, 16]], p0=r0, n=64),
                                     view(ps, 6 * 512, [[16, HK], [1, 16]], p0=r0, n=64), ACT.Copy)
            ins.then_inc(kc_out, 1)
            split(14, (1,))
            proj_evac(q_rows)
            split(15, (0,))
            turn_q(0, 1, 4, 5)
            split(15, (1,))
            cmp_exp(0)

            def exp_unit(i, w, n, parts):
                act.wait_ge(masked[i], w + 1)
                if w >= 4:
                    act.wait_ge(normed[i], w - 3)
                for br in range(parts):
                    p = probs[:, w % 4, br * n:(br + 1) * n]
                    ins = act.activation(p, p, ACT.Exp, bias=mn[:, w % 4, br:br + 1], scale=-1.0,
                                         accum_out=l_u[:, w % 4, br:br + 1])
                ins.then_inc(expd[i], 1)

            def ot_evac(hk):
                act.wait_ge(pv_done[0], hk + 1)
                act.activation(xt_hi[:, 2 * hk:2 * hk + 2, :],
                               bank(5 + hk % 2).rearrange("p (a t) -> p a t", a=2), ACT.Copy)\
                   .then_inc(ot_hi[0], 1)

            def pt_evac(i, w, n):
                act.wait_ge(pt_psum[i], w + 1)
                act.activation(p_t[:, w % 4, 0:n], bank(3 + w % 2, 0, n), ACT.Copy).then_inc(pt_out[i], 1)

            exp_unit(0, 0, P, 2)
            exp_unit(0, 1, P, 2)
            proj_evac(q_rows)
            turn_q(1, 0, 7, 5)
            for s in range(2, U_NSA + 4):
                if s == 11:
                    cmp_exp(1)
                if s in (2, 16):
                    cmp_turned(int(s == 16))
                if U_NSA <= s < U_NSA + 2:
                    split(16, (s - U_NSA,))
                if 3 <= s < U_NSA + 3:
                    pt_evac(0, s - 3, 2 * P * (unit_nsa(s - 3)[1] + 1))
                if s == 3:
                    turn_q(1, 1, 7, 5)
                if s < U_NSA:
                    exp_unit(0, s, P * (unit_nsa(s)[1] + 1), 2)
                if s >= 14 and s % 8 == 6:
                    ot_evac((s - 14) // 8)
            ot_evac(HK - 1)
            def post_squares(b, m):
                act.wait_ge(acc_done[b], m + 1)
                act.activation(tmp[:, m, :], ps[:, 2 * m:2 * m + 2, :].rearrange("p a c -> p (a c)"),
                               ACT.Square, accum_out=ssq[:, MT + m:MT + m + 1]).then_inc(sq_post[b], 1)

            def to_ffn(b, n, gain):
                split(n + 3)
                split(n + 4)
                split(n + 5)
                post_squares(b, 0)
                split(n + 6)
                split(n + 7)
                xt_out(b, 0, 0, gain)
                xt_out(b, 0, 1, gain)
                post_squares(b, 1)
                h_squares(b, 0)

            def ffn(layer, n0):
                b = 1 + 2 * layer

                def silu_step(j, m):
                    act.wait_ge(gu_done[layer], ffn_order(j, m) + 1)
                    act.activation(silu[:, m, :], bank(gu_bank(j, m), 0, 256), ACT.Silu, scale=rs[:, m:m + 1])\
                       .then_inc(silu_done[layer], 1)

                def ht_out(j, m):
                    act.wait_ge(ht_psum[layer], ffn_order(j, m) + 1)
                    act.activation(view(st_hi, m * P, [[S, 2], [1, P]]),
                                   bank(6 + m, 0, 256).rearrange("p (a t) -> p a t", a=2), ACT.Copy)\
                       .then_inc(ht_hi[layer], 1)

                def step(j, nx):
                    split(nx)
                    ht_out(j - 1, 1)
                    split(nx + 1, (0,))
                    silu_step(j, 0)
                    split(nx + 1, (1,))
                    split(nx + 2, (0,))
                    ht_out(j, 0)
                    split(nx + 2, (1,))
                    silu_step(j, 1)

                gain = 2 + layer
                split(Piece(n0 + 4))
                act.wait_ge(rs_ready[b], 1)
                silu_step(0, 0)
                xt_out(b, 1, 0, gain)
                xt_out(b, 1, 1, gain)
                ht_out(0, 0)
                silu_step(1, 0)
                h_squares(b, 1)
                split(Piece(n0 + 5))
                act.wait_ge(rs_ready[b], 2)
                silu_step(0, 1)
                ht_out(1, 0)
                split(Piece(n0 + 6))
                ht_out(0, 1)
                silu_step(1, 1)
                split(Piece(n0 + 7))
                with act.Fori(0, (FJ - 3) // 2) as it:
                    for s in range(2):
                        step(it * 2 + (2 + s), Piece(n0 + 8 + 3 * s, it))
                j, nx = FJ - 1, Piece(n0 + 3 * FJ - 1)
                split(nx)
                ht_out(j - 1, 1)
                split(nx + 1, (0,))
                silu_step(j, 0)
                split(nx + 1, (1,))
                ht_out(j, 0)
                split(nx + 2, (0,))
                post_squares(b + 1, 0)
                split(nx + 2, (1,))
                silu_step(j, 1)
                ht_out(j, 1)
                if layer == 0:
                    xt_out(2, 0, 0, 1)
                    xt_out(2, 0, 1, 1)
                    h_squares(2, 0)
                post_squares(b + 1, 1)
                split(n0 + FFN_PIECES + 2)

            to_ffn(1, N_NSAO, 2)
            ffn(0, N_FFN0)
            act.sem_inc(proj_out[1], 2)
            act.sem_inc(turn_out[1], 2)

            def dil_proj(hg, pat, n, first=False):
                e0 = 18 * hg
                t0 = 12 * hg

                def evac(c, m):
                    act.wait_ge(proj_done[1], pat * 6 + (e0 + tile_order(c, m, first) + 1))
                    dst = stage_dil[:, m, :] if c < 2 else view(v_dil, pat * (MT * 512) + m * 512, [[1, 512]])
                    if first and c == 0:
                        act.wait_ge(rs_ready[2], m + 1)
                    if first and (c, m) == (2, 0):
                        act.wait_ge(rs_perm_ready, 1)
                    scale = (rs if c < 2 else rs_perm)[:, m:m + 1]
                    act.activation(dst, bank(proj_bank(c, m, first)), ACT.Copy, scale=scale)\
                       .then_inc(proj_out[1], 1)

                def turn(c, m):
                    act.wait_ge(turned[1], pat * 4 + (t0 + tile_order(c, m, first) + 1))
                    act.activation(view(qk_t, pat * (2 * 4 * S) + (c * 4 * S + m * 64), [[S, 4], [P, 2], [1, 64]]),
                                   view(ps, (2 + m) * 512, [[P, 4], [1, 2], [2, 64]]), ACT.Copy,
                                   scale=1.0 if c else -SCALE)\
                       .then_inc(turn_out[1], 1)

                if first:
                    split(n)
                    evac(0, 0)
                    xt_out(2, 1, 0, 1)
                    xt_out(2, 1, 1, 1)
                    turn(0, 0)
                    evac(1, 0)
                    h_squares(2, 1)
                    split(n + 1)
                    split(n + 2)
                    turn(1, 0)
                    evac(0, 1)
                    split(n + 3)
                    turn(0, 1)
                    evac(1, 1)
                    split(n + 4)
                    evac(2, 0)
                    split(n + 5)
                    evac(2, 1)
                    turn(1, 1)
                    return
                split(n)
                evac(0, 0)
                split(n + 1)
                evac(0, 1)
                split(n + 2, (0,))
                turn(0, 0)
                split(n + 2, (1,))
                evac(1, 0)
                turn(0, 1)
                split(n + 3)
                evac(1, 1)
                split(n + 4, (0,))
                turn(1, 0)
                split(n + 4, (1,))
                evac(2, 0)
                split(n + 5)
                evac(2, 1)
                turn(1, 1)

            def ot_dil(hg, jq):
                act.wait_ge(pv_done[1], 2 * hg + jq + 1)
                src, dst = ot_views(hg, jq, xt_hi)
                act.activation(dst, src, ACT.Copy).then_inc(ot_hi[1], 1)

            for hg in range(2):
                if hg == 0:
                    dil_proj(0, 0, Piece(N_DIL + AHEAD), first=True)
                with act.Fori(0, 3 - (hg == 0)) as it:
                    k = int(hg == 0)
                    dil_proj(hg, it + k, Piece(N_DIL + 18 * hg + 6 * k + AHEAD, it))
                for s in range(16 + 4):
                    if 3 <= s < 19:
                        pt_evac(1, 16 * hg + s - 3, 512)
                    if s < 16:
                        exp_unit(1, 16 * hg + s, 512, 1)
                    if hg == 1 and s in (1, 5, 14):
                        ot_dil(*{1: (0, 0), 5: (0, 1), 14: (1, 0)}[s])
            ot_dil(1, 1)
            to_ffn(3, N_DILO, 3)
            ffn(1, N_FFN1)

        @block.vector
        def _(dve):
            done = [0]

            def link(ins):
                done[0] += 1
                ins.then_inc(dve_step, 1)
                dve.wait_ge(dve_step, done[0])

            def split(n, halves=(0, 1)):
                if isinstance(n, int):
                    n = Piece(n)
                if n.n0 >= N_END:
                    return
                for k in halves:
                    dve.wait_ge(hi_ready, n.halves(k + 1))
                    c = 1024 * k
                    dve.tensor_tensor(w_lo[:, n.slot, c:c + 1024], w_raw[:, n.raw, c:c + 1024],
                                      w_hi[:, n.slot, c:c + 1024].bitcast(F32), ALU.subtract)\
                       .then_inc(lo_ready, 1)

            def rsqrt(total, dst):
                v, hv, y, t = (nt[:, i:i + 1] for i in range(4))
                dve.tensor_scalar(hv, total, -0.5 / D, -0.5 * EPS, ALU.mult, ALU.add)
                link(dve.tensor_scalar(v, total, 1.0 / D, EPS, ALU.mult, ALU.add))
                link(dve.tensor_scalar(y.bitcast(I32), v.bitcast(I32), 1, None, ALU.logical_shift_right))
                link(dve.tensor_scalar(y.bitcast(I32), y.bitcast(I32), -1.0, float(0x5F3759DF),
                                       ALU.mult, ALU.add))
                for i in range(3):
                    link(dve.scalar_tensor_tensor(t, y, hv, y, ALU.mult, ALU.mult))
                    last = dve.scalar_tensor_tensor(y if i < 2 else dst, t, 1.5, y, ALU.add, ALU.mult)
                    if i < 2:
                        link(last)
                return last

            def h_rs(b, m):
                dve.wait_ge(sq_h[b], m + 1)
                rsqrt(ssq[:, m:m + 1], rs[:, m:m + 1]).then_inc(rs_ready[b], 1)
                dve.wait_ge(rs_ready[b], m + 1)

            def xt_lo_out(b, m, half, gain):
                dve.wait_ge(xt_hi_ready[b], 2 * m + half + 1)
                for k in range(4):
                    kt = 4 * half + k
                    src, dst = xt_views(b, m, half, kt, xt_lo)
                    _, hi = xt_views(b, m, half, kt, xt_hi)
                    ins = dve.scalar_tensor_tensor(dst, src, g_t[:, 8 * gain + kt:8 * gain + kt + 1],
                                                   hi.bitcast(F32), ALU.mult, ALU.subtract)
                ins.then_inc(xt_ready[b], 1)

            dve.wait_ge(rows_t, 1)
            dve.tensor_copy(g_t[:, :], bank(2, 0, 48)).then_inc(gt_ready, 1)
            xt_lo_out(0, 0, 0, 0)
            split(0)
            xt_lo_out(0, 0, 1, 0)
            split(1)
            xt_lo_out(0, 1, 0, 0)
            xt_lo_out(0, 1, 1, 0)
            for m in range(MT):
                h_rs(0, m)
            split(2)
            dve.wait_ge(gw_hi_ready, 1)
            dve.tensor_tensor(gw_lo[:, :, :], gw_raw[:, :, :], gw_hi[:, :, :].bitcast(F32), ALU.subtract)\
               .then_inc(gw_ready, 1)
            dve.wait_ge(pos_loaded, 16)
            dve.wait_ge(rope_ready, 1)
            link(dve.tensor_copy(pos_f[:, :], pos_i[:, :]))
            link(dve.tensor_tensor(ang[:, :, :], view(pos_f, 0, [[1, MT], [0, 8]]),
                                   view(inv_f, 0, [[0, MT], [1, 8]]), ALU.mult))
            link(dve.tensor_scalar(turns[:, :, :], ang[:, :, :], 1.0 / TWO_PI, MAGIC, ALU.mult, ALU.add))
            link(dve.tensor_scalar(turns[:, :, :], turns[:, :, :], MAGIC, None, ALU.subtract))
            c1 = 6.28125
            c2 = float(np.floor((TWO_PI - c1) * 2.0 ** 21) / 2.0 ** 21)
            for c in (c1, c2, TWO_PI - c1 - c2):
                link(dve.scalar_tensor_tensor(ang[:, :, :], turns[:, :, :], -c, ang[:, :, :],
                                              ALU.mult, ALU.add))
            link(dve.tensor_scalar(ang[:, :, :], ang[:, :, :], 3.1415925, -3.1415925, ALU.min, ALU.max))
            link(dve.scalar_tensor_tensor(half_pi[:, :, :], ang[:, :, :], -1.0, ang[:, :, :],
                                          ALU.mult, ALU.min))
            dve.tensor_scalar(half_pi[:, :, :], half_pi[:, :, :], TWO_PI / 4, None, ALU.add)\
               .then_inc(angles_ready, 1)

            def rope(i, e, stage, m, heads, table):
                a, b = rope_a[:, 0:heads, :], rope_b[:, 0:heads, :]
                x16 = view(stage, m * 512, [[DH, heads], [1, ROT]])
                x1 = view(stage, m * 512, [[DH, heads], [1, 8]])
                x2 = view(stage, m * 512 + 8, [[DH, heads], [1, 8]])
                dve.wait_ge(proj_out[i], e)
                dve.tensor_tensor(a, x16, view(cos2, table * ROT, [[0, heads], [1, ROT]]), ALU.mult)
                dve.tensor_tensor(rope_b[:, 0:heads, 0:8], x2, view(sin2, table * ROT, [[0, heads], [1, 8]]),
                                  ALU.mult)
                link(dve.tensor_tensor(rope_b[:, 0:heads, 8:16], x1,
                                       view(sin2, table * ROT + 8, [[0, heads], [1, 8]]), ALU.mult))
                dve.tensor_tensor(x16, a, b, ALU.add).then_inc(roped[i], 1)
                dve.wait_ge(roped[i], e - 2)

            split(3)
            split(4)
            dve.wait_ge(rope_ready, 2)
            dve.tensor_scalar(sin2[:, :, 0:8], sin2[:, :, 8:16], -1.0, None, ALU.mult)
            link(dve.tensor_copy(cos2[:, :, 8:16], cos2[:, :, 0:8]))

            def pair_copy(m, b):
                t = view(ps, b * 512, [[P, 4], [1, P]], n=64)
                dve.tensor_copy(view(pair, HK * S + m * P, [[S, 4], [1, P]], n=64), t)
                lo = 1 if m == 0 else 0
                return dve.tensor_copy(
                    view(pair, HK * S + m * P - 1 + lo, [[S, 4], [1, P - lo]], p0=64, n=64),
                    view(ps, b * 512 + lo, [[P, 4], [1, P - lo]], p0=64, n=64))

            def blocks(kv):
                for k0 in (0, 8):
                    ins = dve.tensor_tensor(view(tb_f, k0 * 64, [[64, 8], [16, HK], [1, NC]]),
                                            view(pair, kv * HK * S + 2 * k0, [[2, 8], [S, HK], [STRIDE, NC]]),
                                            view(g_t, 32 + k0, [[1, 8], [0, HK], [0, NC]]), ALU.add)
                ins.then_inc(tb_f_ready, 1)

            def block_lo(kv):
                dve.wait_ge(tb_hi_ready, kv + 1)
                dve.tensor_tensor(tb_lo[:, :, kv, :], tb_f[:, :, :, :].rearrange("p a b c -> p a (b c)"),
                                  tb_hi[:, :, kv, :].bitcast(F32), ALU.subtract).then_inc(tb_ready, 1)
                dve.wait_ge(tb_ready, kv + 1)

            link(dve.memset(tb_f[:, :, :, :], 0.0))
            dve.wait_ge(turned[0], 1)
            pair_copy(0, 4).then_inc(pair_dve, 1)
            split(5)
            rope(0, 3, stage_nsa, 0, 2 * HK, 0)
            dve.wait_ge(turned[0], 2)
            pair_copy(1, 6).then_inc(pair_dve, 1)
            split(6)
            rope(0, 4, stage_nsa, 1, 2 * HK, 1)
            dve.wait_ge(pair_act, 2)
            blocks(0)
            block_lo(0)
            dve.wait_ge(pair_dve, 2)
            blocks(1)
            split(7, (0,))
            block_lo(1)
            split(7, (1,))
            rope(0, 5, stage_nsa, 0, 2 * HK, 0)
            split(8)
            rope(0, 6, stage_nsa, 1, 2 * HK, 1)
            split(9)
            split(10)
            split(11)
            dve.wait_ge(hid_exp, 2)
            link(dve.tensor_scalar(e_hid[:, :], e_hid[:, :], 1.0, None, ALU.add))
            link(dve.reciprocal(e_hid[:, :], e_hid[:, :]))
            for kv, b in enumerate((3, 6)):
                r = slice(64 * kv, 64 * kv + 64)
                ins = dve.tensor_tensor(hid_r[r, :], ps[r, b, 0:256], e_hid[r, :], ALU.mult)
            ins.then_inc(hid_ready, 1)
            dve.wait_ge(gate_exp, 2)
            flat = gates[:, :, :].rearrange("p a b -> p (a b)")
            link(dve.tensor_scalar(flat, flat, 1.0, None, ALU.add))
            link(dve.reciprocal(flat, flat))
            split(12)
            dve.wait_ge(hid_psum, 1)
            dve.tensor_copy(hid_k[:, :, :], view(ps, 3 * 512, [[P, 2], [1, 64]]))
            dve.tensor_copy(hid_v[:, 0:HK, :, :], view(ps, 3 * 512 + 64, [[16, HK], [0, G], [1, 16]]))
            dve.tensor_copy(hid_v[:, HK:2 * HK, :, :], view(ps, 3 * 512 + P + 64, [[16, HK], [0, G], [1, 16]]))\
               .then_inc(hid_out, 1)
            rope(0, 7, stage_rot, 0, 8, 0)
            split(13)
            rope(0, 8, stage_rot, 1, 8, 1)
            split(14)
            dve.wait_ge(kc_out, 1)
            dve.wait_ge(masks_ready, 4)
            for hk in range(HK):
                ins = dve.tensor_tensor(view(vc_bd, hk * G * DH, [[DH, G], [1, DH]], n=64),
                                        view(ps, 6 * 512 + P + hk * DH, [[0, G], [1, DH]], n=64),
                                        view(bd_mask, 0, [[1, G], [0, DH]], n=64), ALU.mult)
            ins.then_inc(vc_out, 1)

            def cmp_scores(r):
                dve.wait_ge(sc_sum, r + 1)
                p, b = p_cmp[:, :, 8 * r:8 * r + 8, :], 7 if r else 3
                link(dve.tensor_tensor(p, bank(b, 0, 256).rearrange("p (m a c) -> p m a c", m=MT, a=8),
                                       view(mask_c, 0, [[16, MT], [0, 8], [1, 16]]), ALU.add))

            def cmp_less_max(r):
                p = p_cmp[:, :, 8 * r:8 * r + 8, :]
                link(dve.tensor_reduce(mx_c[:, :, 8 * r:8 * r + 8], p, AX, ALU.max))
                dve.tensor_tensor(p, p, view(mx_c, 8 * r, [[H, MT], [1, 8], [0, 16]]), ALU.subtract)\
                   .then_inc(sc_ready, 1)

            def cmp_sums(r):
                dve.wait_ge(pc_exp, r + 1)
                p, l = p_cmp[:, :, 8 * r:8 * r + 8, :], l_c[:, :, 8 * r:8 * r + 8]
                link(dve.tensor_reduce(l, p, AX, ALU.add))
                link(dve.reciprocal(l, l))
                link(dve.tensor_tensor(l, l, gates[:, :, 8 * r:8 * r + 8], ALU.mult))

            def cmp_probs(r):
                p = p_cmp[:, :, 8 * r:8 * r + 8, :]
                link(dve.tensor_tensor(p, p, view(l_c, 8 * r, [[H, MT], [1, 8], [0, 16]]), ALU.mult))
                dve.tensor_tensor(p, p, view(valid_c, 0, [[16, MT], [0, 8], [1, 16]]), ALU.mult)\
                   .then_inc(pc_ready, 1)

            rope(0, 9, stage_rot, 0, 8, 0)
            split(15)
            cmp_scores(0)
            cmp_less_max(0)
            def mask_unit(i, w, n, masks):
                dve.wait_ge(scores[i], w + 1)
                if w >= 4:
                    dve.wait_ge(pt_psum[i], w - 3)
                for br, mask in enumerate(masks):
                    ins = dve.tensor_tensor_reduce(
                        out=probs[:, w % 4, br * n:(br + 1) * n], in0=bank(score_bank(w), br * n, n),
                        in1=mask, scale=1.0, scalar=INF, op0=ALU.add, op1=ALU.min,
                        accum_out=mn[:, w % 4, br:br + 1])
                ins.then_inc(masked[i], 1)

            def norm_unit(i, w, n, gate_cols):
                dve.wait_ge(expd[i], w + 1)
                k = len(gate_cols)
                link(dve.reciprocal(rl[:, w % 4, 0:k], l_u[:, w % 4, 0:k]))
                for br, gate in enumerate(gate_cols):
                    p = probs[:, w % 4, br * n:(br + 1) * n]
                    if gate is None:
                        ins = dve.tensor_scalar(p, p, rl[:, w % 4, br:br + 1], None, ALU.mult)
                    else:
                        ins = dve.tensor_scalar(p, p, rl[:, w % 4, br:br + 1], gate, ALU.mult, ALU.mult)
                ins.then_inc(normed[i], 1)

            def norm_nsa(u):
                hd, m = unit_nsa(u)
                c = H + hd
                norm_unit(0, u, P * (m + 1), [gates[:, m, c:c + 1], gates[:, m, c + H:c + H + 1]])

            def ot_lo(hk):
                dve.wait_ge(ot_hi[0], hk + 1)
                kts = slice(2 * hk, 2 * hk + 2)
                dve.tensor_tensor(xt_lo[:, kts, :], bank(5 + hk % 2).rearrange("p (a t) -> p a t", a=2),
                                  xt_hi[:, kts, :].bitcast(F32), ALU.subtract).then_inc(ot_ready[0], 1)

            mask_unit(0, 0, P, [mask_nsa[:, P:2 * P]] * 2)
            mask_unit(0, 1, P, [mask_nsa[:, P:2 * P]] * 2)
            norm_nsa(0)
            cmp_sums(0)
            cmp_probs(0)
            rope(0, 10, stage_rot, 1, 8, 1)
            second_half = {8: cmp_scores, 9: cmp_less_max, 12: cmp_sums, 13: cmp_probs}
            for s in range(2, U_NSA + 1):
                if s < U_NSA:
                    n = P * (unit_nsa(s)[1] + 1)
                    mask_unit(0, s, n, [mask_nsa[:, 2 * P - n:2 * P]] * 2)
                norm_nsa(s - 1)
                if s in second_half:
                    second_half[s](1)
                if s >= 15 and s % 8 == 7:
                    ot_lo((s - 15) // 8)
            split(16)
            ot_lo(HK - 1)

            def add_post(b, m):
                dve.wait_ge(sq_post[b], m + 1)
                link(rsqrt(ssq[:, MT + m:MT + m + 1], rs_post[:, m:m + 1]))
                if m == 0:
                    dve.wait_ge(gp_loaded[b - 1], 16)
                for half in range(2):
                    c = slice(512 * half, 512 * half + 512)
                    dve.scalar_tensor_tensor(tmp[:, m, c], bank(2 * m + half), rs_post[:, m:m + 1],
                                             g_post[:, c], ALU.mult, ALU.mult).then_inc(post_ready[b], 1)

            def to_ffn(b, n, gain):
                split(n + 3)
                split(n + 4)
                split(n + 5)
                add_post(b, 0)
                split(n + 6)
                split(n + 7)
                xt_lo_out(b, 0, 0, gain)
                xt_lo_out(b, 0, 1, gain)
                add_post(b, 1)
                h_rs(b, 0)

            def ffn(layer, n0):
                def hs_step(j, m):
                    dve.wait_ge(silu_done[layer], ffn_order(j, m) + 1)
                    dve.scalar_tensor_tensor(hs[:, m, :], bank(gu_bank(j, m), 256, 256), rs[:, m:m + 1],
                                             silu[:, m, :], ALU.mult, ALU.mult).then_inc(hs_ready[layer], 1)

                def ht_out(j, m):
                    dve.wait_ge(ht_hi[layer], ffn_order(j, m) + 1)
                    hi = view(st_hi, m * P, [[S, 2], [1, P]])
                    dve.tensor_tensor(view(st_lo, m * P, [[S, 2], [1, P]]),
                                      bank(6 + m, 0, 256).rearrange("p (a t) -> p a t", a=2),
                                      hi.bitcast(F32), ALU.subtract).then_inc(ht_ready[layer], 1)

                def step(j, nx):
                    split(nx)
                    ht_out(j - 1, 1)
                    split(nx + 1, (0,))
                    hs_step(j, 0)
                    split(nx + 1, (1,))
                    split(nx + 2, (0,))
                    ht_out(j, 0)
                    split(nx + 2, (1,))
                    hs_step(j, 1)

                b, gain = 1 + 2 * layer, 2 + layer
                hs_step(0, 0)
                xt_lo_out(b, 1, 0, gain)
                xt_lo_out(b, 1, 1, gain)
                ht_out(0, 0)
                hs_step(1, 0)
                split(Piece(n0 + 4))
                h_rs(b, 1)
                split(Piece(n0 + 5))
                hs_step(0, 1)
                ht_out(1, 0)
                split(Piece(n0 + 6))
                ht_out(0, 1)
                hs_step(1, 1)
                split(Piece(n0 + 7))
                with dve.Fori(0, (FJ - 3) // 2) as it:
                    for s in range(2):
                        step(it * 2 + (2 + s), Piece(n0 + 8 + 3 * s, it))
                j, nx = FJ - 1, Piece(n0 + 3 * FJ - 1)
                split(nx)
                ht_out(j - 1, 1)
                split(nx + 1, (0,))
                hs_step(j, 0)
                split(nx + 1, (1,))
                ht_out(j, 0)
                split(nx + 2, (0,))
                add_post(2 + 2 * layer, 0)
                split(nx + 2, (1,))
                hs_step(j, 1)
                ht_out(j, 1)
                if layer == 0:
                    xt_lo_out(2, 0, 0, 1)
                    xt_lo_out(2, 0, 1, 1)
                    h_rs(2, 0)
                add_post(2 + 2 * layer, 1)
                split(n0 + FFN_PIECES + 2)

            to_ffn(1, N_NSAO, 2)
            ffn(0, N_FFN0)
            def dil_proj(hg, pat, n, first=False):
                e0 = 18 * hg

                def rot(c, m):
                    e = tile_order(c, m, first)
                    rope_dil(pat * 6 + (e0 + e + 3), pat * 4 + (12 * hg + e + 1), m)

                if first:
                    split(n)
                    rot(0, 0)
                    xt_lo_out(2, 1, 0, 1)
                    xt_lo_out(2, 1, 1, 1)
                    rot(1, 0)
                    h_rs(2, 1)
                    split(n + 1)
                    split(n + 2, (0,))
                    rot(0, 1)
                    split(n + 2, (1,))
                    split(n + 3)
                    rot(1, 1)
                    dve.wait_ge(rs_turned, 1)
                    dve.tensor_copy(rs_perm[:, :], bank(7, 0, MT)).then_inc(rs_perm_ready, 1)
                    split(n + 4)
                    split(n + 5)
                    return
                split(n)
                rot(0, 0)
                split(n + 1)
                rot(0, 1)
                split(n + 2)
                rot(1, 0)
                split(n + 3)
                rot(1, 1)
                split(n + 4)
                split(n + 5)

            def rope_dil(staged, products, m):
                x16 = view(stage_dil, m * 512, [[DH, 8], [1, ROT]])
                table = m
                dve.wait_ge(proj_out[1], staged)
                dve.tensor_tensor(rope_a[:, :, :], x16, view(cos2, table * ROT, [[0, 8], [1, ROT]]), ALU.mult)
                dve.tensor_tensor(rope_b[:, :, 0:8], view(stage_dil, m * 512 + 8, [[DH, 8], [1, 8]]),
                                  view(sin2, table * ROT, [[0, 8], [1, 8]]), ALU.mult)
                dve.tensor_tensor(rope_b[:, :, 8:16], view(stage_dil, m * 512, [[DH, 8], [1, 8]]),
                                  view(sin2, table * ROT + 8, [[0, 8], [1, 8]]), ALU.mult)\
                   .then_inc(rope_parts, 1)
                dve.wait_ge(rope_parts, products)
                dve.tensor_tensor(x16, rope_a[:, :, :], rope_b[:, :, :], ALU.add).then_inc(roped[1], 1)
                dve.wait_ge(roped[1], products)

            def ot_dil(hg, jq):
                dve.wait_ge(ot_hi[1], 2 * hg + jq + 1)
                src, dst = ot_views(hg, jq, xt_lo)
                _, hi = ot_views(hg, jq, xt_hi)
                dve.tensor_tensor(dst, src, hi.bitcast(F32), ALU.subtract).then_inc(ot_ready[1], 1)

            for hg in range(2):
                if hg == 0:
                    dil_proj(0, 0, Piece(N_DIL + AHEAD), first=True)
                with dve.Fori(0, 3 - (hg == 0)) as it:
                    k = int(hg == 0)
                    dil_proj(hg, it + k, Piece(N_DIL + 18 * hg + 6 * k + AHEAD, it))
                if hg == 0:
                    dve.wait_ge(dilmask_ready, 1)
                for s in range(16 + 1):
                    if s < 16:
                        mask_unit(1, 16 * hg + s, 512, [mask_dil[:, s % 2, :]])
                    if s >= 1:
                        norm_unit(1, 16 * hg + s - 1, 512, [None])
                    if hg == 1 and s in (2, 6, 15):
                        ot_dil(*{2: (0, 0), 6: (0, 1), 15: (1, 0)}[s])
            ot_dil(1, 1)
            to_ffn(3, N_DILO, 3)
            ffn(1, N_FFN1)

        @block.tensor
        def _(pe):
            owed = [0]

            def mm(o, s, m, start, stop):
                ins = pe.matmul(o, s, m, start=start, stop=stop)
                if owed[0]:
                    owed[0] = 0
                    ins.then_inc(piece_used, 1)
                    return None
                return ins

            def turn(b, k, src, n=P):
                ins = pe.transpose(ps[0:n, b, P * k:P * k + P], src, ident[:, :])
                if owed[0]:
                    owed[0] = 0
                    ins.then_inc(piece_used, 1)
                    return None
                return ins

            def three(o, s_hi, s_lo, m_hi, m_lo, start, stop):
                mm(o, s_hi, m_hi, start, False)
                mm(o, s_hi, m_lo, False, False)
                return mm(o, s_lo, m_hi, False, stop)

            def gemm(b, m, pc, first, last, done=None, mid=None, need=None, by_parity=False):
                for half in range(2):
                    if half and mid:
                        mid()
                    if need:
                        need(half)
                    p = pc + half
                    for u in range(4):
                        if first and u % 2 == 0:
                            pe.wait_ge(lo_ready, p.halves(u // 2 + 1))
                        kt, c = 4 * half + u, 512 * u
                        cols = slice(m, S, 2) if by_parity else slice(m * P, (m + 1) * P)
                        ins = three(bank(b), xt_hi[:, kt, cols], xt_lo[:, kt, cols],
                                    w_hi[:, p.slot, c:c + 512], w_lo[:, p.slot, c:c + 512],
                                    kt == 0, kt == KT - 1)
                    if half == 0:
                        if last:
                            ins.then_inc(piece_used, 1)
                    elif done is not None:
                        ins.then_inc(done, 1)
                        owed[0] = int(last)
                    elif last:
                        ins.then_inc(piece_used, 1)

            def xt_turn(b, m, half, src):
                for k in range(4):
                    kt = 4 * half + k
                    ins = turn(xt_bank(b, m, half), k, src[:, m, kt * P:(kt + 1) * P])
                ins.then_inc(xt_psum[b], 1)

            pe.wait_ge(ident_ready, 1)
            for m in range(MT):
                pe.wait_ge(x_loaded[m], 16)
                for half in range(2):
                    xt_turn(0, m, half, h)
                if m == 0:
                    pe.wait_ge(rows_loaded, 48)
                    pe.transpose(bank(2, 0, 48), rows[:, :], ident[0:48, 0:48]).then_inc(rows_t, 1)

            def nsa_gemm(e, n, mid=None):
                if e >= 2:
                    pe.wait_ge(proj_out[0], e - 1)
                m = e % 2
                need = (lambda half: pe.wait_ge(xt_ready[0], 2 * m + half + 1)) if e < 2 else None
                gemm(m, m, Piece(n), m == 0, m == 1, done=proj_done[0], need=need,
                     mid=mid)

            def turn_cmp(m, banks):
                pe.wait_ge(proj_out[0], m + 1)
                for stage, b in zip((stage_nsa, stage_rot), banks):
                    for k in range(HK):
                        ins = turn(b, k, stage[:, m, P * k:P * k + P])
                ins.then_inc(turned[0], 1)

            def turn_kv(t, m, b):
                pe.wait_ge(roped[0], t + 1)
                for k in range(HK):
                    ins = turn(b, k, stage_nsa[:, m, P * k:P * k + P])
                ins.then_inc(turned[0], 1)

            def turn_q(t, m, b_plain, b_rot):
                pe.wait_ge(roped[0], t + 1)
                for stage, b in ((stage_nsa, b_plain), (stage_rot, b_rot)):
                    for k in range(4):
                        ins = turn(b, k, stage[:, m, P * k:P * k + P])
                ins.then_inc(turned[0], 1)

            def compress(kv, n, b):
                pe.wait_ge(tb_ready, 2)
                for kt in range(16):
                    p, c = Piece(n + kt // 8), (kt % 8) * 256
                    if kt % 4 == 0:
                        pe.wait_ge(lo_ready, p.halves(kt % 8 // 4 + 1))
                    ins = three(bank(b, 0, 256), tb_hi[:, kt, :, :].rearrange("p a b -> p (a b)"),
                                tb_lo[:, kt, :, :].rearrange("p a b -> p (a b)"),
                                w_hi[:, p.slot, c:c + 256], w_lo[:, p.slot, c:c + 256], kt == 0, kt == 15)
                    if kt == 7:
                        ins.then_inc(piece_used, 1)
                ins.then_inc(hid_sum, 1)
                owed[0] = 1

            nsa_gemm(0, N_CMPKV)
            nsa_gemm(1, N_CMPKV)
            pe.wait_ge(gw_ready, 1)
            for kt in range(KT):
                ins = three(bank(3, 0, 256), gw_hi[:, kt, :], gw_lo[:, kt, :],
                            xt_hi[:, kt, :], xt_lo[:, kt, :], kt == 0, kt == KT - 1)
            ins.then_inc(gate_sum, 1)
            turn_cmp(0, (2, 4))
            nsa_gemm(2, N_SEL)
            turn_cmp(1, (5, 6))
            pe.wait_ge(gate_copied, 1)
            for m in range(MT):
                ins = pe.transpose(bank(3, 256 + 48 * m, 48), gates_t[:, m * P:(m + 1) * P], ident[0:48, 0:48])
            ins.then_inc(gate_turned, 1)
            nsa_gemm(3, N_SEL)
            turn_kv(0, 0, 7)
            nsa_gemm(4, N_WIN)
            pe.wait_ge(pair_act, 1)
            turn_kv(1, 1, 2)
            nsa_gemm(5, N_WIN)
            pe.wait_ge(gate_exp, 1)
            compress(0, N_WK1, 3)
            pe.wait_ge(pair_dve, 1)
            turn_kv(2, 0, 4)
            pe.wait_ge(pair_dve, 2)
            compress(1, N_WV1, 6)
            pe.wait_ge(pair_act, 2)
            turn_kv(3, 1, 5)
            nsa_gemm(6, N_Q)
            pe.wait_ge(hid_ready, 1)
            for k in range(2):
                ins = turn(3, k, hid_r[:, P * k:P * k + P])
            ins.then_inc(hid_psum, 1)
            nsa_gemm(7, N_Q)
            pe.wait_ge(turn_out[0], 2)
            turn_q(4, 0, 7, 2)
            pe.wait_ge(w2_loaded, 48)
            pe.wait_ge(hid_out, 1)
            for kt in range(2):
                mm(bank(6, 0, 64), w2k[:, kt, :, :].rearrange("p a d -> p (a d)"), hid_k[:, kt, :],
                   kt == 0, kt == 1)
            for hk in range(HK):
                for kt in range(2):
                    ins = mm(ps[0:64, 6, P + hk * DH:P + hk * DH + DH],
                             hid_v[:, HK * kt + hk, :, :].rearrange("p g c -> p (g c)"), w2v[:, kt, :],
                             kt == 0, kt == 1)
            ins.then_inc(kc_sum, 1)
            nsa_gemm(8, N_Q + 2)
            pe.wait_ge(turn_out[0], 4)
            turn_q(5, 1, 4, 5)

            def cmp_scores(r):
                pe.wait_ge(kc_out, 1)
                pe.wait_ge(turn_out[0], 6 + 2 * r)
                for m in range(MT):
                    for k in range(4):
                        ins = pe.matmul(bank(7 if r else 3, P * m + 32 * k, 32),
                                        qu_t[:, 4 * r + k, m * P:(m + 1) * P],
                                        kc_bd[:, (4 * r + k) // 2, :], start=True, stop=True)
                ins.then_inc(sc_sum, 1)

            def cmp_turn(r):
                pe.wait_ge(pc_ready, r + 1)
                for k in range(4):
                    hk, m = 2 * r + k // 2, k % 2
                    ins = pe.transpose(ps[0:64, 6 + r, P * k:P * k + P],
                                       p_cmp[:, m, G * hk:G * hk + G, :].rearrange("p a c -> p (a c)"),
                                       ident[:, :])
                ins.then_inc(pct_psum, 1)

            U = U_NSA

            def scores_nsa(u):
                hd, m = unit_nsa(u)
                n = P * (m + 1)
                if u >= 3:
                    pe.wait_ge(masked[0], u - 2)
                pe.matmul(bank(score_bank(u), 0, 2 * n), q_t[:, hd // 2, m * P:(m + 1) * P],
                          k_z[:, hd % 2, :, hd // G, 0:n], start=True, stop=True).then_inc(scores[0], 1)

            def start_attention():
                cmp_scores(0)
                pe.wait_ge(masks_ready, 4)
                pe.wait_ge(proj_out[0], 9)
                scores_nsa(0)
                scores_nsa(1)

            nsa_gemm(9, N_Q + 2, mid=start_attention)
            turn_q(6, 0, 7, 5)
            pe.wait_ge(vc_out, 1)
            pe.wait_ge(proj_out[0], 10)

            def turn_probs(i, w, blocks):
                pe.wait_ge(normed[i], w + 1)
                if w >= 2:
                    pe.wait_ge(pt_out[i], w - 1)
                for k in range(blocks):
                    ins = pe.transpose(bank(3 + w % 2, P * k, P), probs[:, w % 4, P * k:P * k + P],
                                       ident[:, :])
                ins.then_inc(pt_psum[i], 1)

            def pv(i, w, o, vs):
                pe.wait_ge(pt_out[i], w + 1)
                for k, v in enumerate(vs):
                    ins = pe.matmul(o, v, p_t[:, w % 4, P * k:P * k + P], start=k == 0,
                                    stop=i == 1 and k == len(vs) - 1, skip_group_check=i == 0)
                return ins

            def pv_nsa(u):
                hd, m = unit_nsa(u)
                hk, c = hd // G, hd // 2 % 2 * S + m * P
                if hk >= 2 and u % 8 == 0:
                    pe.wait_ge(ot_ready[0], hk - 1)
                pv(0, u, view(ps, (5 + hk % 2) * 512 + c, [[1, P]], p0=DH * (hd % 2), n=DH),
                   [v_nsa[:, br, kb, hk * DH:(hk + 1) * DH] for br in range(2) for kb in range(m + 1)])
                if hd % 2:
                    if u < 4:
                        pe.wait_ge(pct_out, 1)
                    elif hk == 2 and hd % G == 1:
                        pe.wait_ge(pct_out, 2)
                    g0 = hd % G // 2 * P
                    ins = pe.matmul(bank(5 + hk % 2, c, P), vc_bd[:, hk, g0:g0 + P], pc_t[:, 2 * hk + m, :],
                                    start=False, stop=True, skip_group_check=True)
                    if u % 8 == 7:
                        ins.then_inc(pv_done[0], 1)

            for s in range(2, U + 5):
                if s < U:
                    scores_nsa(s)
                if s == 2:
                    cmp_turn(0)
                if s == 3:
                    pe.wait_ge(turn_out[0], 7)
                    turn_q(7, 1, 7, 5)
                if s == 4:
                    pe.wait_ge(turn_out[0], 8)
                if s == 6:
                    cmp_scores(1)
                if s == 15:
                    cmp_turn(1)
                if 3 <= s < U + 3:
                    turn_probs(0, s - 3, 2 * (unit_nsa(s - 3)[1] + 1))
                if s >= 5:
                    pv_nsa(s - 5)

            def out_proj(b, n, ready):
                pcs = (Piece(n), Piece(n + 2))
                gemm(0, 0, pcs[0], True, False, need=lambda half: pe.wait_ge(ready, 2 * half + 2))
                gemm(1, 0, pcs[1], True, False, done=acc_done[b])
                gemm(2, 1, pcs[0], False, True)

                def turn_m0():
                    for half in range(2):
                        pe.wait_ge(h_ready[b], half + 1)
                        xt_turn(b, 0, half, h)

                gemm(3, 1, pcs[1], False, True, done=acc_done[b], mid=turn_m0)

            def turn_h2(m, half):
                pe.wait_ge(h_ready[2], 2 * m + half + 1)
                xt_turn(2, m, half, h)

            def ffn(layer, n0):
                b = 1 + 2 * layer

                def gu(j, m, pc, mid=None, need=None):
                    gemm(gu_bank(j, m), m, pc, m == 0, m == 1, done=gu_done[layer], mid=mid, need=need)

                def ht_turn(j, m):
                    pe.wait_ge(hs_ready[layer], ffn_order(j, m) + 1)
                    for k in range(2):
                        ins = turn(6 + m, k, hs[:, m, P * k:P * k + P])
                    ins.then_inc(ht_psum[layer], 1)

                def down(j, m, pc, first=False, last=False):
                    pe.wait_ge(ht_ready[layer], ffn_order(j, m) + 1)
                    if m == 0:
                        pe.wait_ge(lo_ready, pc.halves(2))
                    for k in range(2):
                        for n in range(2):
                            c = k * D + 512 * n
                            cols = slice(k * S + m * P, k * S + (m + 1) * P)
                            ins = three(bank(2 * m + n), st_hi[:, cols], st_lo[:, cols],
                                        w_hi[:, pc.slot, c:c + 512], w_lo[:, pc.slot, c:c + 512],
                                        first and k == 0, last and k == 1)
                    if last:
                        ins.then_inc(acc_done[b + 1], 1)
                    elif m == 1:
                        ins.then_inc(piece_used, 1)

                def step(j, pc):
                    gu(j, 0, pc, mid=lambda: ht_turn(j - 1, 1))
                    down(j - 1, 0, pc + 2)
                    gu(j, 1, pc, mid=lambda: ht_turn(j, 0))
                    down(j - 1, 1, pc + 2)

                def need(m):
                    return lambda half: pe.wait_ge(xt_ready[b], 2 * m + half + 1)

                def turn_h():
                    for half in range(2):
                        pe.wait_ge(h_ready[b], 3 + half)
                        pe.wait_ge(xt_ready[b], 1 + half)
                        xt_turn(b, 1, half, h)

                gu(0, 0, Piece(n0), need=need(0))
                gu(1, 0, Piece(n0 + 2), mid=turn_h)
                pe.wait_ge(xt_ready[b], 3)
                ht_turn(0, 0)
                gu(0, 1, Piece(n0), need=need(1))
                down(0, 0, Piece(n0 + 4), first=True)
                ht_turn(1, 0)
                gu(1, 1, Piece(n0 + 2), mid=lambda: ht_turn(0, 1))
                down(0, 1, Piece(n0 + 4), first=True)
                assert owed[0] == 0
                with pe.Fori(0, (FJ - 3) // 2) as it:
                    for s in range(2):
                        step(it * 2 + (2 + s), Piece(n0 + 5 + 3 * s, it))
                j, pc, end = FJ - 1, Piece(n0 + 3 * FJ - 4), Piece(n0 + FFN_PIECES - 1)
                gu(j, 0, pc, mid=lambda: ht_turn(j - 1, 1))
                down(j - 1, 0, pc + 2)
                ht_turn(j, 0)
                down(j, 0, end, last=True)
                gu(j, 1, pc)
                down(j - 1, 1, pc + 2)
                ht_turn(j, 1)
                if layer == 0:
                    turn_h2(0, 0)
                    turn_h2(0, 1)
                down(j, 1, end, last=True)
                owed[0] = 1

            out_proj(1, N_NSAO, ot_ready[0])
            ffn(0, N_FFN0)

            def turn_rs():
                pe.wait_ge(rs_ready[2], 2)
                for m in range(MT):
                    for par in range(2):
                        ins = pe.matmul(ps[64 * m:64 * m + 64, 7, par:par + 1],
                                        view(ident, par, [[2, 64]]), rs[:, m:m + 1], start=True, stop=True)
                ins.then_inc(rs_turned, 1)

            def dil_proj(hg, pat, n, first=False):
                def proj(c, m, **hooks):
                    pe.wait_ge(proj_out[1], pat * 6 + (18 * hg + tile_order(c, m, first) + 1))
                    gemm(proj_bank(c, m, first), m, n + 2 * c, m == 0, m == 1, done=proj_done[1],
                         by_parity=c == 2, **hooks)

                def turns_of(c, m):
                    t = tile_order(c, m, first)
                    pe.wait_ge(roped[1], pat * 4 + (12 * hg + t + 1))
                    pe.wait_ge(turn_out[1], pat * 4 + (12 * hg + t + 1 + (first and c)))
                    for k in range(4):
                        ins = turn(2 + m, k, stage_dil[:, m, P * k:P * k + P])
                    ins.then_inc(turned[1], 1)

                if first:
                    def need(m):
                        return lambda half: pe.wait_ge(xt_ready[2], 2 * m + half + 1)

                    proj(0, 0, need=need(0))
                    turn_h2(1, 0)
                    turn_h2(1, 1)
                    proj(1, 0, mid=lambda: turns_of(0, 0))
                    proj(0, 1, need=need(1), mid=lambda: turns_of(1, 0))
                    proj(1, 1, mid=lambda: turns_of(0, 1))
                    turn_rs()
                    proj(2, 0)
                    proj(2, 1)
                    turns_of(1, 1)
                    return
                proj(0, 0)
                proj(0, 1)
                turns_of(0, 0)
                proj(1, 0)
                turns_of(0, 1)
                proj(1, 1)
                turns_of(1, 0)
                proj(2, 0)
                proj(2, 1)
                turns_of(1, 1)

            def qk(pat, t, j, c, n):
                return view(qk_t, ((pat * 2 + t) * 4 + j // 2) * S + c, [[1, n]], p0=DH * (j % 2), n=DH)

            def scores_dil(hg, u):
                j, m, w = u // 2, u % 2, 16 * hg + u
                if w >= 3:
                    pe.wait_ge(masked[1], w - 2)
                for pat, c, k0, n in ((0, 0, 0, S), (1, 256, m * P, P), (2, 384, m * P, P)):
                    ins = pe.matmul(bank(score_bank(w), c, n), qk(pat, 0, j, m * P, P), qk(pat, 1, j, k0, n),
                                    start=True, stop=True)
                ins.then_inc(scores[1], 1)

            def pv_dil(hg, u):
                j, m = u // 2, u % 2
                if (hg, u) == (1, 8):
                    pe.wait_ge(ot_ready[1], 1)
                ins = pv(1, 16 * hg + u,
                         view(ps, ot_bank(hg, j // 4) * 512 + (j // 2 % 2) * S + m * P, [[1, P]],
                              p0=DH * (j % 2), n=DH),
                         [v_dil[:, pat, mk, j * DH:(j + 1) * DH]
                          for pat, mk in ((0, 0), (0, 1), (1, m), (2, m))])
                if u % 8 == 7:
                    ins.then_inc(pv_done[1], 1)

            for hg in range(2):
                if hg == 0:
                    dil_proj(0, 0, Piece(N_DIL), first=True)
                assert owed[0] == 0
                with pe.Fori(0, 3 - (hg == 0)) as it:
                    k = int(hg == 0)
                    dil_proj(hg, it + k, Piece(N_DIL + 18 * hg + 6 * k, it))
                pe.wait_ge(proj_out[1], 2 + 18 * (hg + 1))
                pe.wait_ge(turn_out[1], 2 + 12 * (hg + 1))
                for s in range(16 + 5):
                    if s < 16:
                        scores_dil(hg, s)
                    if 3 <= s < 19:
                        turn_probs(1, 16 * hg + s - 3, 4)
                    if s >= 5:
                        pv_dil(hg, s - 5)
            out_proj(3, N_DILO, ot_ready[1])
            ffn(1, N_FFN1)


_IN = ["x", "positions", "norm_mix_pre", "norm_mix_post", "norm_ffn_pre", "norm_ffn_post", "ffn_w_gu",
       "ffn_w_down", "nsa_w_in", "nsa_cmp_pos", "nsa_cmp_wk1", "nsa_cmp_wk2", "nsa_cmp_wv1",
       "nsa_cmp_wv2", "nsa_w_o", "dil_w_in", "dil_w_o"]


def kernel(**inputs):
    import concourse.bacc as bacc
    from concourse.bass_utils import run_bass_kernel_spmd

    nc = bacc.Bacc("TRN2", target_bir_lowering=False, num_devices=1)
    arrays, args = {}, []
    for name in _IN:
        a = np.ascontiguousarray(inputs[name])
        arrays[f"in_{name}"] = a
        args.append(nc.dram_tensor(f"in_{name}", a.shape, mybir.dt.from_np(a.dtype),
                                   kind="ExternalInput").ap())
    out = nc.dram_tensor("out_h", (1, S, D), F32, kind="ExternalOutput").ap()
    build(nc, *args, out)
    result = run_bass_kernel_spmd(nc, [arrays], core_ids=[0])
    return result.results[0]["out_h"]
```
